# Optimizing a Trainium2 kernel written in Bass

```python
import math
import jax
import jax.numpy as jnp
from jax import lax
import numpy as np
import jax, jax.numpy as jnp

D_MODEL = 1024
BATCH = 1
SEQ = 512
DEPTH = 2

D_FF = 4 * D_MODEL
NORM_EPS = 1e-6
N_EVEN = (DEPTH + 1) // 2
N_ODD = DEPTH // 2

GDN_HEADS = 8
GDN_HEAD_DIM = 64
GDN_WIDTH = GDN_HEADS * GDN_HEAD_DIM
GDN_CONV = 4
GDN_CHUNK = 64

SC_WIDTH = D_MODEL - GDN_WIDTH
SC_CONV = 3

EVEN_IN = 4 * GDN_WIDTH + 2 * GDN_HEADS + 3 * SC_WIDTH

NSA_HEADS = 16
NSA_HEAD_DIM = D_MODEL // NSA_HEADS
NSA_KV_GROUPS = 4
NSA_HPG = NSA_HEADS // NSA_KV_GROUPS
NSA_KV_WIDTH = NSA_KV_GROUPS * NSA_HEAD_DIM
CMP_BLOCK = 32
CMP_STRIDE = 16
CMP_HIDDEN = 256
SEL_BLOCK = 64
N_SELECT = 16
WINDOW = 512
Q_BLOCK = 128
ODD_IN = NSA_HEADS * NSA_HEAD_DIM + 6 * NSA_KV_WIDTH + 3 * NSA_HEADS

ROPE_THETA = 500000.0
ROPE_DIM = NSA_HEAD_DIM // 4


def _split_points(sizes):
    return [int(v) for v in np.cumsum(sizes)[:-1]]

def rms_norm(x, w):
    xf = x.astype(jnp.float32)
    y = xf * lax.rsqrt(jnp.mean(xf * xf, axis=-1, keepdims=True) + NORM_EPS)
    return (y * w.astype(jnp.float32)).astype(x.dtype)

def l2_normalize(x):
    xf = x.astype(jnp.float32)
    return xf * lax.rsqrt(jnp.sum(xf * xf, axis=-1, keepdims=True) + NORM_EPS)

def causal_dwconv(x, w):
    k_width = w.shape[0]
    t_len = x.shape[1]
    xp = jnp.pad(x, ((0, 0), (k_width - 1, 0), (0, 0)))
    return sum(xp[:, j:j + t_len] * w[j] for j in range(k_width))

def masked_softmax(s, mask):
    s = jnp.where(mask, s, -jnp.inf)
    m = jnp.max(s, axis=-1, keepdims=True)
    m = jnp.where(jnp.isfinite(m), m, 0.0)
    e = jnp.exp(s - m)
    den = jnp.sum(e, axis=-1, keepdims=True)
    return e / jnp.where(den > 0.0, den, 1.0)

def rope_tables(t_len):
    inv_freq = ROPE_THETA ** (-jnp.arange(0, ROPE_DIM, 2, dtype=jnp.float32) / ROPE_DIM)
    ang = jnp.arange(t_len, dtype=jnp.float32)[:, None] * inv_freq[None, :]
    return jnp.cos(ang), jnp.sin(ang)

def apply_partial_rope(x, cos, sin):
    half = ROPE_DIM // 2
    xf = x.astype(jnp.float32)
    x1, x2, rest = xf[..., :half], xf[..., half:ROPE_DIM], xf[..., ROPE_DIM:]
    c = cos[None, :, None, :]
    s = sin[None, :, None, :]
    return jnp.concatenate([x1 * c - x2 * s, x2 * c + x1 * s, rest], axis=-1).astype(x.dtype)

def squared_relu_mlp(h, w_up, w_down):
    return jnp.square(jax.nn.relu(h @ w_up)) @ w_down

def gated_delta_rule_chunked(q, k, v, g, beta):
    f32 = jnp.float32
    b_sz, t_len, n_h, dk = q.shape
    dv = v.shape[-1]
    c = GDN_CHUNK
    n_chunks = t_len // c

    def chunks(a):
        a = a.astype(f32).reshape((b_sz, n_chunks, c, n_h) + a.shape[3:])
        return jnp.moveaxis(a, (1, 3), (0, 2))

    qc = chunks(q) * (dk ** -0.5)
    kc = chunks(k)
    vc = chunks(v)
    bc = chunks(beta)
    gc = jnp.cumsum(chunks(g), axis=-1)
    incl = jnp.tril(jnp.ones((c, c), bool))
    strict = jnp.tril(jnp.ones((c, c), bool), -1)
    decay = jnp.exp(jnp.where(incl, gc[..., :, None] - gc[..., None, :], -jnp.inf))
    kb = kc * bc[..., None]
    m_low = jnp.where(strict, jnp.einsum('nbhik,nbhjk->nbhij', kb, kc) * decay, 0.0)
    a_mat = m_low + jnp.eye(c, dtype=f32)
    u = lax.linalg.triangular_solve(a_mat, vc * bc[..., None], left_side=True, lower=True, unit_diagonal=True)
    w = lax.linalg.triangular_solve(a_mat, kb * jnp.exp(gc)[..., None], left_side=True, lower=True, unit_diagonal=True)
    attn = jnp.einsum('nbhik,nbhjk->nbhij', qc, kc) * decay

    def step(state, inp):
        q_c, k_c, u_c, w_c, attn_c, g_c = inp
        v_new = u_c - jnp.einsum('bhck,bhkv->bhcv', w_c, state)
        o_c = (jnp.einsum('bhck,bhkv->bhcv', q_c * jnp.exp(g_c)[..., None], state)
               + jnp.einsum('bhij,bhjv->bhiv', attn_c, v_new))
        g_last = g_c[..., -1:]
        state = (state * jnp.exp(g_last)[..., None]
                 + jnp.einsum('bhck,bhcv->bhkv', k_c * jnp.exp(g_last - g_c)[..., None], v_new))
        return state, o_c

    s0 = jnp.zeros((b_sz, n_h, dk, dv), f32)
    _, o = lax.scan(step, s0, (qc, kc, u, w, attn, gc))
    return jnp.moveaxis(o, (0, 2), (1, 3)).reshape(b_sz, t_len, n_h, dv)

def gdn_shortconv_mixer(h, w_in, qkv_conv, a_log, dt_bias, o_norm, sc_conv, w_out):
    f32 = jnp.float32
    b_sz, t_len, _ = h.shape
    sizes = (3 * GDN_WIDTH, GDN_WIDTH, GDN_HEADS, GDN_HEADS, SC_WIDTH, SC_WIDTH, SC_WIDTH)
    qkv, z, a, b, b_gate, c_gate, hs = jnp.split(h @ w_in, _split_points(sizes), axis=-1)
    qkv = jax.nn.silu(causal_dwconv(qkv, qkv_conv))
    q, k, v = [t.reshape(b_sz, t_len, GDN_HEADS, GDN_HEAD_DIM) for t in jnp.split(qkv, 3, axis=-1)]
    g = -jnp.exp(a_log.astype(f32)) * jax.nn.softplus(a.astype(f32) + dt_bias.astype(f32))
    beta = jax.nn.sigmoid(b.astype(f32))
    o = gated_delta_rule_chunked(l2_normalize(q), l2_normalize(k), v, g, beta)
    o = rms_norm(o, o_norm) * jax.nn.silu(z.reshape(b_sz, t_len, GDN_HEADS, GDN_HEAD_DIM).astype(f32))
    y_a = o.reshape(b_sz, t_len, GDN_WIDTH).astype(h.dtype)
    y_b = b_gate * causal_dwconv(c_gate * hs, sc_conv)
    return jnp.concatenate([y_a, y_b], axis=-1) @ w_out

def compress_blocks(x, pos, w1, w2):
    b_sz, t_len, g_sz, d = x.shape
    r = CMP_BLOCK // CMP_STRIDE
    n_cmp = t_len // CMP_STRIDE - r + 1
    ch = x.reshape(b_sz, t_len // CMP_STRIDE, CMP_STRIDE, g_sz, d)
    blk = jnp.concatenate([ch[:, i:i + n_cmp] for i in range(r)], axis=2)
    blk = blk + pos[None, None, :, None, :].astype(x.dtype)
    blk = jnp.moveaxis(blk, 3, 2).reshape(b_sz, n_cmp, g_sz, CMP_BLOCK * d)
    return jax.nn.silu(blk @ w1) @ w2

def gather_blocks(blocks, idx):
    return jax.vmap(jax.vmap(lambda bl, ix: bl[ix]))(blocks, idx)

def nsa_mixer(h, w_in, cmp_pos, cmp_k_w1, cmp_k_w2, cmp_v_w1, cmp_v_w2, w_out):
    f32 = jnp.float32
    b_sz, t_len, _ = h.shape
    n_g, hpg, dh = NSA_KV_GROUPS, NSA_HPG, NSA_HEAD_DIM
    sizes = (NSA_HEADS * dh,) + (NSA_KV_WIDTH,) * 6 + (3 * NSA_HEADS,)
    q, k_c, v_c, k_s, v_s, k_w, v_w, gl = jnp.split(h @ w_in, _split_points(sizes), axis=-1)
    q = q.reshape(b_sz, t_len, NSA_HEADS, dh)
    k_c, v_c, k_s, v_s, k_w, v_w = [a.reshape(b_sz, t_len, n_g, dh) for a in (k_c, v_c, k_s, v_s, k_w, v_w)]
    gates = jax.nn.sigmoid(gl.astype(f32)).reshape(b_sz, t_len, n_g, hpg, 3)
    cos, sin = rope_tables(t_len)
    q_r = apply_partial_rope(q, cos, sin)
    k_s = apply_partial_rope(k_s, cos, sin)
    k_w = apply_partial_rope(k_w, cos, sin)
    kc_blk = compress_blocks(k_c, cmp_pos, cmp_k_w1, cmp_k_w2).astype(f32)
    vc_blk = compress_blocks(v_c, cmp_pos, cmp_v_w1, cmp_v_w2).astype(f32)
    n_cmp = kc_blk.shape[1]
    cmp_end = jnp.arange(n_cmp) * CMP_STRIDE + CMP_BLOCK - 1
    n_sel_blocks = t_len // SEL_BLOCK
    n_sel = min(N_SELECT, n_sel_blocks)
    c_start = jnp.arange(n_cmp)[:, None] * CMP_STRIDE
    s_start = jnp.arange(n_sel_blocks)[None, :] * SEL_BLOCK
    overlap = ((c_start < s_start + SEL_BLOCK) & (c_start + CMP_BLOCK > s_start)).astype(f32)
    ks_blk = jnp.moveaxis(k_s.reshape(b_sz, n_sel_blocks, SEL_BLOCK, n_g, dh), 3, 1)
    vs_blk = jnp.moveaxis(v_s.reshape(b_sz, n_sel_blocks, SEL_BLOCK, n_g, dh), 3, 1)
    pad = ((0, 0), (WINDOW, 0), (0, 0), (0, 0))
    kw_pad = jnp.pad(k_w, pad)
    vw_pad = jnp.pad(v_w, pad)
    scale = dh ** -0.5
    blk_ids = jnp.arange(n_sel_blocks)
    in_blk = jnp.arange(SEL_BLOCK)
    win_off = jnp.arange(Q_BLOCK + WINDOW)

    def query_block(qb):
        q0 = qb * Q_BLOCK
        t = q0 + jnp.arange(Q_BLOCK)
        take = lambda a: lax.dynamic_slice_in_dim(a, q0, Q_BLOCK, axis=1)
        qn = take(q).astype(f32).reshape(b_sz, Q_BLOCK, n_g, hpg, dh) * scale
        qr = take(q_r).astype(f32).reshape(b_sz, Q_BLOCK, n_g, hpg, dh) * scale
        p_c = masked_softmax(jnp.einsum('bqghd,bcgd->bghqc', qn, kc_blk), cmp_end[None, :] <= t[:, None])
        o_c = jnp.einsum('bghqc,bcgd->bqghd', p_c, vc_blk)
        imp = jnp.einsum('bghqc,cs->bgqs', p_c, overlap)
        cur = (t // SEL_BLOCK)[:, None]
        js = blk_ids[None, :]
        forced = (js == 0) | (js == cur) | (js == cur - 1)
        imp = jnp.where(js > cur, -jnp.inf, jnp.where(forced, jnp.inf, imp))
        _, idx = lax.top_k(imp, n_sel)
        k_sel = gather_blocks(ks_blk, idx).astype(f32).reshape(b_sz, n_g, Q_BLOCK, n_sel * SEL_BLOCK, dh)
        v_sel = gather_blocks(vs_blk, idx).astype(f32).reshape(b_sz, n_g, Q_BLOCK, n_sel * SEL_BLOCK, dh)
        kpos = (idx[..., None] * SEL_BLOCK + in_blk).reshape(b_sz, n_g, Q_BLOCK, n_sel * SEL_BLOCK)
        p_s = masked_softmax(jnp.einsum('bqghd,bgqkd->bghqk', qr, k_sel), (kpos <= t[:, None])[:, :, None])
        o_s = jnp.einsum('bghqk,bgqkd->bqghd', p_s, v_sel)
        spos = q0 - WINDOW + win_off
        dist = t[:, None] - spos[None, :]
        m_w = (dist >= 0) & (dist < WINDOW) & (spos[None, :] >= 0)
        kwin = lax.dynamic_slice_in_dim(kw_pad, q0, Q_BLOCK + WINDOW, axis=1).astype(f32)
        vwin = lax.dynamic_slice_in_dim(vw_pad, q0, Q_BLOCK + WINDOW, axis=1).astype(f32)
        p_w = masked_softmax(jnp.einsum('bqghd,bkgd->bghqk', qr, kwin), m_w)
        o_w = jnp.einsum('bghqk,bkgd->bqghd', p_w, vwin)
        g = take(gates)
        o = g[..., 0:1] * o_c + g[..., 1:2] * o_s + g[..., 2:3] * o_w
        return o.reshape(b_sz, Q_BLOCK, NSA_HEADS * dh).astype(h.dtype)

    out = lax.map(query_block, jnp.arange(t_len // Q_BLOCK))
    out = jnp.moveaxis(out, 0, 1).reshape(b_sz, t_len, NSA_HEADS * dh)
    return out @ w_out

def first_inputs(seed: int = 0) -> dict:
    key = jax.random.key(seed)
    ks = jax.random.split(key, 24)
    f32 = jnp.float32

    def nrm(k, shape, scale):
        return jax.random.normal(k, shape, f32) * scale

    def gain(k, shape):
        return 1.0 + 0.01 * jax.random.normal(k, shape, f32)

    dt = jnp.exp(jax.random.uniform(ks[9], (N_EVEN, GDN_HEADS), f32, math.log(1e-3), math.log(0.1)))
    return {
        'x': nrm(ks[0], (BATCH, SEQ, D_MODEL), 1.0),
        'mix_norm': gain(ks[1], (DEPTH, D_MODEL)),
        'mlp_norm': gain(ks[2], (DEPTH, D_MODEL)),
        'w_up': nrm(ks[3], (DEPTH, D_MODEL, D_FF), D_MODEL ** -0.5),
        'w_down': nrm(ks[4], (DEPTH, D_FF, D_MODEL), D_FF ** -0.5),
        'final_norm': gain(ks[5], (D_MODEL,)),
        'ev_w_in': nrm(ks[6], (N_EVEN, D_MODEL, EVEN_IN), D_MODEL ** -0.5),
        'ev_qkv_conv': nrm(ks[7], (N_EVEN, GDN_CONV, 3 * GDN_WIDTH), GDN_CONV ** -0.5),
        'ev_a_log': jnp.log(jax.random.uniform(ks[8], (N_EVEN, GDN_HEADS), f32, 1.0, 16.0)),
        'ev_dt_bias': dt + jnp.log(-jnp.expm1(-dt)),
        'ev_o_norm': gain(ks[10], (N_EVEN, GDN_HEAD_DIM)),
        'ev_sc_conv': nrm(ks[11], (N_EVEN, SC_CONV, SC_WIDTH), SC_CONV ** -0.5),
        'ev_w_out': nrm(ks[12], (N_EVEN, GDN_WIDTH + SC_WIDTH, D_MODEL), D_MODEL ** -0.5),
        'od_w_in': nrm(ks[13], (N_ODD, D_MODEL, ODD_IN), D_MODEL ** -0.5),
        'od_cmp_pos': nrm(ks[14], (N_ODD, CMP_BLOCK, NSA_HEAD_DIM), 0.1),
        'od_cmp_k_w1': nrm(ks[15], (N_ODD, CMP_BLOCK * NSA_HEAD_DIM, CMP_HIDDEN), (CMP_BLOCK * NSA_HEAD_DIM) ** -0.5),
        'od_cmp_k_w2': nrm(ks[16], (N_ODD, CMP_HIDDEN, NSA_HEAD_DIM), CMP_HIDDEN ** -0.5),
        'od_cmp_v_w1': nrm(ks[17], (N_ODD, CMP_BLOCK * NSA_HEAD_DIM, CMP_HIDDEN), (CMP_BLOCK * NSA_HEAD_DIM) ** -0.5),
        'od_cmp_v_w2': nrm(ks[18], (N_ODD, CMP_HIDDEN, NSA_HEAD_DIM), CMP_HIDDEN ** -0.5),
        'od_w_out': nrm(ks[19], (N_ODD, NSA_HEADS * NSA_HEAD_DIM, D_MODEL), D_MODEL ** -0.5),
    }

def first_block(x, mix_norm, mlp_norm, w_up, w_down, final_norm,
              ev_w_in, ev_qkv_conv, ev_a_log, ev_dt_bias, ev_o_norm, ev_sc_conv, ev_w_out,
              od_w_in, od_cmp_pos, od_cmp_k_w1, od_cmp_k_w2, od_cmp_v_w1, od_cmp_v_w2, od_w_out):
    for layer in range(DEPTH):
        h = rms_norm(x, mix_norm[layer])
        i = layer // 2
        if layer % 2 == 0:
            x = x + gdn_shortconv_mixer(h, ev_w_in[i], ev_qkv_conv[i], ev_a_log[i], ev_dt_bias[i],
                                        ev_o_norm[i], ev_sc_conv[i], ev_w_out[i])
        else:
            x = x + nsa_mixer(h, od_w_in[i], od_cmp_pos[i], od_cmp_k_w1[i], od_cmp_k_w2[i],
                              od_cmp_v_w1[i], od_cmp_v_w2[i], od_w_out[i])
        x = x + squared_relu_mlp(rms_norm(x, mlp_norm[layer]), w_up[layer], w_down[layer])
    return rms_norm(x, final_norm)


N_HEADS = D_MODEL // 128
QK_NOPE_DIM = 64
QK_ROPE_DIM = 32
QK_HEAD_DIM = QK_NOPE_DIM + QK_ROPE_DIM
V_HEAD_DIM = 64
ATTN_WIDTH = N_HEADS * V_HEAD_DIM
Q_LORA_RANK = D_MODEL // 4
KV_LORA_RANK = D_MODEL // 4
ROPE_THETA_2 = 10000.0
FOURIER_WIDTH = D_MODEL // 2
FOURIER_GROUP_DIM = 128
N_FOURIER_GROUPS = FOURIER_WIDTH // FOURIER_GROUP_DIM
N_BRANCHES = 2
IN_WIDTH = (Q_LORA_RANK + KV_LORA_RANK + QK_ROPE_DIM + ATTN_WIDTH
            + 2 * FOURIER_WIDTH + N_BRANCHES * D_MODEL)


def _rms_norm(x, g):
    xf = x.astype(jnp.float32)
    y = xf * lax.rsqrt(jnp.mean(xf * xf, axis=-1, keepdims=True) + NORM_EPS)
    return (y * g.astype(jnp.float32)).astype(x.dtype)

def _rope_tables(seq_len, dtype):
    half = QK_ROPE_DIM // 2
    inv_freq = ROPE_THETA_2 ** (-jnp.arange(half, dtype=jnp.float32) / half)
    pos = jnp.arange(seq_len, dtype=jnp.float32)
    ang = pos[:, None] * inv_freq[None, :]
    return jnp.cos(ang).astype(dtype), jnp.sin(ang).astype(dtype)

def _apply_rope(x, cos, sin):
    half = QK_ROPE_DIM // 2
    x1, x2 = x[..., :half], x[..., half:]
    c, s = cos[:, None, :], sin[:, None, :]
    return jnp.concatenate([x1 * c - x2 * s, x2 * c + x1 * s], axis=-1)

def _split_in(p):
    sizes = [Q_LORA_RANK, KV_LORA_RANK, QK_ROPE_DIM, ATTN_WIDTH,
             FOURIER_WIDTH, FOURIER_WIDTH, D_MODEL]
    idx = []
    acc = 0
    for s in sizes:
        acc += s
        idx.append(acc)
    return jnp.split(p, idx, axis=-1)

def _bidirectional_attention(q, k, v):
    b, h, s, dk = q.shape
    nb = s // Q_BLOCK
    scale = QK_HEAD_DIM ** -0.5
    qb = q.reshape(b, h, nb, Q_BLOCK, dk).transpose(2, 0, 1, 3, 4)

    def one_block(q_blk):
        sc = jnp.einsum('bhqd,bhkd->bhqk', q_blk, k).astype(jnp.float32) * scale
        p = jax.nn.softmax(sc, axis=-1)
        return jnp.einsum('bhqk,bhkd->bhqd', p.astype(v.dtype), v)

    o = lax.map(one_block, qb)
    return o.transpose(1, 2, 0, 3, 4).reshape(b, h, s, V_HEAD_DIM)

def _mla_branch(c_q, c_kv, k_pe, q_latent_g, kv_latent_g, w_uq, w_ukv,
                q_head_g, k_head_g, cos, sin):
    b, s, _ = c_q.shape
    q = (_rms_norm(c_q, q_latent_g) @ w_uq).reshape(b, s, N_HEADS, QK_HEAD_DIM)
    kv = (_rms_norm(c_kv, kv_latent_g) @ w_ukv).reshape(b, s, N_HEADS, QK_NOPE_DIM + V_HEAD_DIM)
    k_nope, v = kv[..., :QK_NOPE_DIM], kv[..., QK_NOPE_DIM:]
    k_pe_h = jnp.broadcast_to(k_pe[:, :, None, :], (b, s, N_HEADS, QK_ROPE_DIM))
    k = jnp.concatenate([k_nope, k_pe_h], axis=-1)
    q = _rms_norm(q, q_head_g)
    k = _rms_norm(k, k_head_g)
    q = jnp.concatenate([q[..., :QK_NOPE_DIM], _apply_rope(q[..., QK_NOPE_DIM:], cos, sin)], axis=-1)
    k = jnp.concatenate([k[..., :QK_NOPE_DIM], _apply_rope(k[..., QK_NOPE_DIM:], cos, sin)], axis=-1)
    o = _bidirectional_attention(q.transpose(0, 2, 1, 3), k.transpose(0, 2, 1, 3),
                                 v.transpose(0, 2, 1, 3))
    return o.transpose(0, 2, 1, 3).reshape(b, s, ATTN_WIDTH)

def _fourier_branch(u):
    b, s, _ = u.shape
    ug = u.astype(jnp.float32).reshape(b, s, N_FOURIER_GROUPS, FOURIER_GROUP_DIM)
    f = jnp.real(jnp.fft.fft2(ug, axes=(1, 3), norm='ortho'))
    return f.reshape(b, s, FOURIER_WIDTH).astype(u.dtype)

def second_inputs(seed: int = 0) -> dict:
    key = jax.random.key(seed)
    ks = jax.random.split(key, 14)
    L, D = DEPTH, D_MODEL

    def nrm(k, shape, fan_in):
        return jax.random.normal(k, shape, jnp.float32) * fan_in ** -0.5

    def gain(k, shape):
        return 1.0 + 0.05 * jax.random.normal(k, shape, jnp.float32)

    return {
        "x": jax.random.normal(ks[0], (BATCH, SEQ, D), jnp.float32),
        "norm_g": gain(ks[1], (L, D)),
        "w_in": nrm(ks[2], (L, D, IN_WIDTH), D),
        "q_latent_g": gain(ks[3], (L, Q_LORA_RANK)),
        "kv_latent_g": gain(ks[4], (L, KV_LORA_RANK)),
        "w_uq": nrm(ks[5], (L, Q_LORA_RANK, N_HEADS * QK_HEAD_DIM), Q_LORA_RANK),
        "w_ukv": nrm(ks[6], (L, KV_LORA_RANK, N_HEADS * (QK_NOPE_DIM + V_HEAD_DIM)), KV_LORA_RANK),
        "q_head_g": gain(ks[7], (L, QK_HEAD_DIM)),
        "k_head_g": gain(ks[8], (L, QK_HEAD_DIM)),
        "w_attn_proj": nrm(ks[9], (L, ATTN_WIDTH, D), ATTN_WIDTH),
        "w_fourier_proj": nrm(ks[10], (L, FOURIER_WIDTH, D), FOURIER_WIDTH),
        "b_merge": 0.1 * jax.random.normal(ks[11], (L, N_BRANCHES, D), jnp.float32),
        "w_out": nrm(ks[12], (L, D, D), D) * (2 * DEPTH) ** -0.5,
    }

def second_block(x, norm_g, w_in, q_latent_g, kv_latent_g, w_uq, w_ukv, q_head_g,
              k_head_g, w_attn_proj, w_fourier_proj, b_merge, w_out):
    _, s, _ = x.shape
    cos, sin = _rope_tables(s, x.dtype)
    for l in range(DEPTH):
        h = _rms_norm(x, norm_g[l])
        p = h @ w_in[l]
        c_q, c_kv, k_pe, z_a, u_f, z_f, g_a, g_f = _split_in(p)
        o_a = _mla_branch(c_q, c_kv, k_pe, q_latent_g[l], kv_latent_g[l], w_uq[l], w_ukv[l],
                          q_head_g[l], k_head_g[l], cos, sin)
        y_a = (o_a * jax.nn.silu(z_a)) @ w_attn_proj[l]
        y_f = (_fourier_branch(u_f) * jax.nn.silu(z_f)) @ w_fourier_proj[l]
        m = (jax.nn.sigmoid(g_a + b_merge[l, 0]) * y_a
             + jax.nn.sigmoid(g_f + b_merge[l, 1]) * y_f)
        x = x + m @ w_out[l]
    return x


def setup_inputs(seed=0):
    out = dict(first_inputs(seed))
    for name, value in second_inputs(seed + 1).items():
        if name != "x":
            out[name + "_2"] = value
    return out


def reference(
    x, mix_norm, mlp_norm, w_up, w_down, final_norm, ev_w_in, ev_qkv_conv, ev_a_log, ev_dt_bias,
    ev_o_norm, ev_sc_conv, ev_w_out, od_w_in, od_cmp_pos, od_cmp_k_w1, od_cmp_k_w2, od_cmp_v_w1,
    od_cmp_v_w2, od_w_out, norm_g_2, w_in_2, q_latent_g_2, kv_latent_g_2, w_uq_2, w_ukv_2,
    q_head_g_2, k_head_g_2, w_attn_proj_2, w_fourier_proj_2, b_merge_2, w_out_2,
):
    x = first_block(
        x, mix_norm, mlp_norm, w_up, w_down, final_norm, ev_w_in, ev_qkv_conv, ev_a_log,
        ev_dt_bias, ev_o_norm, ev_sc_conv, ev_w_out, od_w_in, od_cmp_pos, od_cmp_k_w1,
        od_cmp_k_w2, od_cmp_v_w1, od_cmp_v_w2, od_w_out,
    )
    return second_block(
        x, norm_g_2, w_in_2, q_latent_g_2, kv_latent_g_2, w_uq_2, w_ukv_2, q_head_g_2,
        k_head_g_2, w_attn_proj_2, w_fourier_proj_2, b_merge_2, w_out_2,
    )


_drawn_inputs = setup_inputs


def setup_inputs(seed=0):
    import zlib

    import numpy as np

    out = dict(_drawn_inputs(seed))
    spreads = {}
    factors = {'mix_norm': 4.146,
     'mlp_norm': 5.125,
     'final_norm': 5.281,
     'ev_o_norm': 8.0,
     'od_cmp_pos': 3.553,
     'norm_g_2': 4.035,
     'q_latent_g_2': 8.0,
     'kv_latent_g_2': 8.0,
     'w_uq_2': 3.502,
     'q_head_g_2': 8.0,
     'k_head_g_2': 8.0,
     'b_merge_2': 7.545}
    for name, (base, spread) in spreads.items():
        noise = np.random.default_rng([zlib.crc32(name.encode()), seed]).standard_normal(out[name].shape)
        drawn = base * np.exp(spread * noise) if base else spread * noise
        out[name] = jnp.asarray(drawn.astype(out[name].dtype))
    for name, factor in factors.items():
        out[name] = (out[name] * factor).astype(out[name].dtype)
    return out
```

```python
import numpy as np
from concourse import mybir

F32 = mybir.dt.float32
F32R = mybir.dt.float32r
ACT = mybir.ActivationFunctionType
ALU = mybir.AluOpType
AX = mybir.AxisListType.X

P = 128
T = 512
D = 1024
KT = D // P
NT = T // P
FF_PARTS = 4
RING = 3
TILES = 8
GEMM_BANKS = 4
EPS = 1e-6

GDN_H, GDN_D = 8, 64
NSA_H, NSA_D, NSA_G = 16, 64, 4
N_CMP = T // 16
KC_ROW = (T + 16) // 2
MLA_H, MLA_QK, MLA_NOPE, MLA_ROPE = 8, 96, 64, 32
FG = 4
LAYERS2 = 2
NEG = -1e30
NSA_HEADS = [4 * (2 * (j // 4) + s) + j % 4 for j in range(8) for s in range(2)]


def columns(widths):
    at, out = 0, {}
    for name, width in widths:
        out[name] = (at, width)
        at += width
    return out, at


COMMON, COMMON_N = columns([("ident", P), ("ones", P)])
PHASE0, PHASE0_N = columns([("blk64", P), ("triu", P), ("notyet", T), ("levels", 7 * P), ("last", P),
                            ("head_row", GDN_H * P), ("pair_row", 4 * P)])
PHASE1, PHASE1_N = columns([("causal", P), ("cmp_mask", NT * N_CMP), ("rot", P), ("cos", T), ("sin", T)])
PHASE2, PHASE2_N = columns([("dft_d", 2 * P), ("rot", P), ("cos", T), ("sin", T)])
PHASE_N = max(PHASE0_N, PHASE1_N, PHASE2_N)
PARAMS, PARAMS_N = columns([
    ("eps", 1), ("mix_norm", 2 * KT), ("mlp_norm", 2 * KT), ("final_norm", KT), ("conv", 12 * 4), ("sc_conv", 4 * 3),
    ("o_norm", 1), ("a_log", 1), ("dt_bias", 1), ("cmp_pos", 16), ("cmp_k_w2", 2 * P), ("cmp_v_w2", 2 * NSA_D),
    ("norm2", LAYERS2 * KT), ("q_latent", LAYERS2 * 2), ("kv_latent", LAYERS2 * 2),
    ("q_head", LAYERS2), ("k_head", LAYERS2), ("merge", LAYERS2 * 2 * KT)])


def rope_rows(theta, rot, base, width):
    f4 = np.float32
    half = rot // 2
    inv = (f4(theta) ** (-np.arange(half, dtype=f4) / f4(half))).astype(f4)
    ang = np.arange(T, dtype=f4)[None, :] * inv[:, None]
    cos, sin, part = np.ones((P, T), f4), np.zeros((P, T), f4), np.zeros((P, P), f4)
    for r0 in range(base, P, width):
        for i in range(half):
            a, b = r0 + i, r0 + half + i
            if b >= P:
                continue
            cos[a] = cos[b] = np.cos(ang[i])
            sin[a] = sin[b] = np.sin(ang[i])
            part[b, a], part[a, b] = -1.0, 1.0
    return cos, sin, part


def constant_arrays():
    f4 = np.float32
    eye, i, j = np.eye(P, dtype=f4), np.arange(P)[None, :], np.arange(P)[:, None]
    common = np.concatenate([eye, np.ones((P, P), f4)], 1)

    levels = []
    for size in (1, 2, 4, 8, 16, 32, 64):
        levels.append((i // (2 * size) == j // (2 * size)) & (i // size % 2 == 1) & (j // size % 2 == 0))
    head_row, pair_row = np.zeros((P, GDN_H, P), f4), np.zeros((P, 4, P), f4)
    for h in range(GDN_H):
        head_row[h, h] = 1.0
        pair_row[h, h // 2, 64 * (h % 2):64 * (h % 2) + 64] = 1.0
    last = np.zeros((P, P), f4)
    last[P - 1] = 1.0
    phase0 = np.concatenate([
        (i // 64 == j // 64).astype(f4), (j <= i).astype(f4), np.tile(np.where(i >= j, f4(0), f4(NEG)), (1, NT)),
        *[m.astype(f4) for m in levels], last, head_row.reshape(P, -1), pair_row.reshape(P, -1)], 1)

    cos, sin, rot = rope_rows(500000.0, NSA_D // 4, 0, NSA_D)
    t = np.arange(T).reshape(NT, P).T[:, :, None]
    c = np.arange(N_CMP)[None, None, :]
    cmp_mask = np.where((c * 16 + 31 <= t) & (c < N_CMP - 1), f4(0), f4(NEG)).reshape(P, -1)
    phase1 = np.concatenate([np.where(i <= j, f4(0), f4(NEG)), cmp_mask, rot, cos, sin], 1)

    cos, sin, rot = rope_rows(10000.0, MLA_ROPE, MLA_NOPE, P)
    ang = 2 * np.pi * (np.arange(P)[:, None] * np.arange(P)[None, :] % P) / P
    norm = 1.0 / np.sqrt(T * P)
    phase2 = np.concatenate([np.cos(ang) * norm, -np.sin(ang) * norm, rot, cos, sin], 1)

    out = [common, phase0, phase1, phase2]
    return [np.ascontiguousarray(a.astype(f4)) for a in out]


def stream_of(inp):
    blocks = []

    def pad(w, cols):
        return np.pad(w, ((0, 0), (0, cols - w.shape[1])))

    def add(tiles):
        tiles = list(tiles)
        assert len(tiles) % TILES == 0
        for n in range(0, len(tiles), TILES):
            blocks.append(np.concatenate(tiles[n:n + TILES], 1))

    def out_major(w):
        return [w[k:k + P, m:m + P] for m in range(0, w.shape[1], P) for k in range(0, w.shape[0], P)]

    def in_major(w):
        return [w[k:k + P, m:m + P] for k in range(0, w.shape[0], P) for m in range(0, w.shape[1], P)]

    def mlp(layer):
        up, down = inp["w_up"][layer], inp["w_down"][layer]
        for q in range(FF_PARTS):
            add(out_major(up[:, q * D:(q + 1) * D]))
            add(out_major(down[q * D:(q + 1) * D]))

    w = inp["ev_w_in"][0]
    ab = np.zeros((D, P), w.dtype)
    ab[:, 0:GDN_H], ab[:, 32:32 + GDN_H] = w[:, 2048:2056], w[:, 2056:2064]
    add(out_major(ab))
    add(out_major(w[:, 0:2048]))
    for m in range(4):
        for first in (2064 + 512, 2064 + 1024, 2064):
            add(out_major(w[:, first + m * P:first + (m + 1) * P]))
    add(out_major(inp["ev_w_out"][0]))
    mlp(0)

    w = inp["od_w_in"][0]
    order = [d for h in NSA_HEADS for d in range(h * NSA_D, (h + 1) * NSA_D)]
    gate = [3 * h + branch for branch in range(3) for h in NSA_HEADS]
    kc, vc, ks, vs, kw, vw = [w[:, 1024 + 256 * n:1280 + 256 * n] for n in range(6)]
    add(out_major(pad(w[:, 2560:2608][:, gate], P)))
    for part in (kc, vc, w[:, order], ks, kw):
        add(out_major(part))
    add(in_major(np.concatenate([vs, vw], 1)))
    add(out_major(inp["od_cmp_k_w1"][0]))
    add(out_major(inp["od_cmp_v_w1"][0]))
    add(out_major(inp["od_w_out"][0][order]))
    mlp(1)

    ang = 2 * np.pi * (np.arange(T)[:, None] * np.arange(T)[None, :] % T) / T
    dft_t = [np.cos(ang).astype(np.float32), np.sin(ang).astype(np.float32)]
    for l in range(LAYERS2):
        w = inp["w_in_2"][l]
        cq, ckv, kpe, za, uf, zf, ga, gf = np.split(w, np.cumsum([256, 256, 32, 512, 512, 512, 1024]), axis=1)
        for part in (cq, ckv, pad(kpe, P), uf):
            add(out_major(part))
        uq = inp["w_uq_2"][l].reshape(256, MLA_H, MLA_QK)
        add(out_major(np.pad(uq, ((0, 0), (0, 0), (0, P - MLA_QK))).reshape(256, MLA_H * P)))
        ukv = inp["w_ukv_2"][l].reshape(256, MLA_H, 2, 64)
        add(out_major(ukv[:, :, 0].reshape(256, 512)))
        add(in_major(ukv[:, :, 1].reshape(256, 512)))
        add(out_major(za))
        add(out_major(zf))
        add(b for k in range(NT) for part in dft_t for b in in_major(part[k * P:(k + 1) * P]))
        pa, pf = out_major(inp["w_attn_proj_2"][l]), out_major(inp["w_fourier_proj_2"][l])
        for m in range(KT):
            add(out_major(ga[:, m * P:(m + 1) * P]))
            add(out_major(gf[:, m * P:(m + 1) * P]))
            add(pa[4 * m:4 * m + 4] + pf[4 * m:4 * m + 4])
        add(out_major(inp["w_out_2"][l]))
    return np.ascontiguousarray(np.stack(blocks))


def parameter_array(inp):
    out = np.zeros((P, PARAMS_N), np.float32)

    def put(name, a, n=0):
        at = PARAMS[name][0] + n
        out[:a.shape[0], at:at + a.shape[1]] = a

    def tiles(v):
        return v.reshape(-1, P).T

    out[:, PARAMS["eps"][0]] = EPS
    for l in range(2):
        put("mix_norm", tiles(inp["mix_norm"][l]), l * KT)
        put("mlp_norm", tiles(inp["mlp_norm"][l]), l * KT)
    put("final_norm", tiles(inp["final_norm"]))
    put("conv", inp["ev_qkv_conv"][0].reshape(4, 12, P).transpose(2, 1, 0).reshape(P, 48))
    put("sc_conv", inp["ev_sc_conv"][0].reshape(3, 4, P).transpose(2, 1, 0).reshape(P, 12))
    put("o_norm", np.tile(inp["ev_o_norm"][0], 2)[:, None])
    put("a_log", inp["ev_a_log"][0][:, None])
    put("dt_bias", inp["ev_dt_bias"][0][:, None])
    put("cmp_pos", inp["od_cmp_pos"][0].reshape(16, P).T)
    for k in range(2):
        put("cmp_k_w2", np.tile(inp["od_cmp_k_w2"][0][k * P:(k + 1) * P], (1, 2)), k * P)
        put("cmp_v_w2", inp["od_cmp_v_w2"][0][k * P:(k + 1) * P], k * NSA_D)
    for l in range(LAYERS2):
        put("norm2", tiles(inp["norm_g_2"][l]), l * KT)
        put("q_latent", tiles(inp["q_latent_g_2"][l]), l * 2)
        put("kv_latent", tiles(inp["kv_latent_g_2"][l]), l * 2)
        put("q_head", inp["q_head_g_2"][l][:, None], l)
        put("k_head", inp["k_head_g_2"][l][:, None], l)
        for branch in range(2):
            put("merge", tiles(inp["b_merge_2"][l, branch]), (l * 2 + branch) * KT)
    return out


def plan_core():
    block, bank, split = {}, {}, {}
    uses, fills, turn, at = [0] * 8, [0] * 8, [0, 0], 0

    def use(key, pool):
        b = pool * GEMM_BANKS + turn[pool] % 4
        turn[pool] += 1
        take(key, b, pool == 1 and key[0] not in ("ssq", "l2", "on", "lat", "hs2"))

    def take(key, b, announced=True):
        bank[key] = (b, uses[b], fills[b])
        uses[b] += 1
        fills[b] += announced

    def gemm(keys, blocks):
        nonlocal at
        for key in keys:
            block[key] = (at, at + blocks - 1)
            use(key, 0)
        at += blocks

    def scratch(*key):
        use(key, 1)

    def splits(*keys):
        for key in keys:
            split[key] = len(split)

    def norm(n):
        scratch("ssq", n)
        if n != "final":
            splits(*[("h", n, k) for k in range(KT)])

    def each(name, *rest, n):
        for m in range(n):
            gemm([(name, *rest, m)], 1)

    def mlp(layer):
        norm(2 * layer + 1)
        for q in range(FF_PARTS):
            each("up", layer, q, n=KT)
            splits(*[("a", layer, q, m) for m in range(KT)])
            each("down", layer, q, n=KT)

    norm(0)
    gemm([("ab",)], 1)
    each("qkv", n=12)
    each("z", n=4)
    for i in range(4):
        for name in ("cg", "hs", "bg"):
            gemm([(name, i)], 1)
        splits(("yb", i))
    for i in range(8):
        scratch("l2", i)
    for name in ("gT", "gc", "gl", "gcr"):
        scratch(name)
    for p in range(4):
        scratch("bb", p)
    for c in range(NT):
        scratch("kt", c)
        scratch("vt", c)
    for p in range(4):
        for name in ("gcb", "kk", "qk"):
            for s in range(2):
                scratch(name, 2 * p + s)
        for level in range(7):
            for name in (("y", "yx", "xt") if level else ("xt",)):
                if level == 6 and name == "xt":
                    continue
                for s in range(2):
                    scratch(name, 2 * p + s, level)
        for s in range(2):
            scratch("u", 2 * p + s)
            scratch("w", 2 * p + s)
    for p in range(4):
        scratch("eg", p)
    for c in range(NT):
        if c:
            scratch("ws", c, 0)
            scratch("ws", c, 1)
        scratch("o", c)
        scratch("ds", c)
    for p in range(4):
        scratch("on", p)
    splits(*[("ya", p) for p in range(4)])
    each("out", 0, n=KT)
    mlp(0)

    norm(2)
    gemm([("gl_gates",)], 1)
    each("kc", n=2)
    each("vc", n=2)
    each("q", n=8)
    each("ks", n=2)
    each("kw", n=2)
    gemm([("v", tt) for tt in range(NT)], 4)
    for kv in range(2):
        for m in range(2):
            gemm([("cmp1", kv, m)], 2)
    scratch("gateT")
    scratch("kcb")
    scratch("vcb")
    for qt in range(NT):
        scratch("sc", qt, 0)
        scratch("sc", qt, 1)
    for i in range(4):
        scratch("pcT", i)
    for i in range(12):
        scratch("rope", i)
    for j in range(8):
        use(("o1", j), 0)
        for s in range(2):
            for qt in range(NT):
                for br in range(2):
                    take(("s1", j, s, qt, br), 4 + br)
                    take(("t1", j, s, qt, br), 6 + br)
    each("out", 1, n=KT)
    mlp(1)
    norm("final")

    for l in range(LAYERS2):
        norm(4 + l)
        each("cq", l, n=2)
        each("ckv", l, n=2)
        each("kpe", l, n=1)
        each("uf", l, n=4)
        for which in range(2):
            scratch("lat", l, which)
        splits(*[("cn", l, i) for i in range(4)])
        for i in range(2):
            gemm([("uq", l, 4 * i + n) for n in range(4)], 1)
        gemm([("kn", l, i) for i in range(4)], 1)
        gemm([("v2", l, tt) for tt in range(NT)], 1)
        for which in range(2):
            for h in range(MLA_H):
                scratch("hs2", l, which, h)
                scratch("rot2", l, which, h)
        each("za", l, n=4)
        each("zf", l, n=4)
        for j in range(4):
            use(("o2", l, j), 0)
            for s in range(2):
                for qt in range(NT):
                    i = (2 * j + s) * NT + qt
                    take(("s2", l, j, s, qt), 4 + i % 2)
                    take(("t2", l, j, s, qt), 6 + i % 2)
            splits(("oa", l, j))
        for g in range(FG):
            for tt in range(NT):
                scratch("dd", l, g, tt)
        gemm([("f", l, g) for g in range(FG)], 4)
        splits(*[("of", l, g) for g in range(FG)])
        for m in range(KT):
            each("ga", l, m, n=1)
            each("gf", l, m, n=1)
            gemm([("ya2", l, m), ("yf2", l, m)], 1)
            splits(("m", l, m))
        each("out2", l, n=KT)
    return block, bank, split, at


class Core:
    pass


def place(nc, c):
    at = (nc.sbuf_base + 63) // 64 * 64
    top = nc.sbuf_usable_end

    def put(name, shape, offset, dtype=F32):
        size = (4 * int(np.prod(shape[1:])) + 31) // 32 * 32
        assert offset + size <= top, (name, offset + size - top)
        return nc.alloc_sbuf_tensor_at(name, shape, dtype, offset=offset), offset + size

    c.x, at = put("x", [P, KT, T], at)
    c.raw, at = put("raw", [P, RING, TILES * P], at)
    c.w_hi, at = put("w_hi", [P, RING, TILES * P], at, F32R)
    c.w_lo, at = put("w_lo", [P, RING, TILES * P], at, F32R)
    c.Y, _ = put("Y", [P, 2, T], at)
    c.stage, at = put("stage", [P, 3, T], at)
    c.common, at = put("common", [P, COMMON_N], at)
    c.params, at = put("params", [P, PARAMS_N], at)
    c.tiny, at = put("tiny", [P, 64], at)
    c.rstd, at = put("rstd", [P, 2, T], at)
    c.XT, _ = put("XT", [P, 2, T], at)
    c.sq, at = put("sq", [P, 2, T], at)
    at = (at + 63) // 64 * 64
    phase = at
    at += 4 * PHASE_N
    at = (at + 63) // 64 * 64
    c.phase0, _ = put("phase0", [P, PHASE0_N], phase)
    c.phase1, _ = put("phase1", [P, PHASE1_N], phase)
    c.phase2, _ = put("phase2", [P, PHASE2_N], phase)
    tail = (top - 2 * 32768) // 64 * 64
    h, a, local = tail, tail + 32768, at
    c.h_hi, _ = put("h_hi", [P, KT, T], h, F32R)
    c.h_lo, _ = put("h_lo", [P, KT, T], h + 16384, F32R)
    c.a_hi, _ = put("a_hi", [P, KT, T], a, F32R)
    c.a_lo, _ = put("a_lo", [P, KT, T], a + 16384, F32R)
    room = tail - local
    assert room > 0

    c.relu, _ = put("relu", [P, 2, T], local)

    c.qkv, o = put("qkv", [P, 12, T], local)
    c.u, _ = put("u", [P, NT, T], local + 8 * 2048)
    c.z, o = put("z", [P, 4, T], o)
    c.egc, _ = put("egc", [P, 4, T], o)
    c.kb, o = put("kb", [P, 4, T], o)
    c.sc, _ = put("sc", [P, 3, T], o)
    c.wT, o = put("wT", [P, 4, T], o)
    c.X, _ = put("X", [P, 2, T], o)
    c.g_row, o = put("g_row", [P, T], o)
    c.e_row, o = put("e_row", [P, T], o)
    c.beta_row, o = put("beta_row", [P, T], o)
    c.gc_row, o = put("gc_row", [P, T], o)
    c.tok, o = put("tok", [P, 8, 32], o)
    c.S, o = put("S", [P, 4, GDN_D], o)
    assert o <= tail, o - tail
    c.kd, o = put("kd", [P, NT, T], h)
    c.gdn_o, _ = put("gdn_o", [P, 4, T], o)
    c.kbe, o = put("kbe", [P, NT, T], o)
    c.vb, o = put("vb", [P, NT, T], o)
    c.vnew, _ = put("vnew", [P, T], o)
    c.MT, o = put("MT", [P, 2, T], o)
    c.ML, o = put("ML", [P, 2, T], o)
    assert o == a
    c.AT0, _ = put("AT0", [P, 4, T], a)
    c.AT1, _ = put("AT1", [P, 4, T], a + 16384)

    c.q, o = put("q", [P, 8, T], local)
    c.ks, o = put("ks", [P, 2, T], o)
    c.kw, o = put("kw", [P, 2, T], o)
    c.v, o = put("v", [P, NT, T], o)
    c.gate_row, o = put("gate_row", [P, T], o)
    c.gate, o = put("gate", [P, NT, 48], o)
    c.kcb, o = put("kcb", [P, P], o)
    c.vcb, o = put("vcb", [P, 4, NSA_D], o)
    c.stat, o = put("stat", [P, 8, 16], o)
    o1 = o
    c.kc_hi, o = put("kc_hi", [P, 2, 5, KC_ROW], o1, F32R)
    c.kc_lo, o = put("kc_lo", [P, 2, 5, KC_ROW], o, F32R)
    assert o <= tail, o - tail
    c.hid_k, o = put("hid_k", [P, 2, P], h)
    c.hid_v, o = put("hid_v", [P, 2, 4 * P], o)
    c.pcT, o = put("pcT", [P, 4, T], o)
    c.cmp_s, _ = put("cmp_s", [P, 2, T], o)
    c.cmp_e, _ = put("cmp_e", [P, 2, T], o + 4096)
    c.prob, o = put("prob", [P, 4, T], o)
    c.rope_t, _ = put("rope_t", [P, 4, T], o)
    c.probT, o = put("probT", [P, 4, T], o)
    c.diag, o = put("diag", [P, 4, P], o)
    c.nb, o = put("nb", [P, 4, 4], o)
    assert o <= a

    c.c, o = put("c", [P, 4, T], local)
    c.v2, _ = put("v2", [P, NT, T], local)
    c.z_a, _ = put("z_a", [P, 4, T], o)
    c.z_f, _ = put("z_f", [P, 4, T], o + 8192)
    c.cn_hi, o = put("cn_hi", [P, 4, T], o, F32R)
    c.cn_lo, o = put("cn_lo", [P, 4, T], o, F32R)
    c.d_hi, _ = put("d_hi", [P, NT, FG, 2 * P], o, F32R)
    c.d_lo, _ = put("d_lo", [P, NT, FG, 2 * P], o + 16384, F32R)
    c.m_hi, _ = put("m_hi", [P, KT, T], o, F32R)
    c.m_lo, _ = put("m_lo", [P, KT, T], o + 16384, F32R)
    c.q2, o = put("q2", [P, MLA_H, T], o)
    c.k2, o = put("k2", [P, MLA_H, T], o)
    c.head_t, _ = put("head_t", [P, 2, T], o)
    c.prob2, o = put("prob2", [P, 2, T], o)
    c.diag2, o = put("diag2", [P, 2, P], o)
    c.nb2, o = put("nb2", [P, 2, 4], o)
    c.sig, _ = put("sig", [P, 4, T], local)
    c.probT2, _ = put("probT2", [P, 2, T], a + 8192)
    c.kpe, _ = put("kpe", [P, T], a + 8192 + 4096)
    assert o <= tail, o - tail
    c.u_f, _ = put("u_f", [P, 4, T], a + 16384 + 8192)


def add_semaphores(nc, ctx, c):
    def sem(name):
        return ctx.enter_context(nc.semaphore(name))

    c.raw_loaded = [sem(f"raw_loaded_{i}") for i in range(RING)]
    c.bank_filled = [sem(f"bank_filled_{i}") for i in range(8)]
    c.bank_read = [sem(f"bank_read_{i}") for i in range(8)]
    c.x_loaded = sem("x_loaded")
    c.common_loaded = sem("common_loaded")
    c.params_loaded = sem("params_loaded")
    c.phase0_loaded = sem("phase0_loaded")
    c.phase1_loaded = sem("phase1_loaded")
    c.phase2_loaded = sem("phase2_loaded")
    c.out_written = sem("out_written")
    c.w_hi_ready = sem("w_hi_ready")
    c.w_lo_ready = sem("w_lo_ready")
    c.block_used = sem("block_used")
    c.split_src = sem("split_src")
    c.split_hi = sem("split_hi")
    c.split_lo = sem("split_lo")
    c.vector_step = sem("vector_step")
    c.scalar_step = sem("scalar_step")
    c.sq_ready = sem("sq_ready")
    c.sq_used = sem("sq_used")
    c.rstd_ready = sem("rstd_ready")
    c.final_ready = sem("final_ready")
    c.silu_done = sem("silu_done")
    c.g_x_ready = sem("g_x_ready")
    c.g_e_ready = sem("g_e_ready")
    c.g_ln_ready = sem("g_ln_ready")
    c.a_exp_ready = sem("a_exp_ready")
    c.g_ready = sem("g_ready")
    c.ekd_in = sem("ekd_in")
    c.ekd_ready = sem("ekd_ready")
    c.egt_ready = sem("egt_ready")
    c.l2_ready = sem("l2_ready")
    c.qe_ready = sem("qe_ready")
    c.vnew_ready = sem("vnew_ready")
    c.ml_ready = sem("ml_ready")
    c.xt_ready = sem("xt_ready")
    c.kc_pad = sem("kc_pad")
    c.kc_hi_ready = sem("kc_hi_ready")
    c.hid_bias = sem("hid_bias")
    c.cmp_shift = sem("cmp_shift")
    c.cmp_exp = sem("cmp_exp")
    c.cmp_p = sem("cmp_p")
    c.rope_ready = sem("rope_ready")
    c.nb_ready = sem("nb_ready")
    c.diag_ready = sem("diag_ready")
    c.attn_out = sem("attn_out")
    c.attn_hi = sem("attn_hi")
    c.kpe_ready = sem("kpe_ready")
    c.head_t_ready = sem("head_t_ready")
    c.head_ready = sem("head_ready")
    c.z_ready = sem("z_ready")
    c.nb2_ready = sem("nb2_ready")
    c.diag2_ready = sem("diag2_ready")
    c.d_hi_ready = sem("d_hi_ready")


def program_tensor(pe, nc, c, block, bank, split):
    mm = nc.tensor.matmul
    ident, ones = c.common[:, 0:P], c.common[:, P:2 * P]
    sums = [0]

    def claim(key):
        b, n, _ = bank[key]
        if n:
            pe.wait_ge(c.bank_read[b], n)
        return c.psum[b]

    def fill(key):
        return c.bank_filled[bank[key][0]]

    def read(key):
        b, n, _ = bank[key]
        pe.wait_ge(c.bank_read[b], n + 1)

    def three(out, w_hi, w_lo, x_hi, x_lo, first, last):
        mm(out, w_hi, x_lo, start=first, stop=False)
        mm(out, w_lo, x_hi, start=False, stop=False)
        return mm(out, w_hi, x_hi, start=False, stop=last)

    def gemm(key, x_hi, x_lo, tile0=0, needs=None, cols=T, view=None):
        out = claim(key)[:, 0:cols]
        if view:
            out = view(out)
        for k in range(len(x_hi)):
            b, t = block[key][0] + (tile0 + k) // TILES, (tile0 + k) % TILES
            if k == 0 or t == 0:
                pe.wait_ge(c.w_lo_ready, b + 1)
            if needs:
                needs(k)
            w = slice(t * P, t * P + P)
            ins = three(out, c.w_hi[:, b % RING, w], c.w_lo[:, b % RING, w], x_hi[k], x_lo[k],
                        k == 0, k == len(x_hi) - 1)
            if t == TILES - 1:
                ins.then_inc(c.block_used, 1)

    def token_major(keys, x_hi, x_lo, n_in, needs=None):
        outs = [claim(key) for key in keys]
        first, last = block[keys[0]]
        for k in range(n_in):
            b, half = first + k // 2, k % 2
            if half == 0:
                pe.wait_ge(c.w_lo_ready, b + 1)
            if needs:
                needs(k)
            w = slice(half * T, half * T + T)
            for tt in range(NT):
                t = slice(tt * P, tt * P + P)
                ins = three(outs[tt][:, :], x_hi[:, k, t], x_lo[:, k, t], c.w_hi[:, b % RING, w], c.w_lo[:, b % RING, w],
                            k == 0, k == n_in - 1)
            if half:
                ins.then_inc(c.block_used, 1)

    def sum_squares(key, over, n=1, rows=P):
        out = claim(key)
        for k in range(n):
            i = sums[0]
            pe.wait_ge(c.sq_ready, i + 1)
            mm(out[0:rows, :], over, c.sq[0:rows, i % 2, :], start=k == 0, stop=k == n - 1).then_inc(c.sq_used, 1)
            sums[0] += 1

    def tiles(t, n=KT, first=0):
        return [t[:, first + k, :] for k in range(n)]

    def parted(*key, first=0):
        return lambda k: pe.wait_ge(c.split_lo, split[(*key, first + k)] + 1)

    def parted_y(k):
        parted("ya")(k) if k < 4 else parted("yb")(k - 4)

    h_hi, h_lo = tiles(c.h_hi), tiles(c.h_lo)
    a_hi, a_lo = tiles(c.a_hi), tiles(c.a_lo)

    def mlp(layer):
        n = 2 * layer + 1
        sum_squares(("ssq", n), ones, KT)
        for q in range(FF_PARTS):
            for m in range(KT):
                gemm(("up", layer, q, m), h_hi, h_lo, needs=parted("h", n) if q == m == 0 else None)
            for m in range(KT):
                gemm(("down", layer, q, m), a_hi, a_lo, needs=parted("a", layer, q) if m == 0 else None)

    pe.wait_ge(c.common_loaded, 16)
    sum_squares(("ssq", 0), ones, KT)
    gemm(("ab",), h_hi, h_lo, needs=parted("h", 0))
    for i in range(12):
        gemm(("qkv", i), h_hi, h_lo)
    for i in range(4):
        gemm(("z", i), h_hi, h_lo)
    for i in range(4):
        for name in ("cg", "hs", "bg"):
            gemm((name, i), h_hi, h_lo)

    k0 = {n: c.phase0[:, a:a + w] for n, (a, w) in PHASE0.items()}
    pe.wait_ge(c.phase0_loaded, 16)
    for i in range(8):
        sum_squares(("l2", i), k0["blk64"])

    out = claim(("gT",))
    pe.wait_ge(c.g_ready, 1)
    read(("ab",))
    for n, row in enumerate((c.g_row, c.beta_row)):
        for ch in range(NT):
            ins = nc.tensor.transpose(out[:, 32 * n + 8 * ch:32 * n + 8 * ch + 8], row[0:8, ch * P:ch * P + P], ident[0:8, 0:8])
    ins.then_inc(fill(("gT",)), 1)
    out = claim(("gc",))
    read(("gT",))
    mm(out[:, 0:32], k0["triu"], c.tok[:, 0, :], start=True, stop=True).then_inc(fill(("gc",)), 1)
    out = claim(("gl",))
    read(("gc",))
    mm(out[:, 0:32], k0["last"], c.tok[:, 2, :], start=True, stop=True).then_inc(fill(("gl",)), 1)
    out = claim(("gcr",))
    for ch in range(NT):
        ins = nc.tensor.transpose(out[0:8, ch * P:ch * P + P], c.tok[:, 2, 8 * ch:8 * ch + 8], ident)
    ins.then_inc(fill(("gcr",)), 1)
    for p in range(4):
        out = claim(("bb", p))
        mm(out[:, :], k0["pair_row"][0:8, p * P:p * P + P], c.beta_row[0:8, :], start=True, stop=True)\
            .then_inc(fill(("bb", p)), 1)
    pe.wait_ge(c.l2_ready, 8)
    for ch in range(NT):
        for name, first in (("kt", 4), ("vt", 8)):
            out = claim((name, ch))
            if name == "vt" and ch == 0:
                pe.wait_ge(c.silu_done, 12)
            for p in range(4):
                ins = nc.tensor.transpose(out[:, p * P:p * P + P], c.qkv[:, first + p, ch * P:ch * P + P], ident)
            ins.then_inc(fill((name, ch)), 1)

    read(("gcr",))
    for p in range(4):
        read(("bb", p))
    chunks = [slice(ch * P, ch * P + P) for ch in range(NT)]
    for p in range(4):
        for s in range(2):
            h = 2 * p + s
            out = claim(("gcb", h))
            mm(out[:, :], k0["head_row"][0:8, h * P:h * P + P], c.gc_row[0:8, :], start=True, stop=False)
            mm(out[:, :], ident, k0["notyet"], start=False, stop=True).then_inc(fill(("gcb", h)), 1)
        for name in ("kk", "qk"):
            for s in range(2):
                r = slice(64 * s, 64 * s + 64)
                out = claim((name, 2 * p + s))
                for t in chunks:
                    right = c.kb[r, p, t] if name == "kk" else c.qkv[r, p, t]
                    ins = mm(out[:, t], c.qkv[r, 4 + p, t], right, start=True, stop=True)
                ins.then_inc(fill((name, 2 * p + s)), 1)
        for level in range(7):
            if level:
                for s in range(2):
                    h, n = 2 * p + s, (6 * p + level - 1) * 2 + s
                    out = claim(("y", h, level))
                    pe.wait_ge(c.ml_ready, n + 1)
                    read(("xt", h, level - 1))
                    for t in chunks:
                        ins = mm(out[:, t], c.ML[:, s, t], c.X[:, s, t], start=True, stop=True)
                    ins.then_inc(fill(("y", h, level)), 1)
                for s in range(2):
                    h = 2 * p + s
                    out = claim(("yx", h, level))
                    read(("y", h, level))
                    for t in chunks:
                        ins = mm(out[:, t], c.Y[:, s, t], c.XT[:, s, t], start=True, stop=True)
                    ins.then_inc(fill(("yx", h, level)), 1)
            if level < 6:
                for s in range(2):
                    h = 2 * p + s
                    out = claim(("xt", h, level))
                    if level:
                        read(("yx", h, level))
                    else:
                        pe.wait_ge(c.xt_ready, h + 1)
                    for t in chunks:
                        ins = nc.tensor.transpose(out[:, t], c.XT[:, s, t], ident)
                    ins.then_inc(fill(("xt", h, level)), 1)
        for s in range(2):
            h = 2 * p + s
            out = claim(("u", h))
            read(("yx", h, 6))
            if p == s == 0:
                read(("kt", NT - 1))
                read(("vt", NT - 1))
            for ch, t in enumerate(chunks):
                ins = mm(out[:, ch * 64:ch * 64 + 64], c.XT[:, s, t], c.vb[:, ch, h * 64:h * 64 + 64], start=True, stop=True)
            ins.then_inc(fill(("u", h)), 1)
            out = claim(("w", h))
            for ch, t in enumerate(chunks):
                ins = mm(out[64 * s:64 * s + 64, t], c.kbe[:, ch, h * 64:h * 64 + 64], c.XT[:, s, t], start=True, stop=True)
            ins.then_inc(fill(("w", h)), 1)
    for p in range(4):
        out = claim(("eg", p))
        mm(out[:, :], k0["pair_row"][0:8, p * P:p * P + P], c.gc_row[0:8, :], start=True, stop=True)\
            .then_inc(fill(("eg", p)), 1)

    for h in range(GDN_H):
        read(("w", h))
    pe.wait_ge(c.qe_ready, 4)
    for ch, t in enumerate(chunks):
        if ch:
            read(("ds", ch - 1))
            for s in range(2):
                out, r = claim(("ws", ch, s)), slice(64 * s, 64 * s + 64)
                for p in range(4):
                    ins = mm(out[:, p * 64:p * 64 + 64], c.wT[r, p, t], c.S[r, p, :], start=True, stop=True)
                ins.then_inc(fill(("ws", ch, s)), 1)
        out = claim(("o", ch))
        if ch:
            read(("ws", ch, 1))
        else:
            pe.wait_ge(c.vnew_ready, 1)
        for h in range(GDN_H):
            r, p = slice(64 * (h % 2), 64 * (h % 2) + 64), h // 2
            o = out[r, p * P:p * P + P]
            if ch:
                mm(o, c.S[r, p, :], c.qkv[r, p, t], start=True, stop=False)
            ins = mm(o, c.vnew[:, h * 64:h * 64 + 64], (c.AT0, c.AT1)[h // 4][:, h % 4, t], start=ch == 0, stop=True)
        ins.then_inc(fill(("o", ch)), 1)
        out = claim(("ds", ch))
        for h in range(GDN_H):
            r, p = slice(64 * (h % 2), 64 * (h % 2) + 64), h // 2
            ins = mm(out[r, p * 64:p * 64 + 64], c.kd[:, ch, h * 64:h * 64 + 64], c.vnew[:, h * 64:h * 64 + 64],
                     start=True, stop=True)
        ins.then_inc(fill(("ds", ch)), 1)
    for p in range(4):
        sum_squares(("on", p), k0["blk64"])
    for m in range(KT):
        gemm(("out", 0, m), a_hi, a_lo, needs=parted_y if m == 0 else None)
    mlp(0)

    sum_squares(("ssq", 2), ones, KT)
    gemm(("gl_gates",), h_hi, h_lo, needs=parted("h", 2))
    for name, n in (("kc", 2), ("vc", 2), ("q", 8), ("ks", 2), ("kw", 2)):
        for i in range(n):
            gemm((name, i), h_hi, h_lo)
    token_major([("v", tt) for tt in range(NT)], c.h_hi, c.h_lo, KT)
    for kv in range(2):
        read((("kc", "vc")[kv], 1))
        for m in range(2):
            rows = [[t[:, kv, :, pp:pp + 8 * (N_CMP - 1) + 1:8] for pp in range(16)] for t in (c.kc_hi, c.kc_lo)]
            gemm(("cmp1", kv, m), rows[0], rows[1], cols=5 * N_CMP,
                 view=lambda o: o.rearrange("p (g c) -> p g c", g=5))
    out = claim(("gateT",))
    read(("gl_gates",))
    for tt in range(NT):
        ins = nc.tensor.transpose(out[:, 48 * tt:48 * tt + 48], c.gate_row[0:48, tt * P:tt * P + P], ident[0:48, 0:48])
    ins.then_inc(fill(("gateT",)), 1)
    pa = {n: c.params[:, a:a + w] for n, (a, w) in PARAMS.items()}
    out = claim(("kcb",))
    read(("cmp1", 0, 0))
    read(("cmp1", 0, 1))
    for k in range(2):
        ins = mm(out[:, 0:P], pa["cmp_k_w2"][:, k * P:k * P + P], c.hid_k[:, k, :], start=k == 0, stop=k == 1)
    ins.then_inc(fill(("kcb",)), 1)
    out = claim(("vcb",))
    read(("cmp1", 1, 0))
    read(("cmp1", 1, 1))
    for g in range(NSA_G):
        for k in range(2):
            ins = mm(out[:, g * 64:g * 64 + 64], c.hid_v[:, k, g * P:g * P + P], pa["cmp_v_w2"][:, k * 64:k * 64 + 64], start=k == 0, stop=k == 1)
    ins.then_inc(fill(("vcb",)), 1)

    read(("kcb",))
    read(("q", 7))
    for qt in range(NT):
        for s in range(2):
            out, r = claim(("sc", qt, s)), slice(64 * s, 64 * s + 64)
            for j in range(8):
                g = 2 * (j // 4) + s
                ins = mm(out[:, j * 32:j * 32 + 32], c.q[r, j, qt * P:qt * P + P], c.kcb[r, g * 32:g * 32 + 32], start=True, stop=True)
            ins.then_inc(fill(("sc", qt, s)), 1)
    for qt in range(NT):
        out = claim(("pcT", qt))
        pe.wait_ge(c.cmp_p, qt + 1)
        for i in range(4):
            ins = nc.tensor.transpose(out[:, i * P:i * P + P], c.cmp_e[:, qt % 2, i * P:i * P + P], ident)
        ins.then_inc(fill(("pcT", qt)), 1)

    pe.wait_ge(c.phase1_loaded, 16)
    k1 = {n: c.phase1[:, a:a + w] for n, (a, w) in PHASE1.items()}
    read(("kw", 1))
    for i in range(12):
        out = claim(("rope", i))
        src = c.q[:, i, :] if i < 8 else (c.ks, c.kw)[(i - 8) // 2][:, i % 2, :]
        mm(out[:, :], k1["rot"], src, start=True, stop=True).then_inc(fill(("rope", i)), 1)
    pe.wait_ge(c.rope_ready, 12)
    read(("vcb",))
    for qt in range(NT):
        read(("v", qt))
        read(("pcT", qt))
    items = [(j, s, qt) for j in range(8) for s in range(2) for qt in range(NT)]
    for i in range(len(items) + 2):
        if i < len(items):
            j, s, qt = items[i]
            r, end = slice(64 * s, 64 * s + 64), (qt + 1) * P
            for br, keys in enumerate((c.ks, c.kw)):
                key = ("s1", j, s, qt, br)
                out = claim(key)
                mm(out[:, 0:end], c.q[r, j, qt * P:end], keys[r, j // 4, 0:end], start=True, stop=False)
                mm(out[:, qt * P:end], ident, k1["causal"], start=False, stop=True).then_inc(fill(key), 1)
        if 1 <= i <= len(items):
            j, s, qt = items[i - 1]
            for br in range(2):
                key, n = ("t1", j, s, qt, br), 2 * (i - 1) + br
                out = claim(key)
                read(("s1", j, s, qt, br))
                pe.wait_ge(c.diag_ready, n + 1)
                for kt in range(qt + 1):
                    ins = mm(out[:, kt * P:kt * P + P], c.prob[:, n % 4, kt * P:kt * P + P], c.diag[:, n % 4, :],
                             start=True, stop=True)
                ins.then_inc(fill(key), 1)
        if i >= 2:
            j, s, qt = items[i - 2]
            n, g = 2 * j + s, 2 * (j // 4) + s
            if s == qt == 0:
                out_o = claim(("o1", j))
            o = out_o[64 * s:64 * s + 64, qt * P:qt * P + P]
            for br in range(2):
                m = 2 * (i - 2) + br
                read(("t1", j, s, qt, br))
                for kt in range(qt + 1):
                    mm(o, c.v[:, kt, br * 256 + g * 64:br * 256 + g * 64 + 64], c.probT[:, m % 4, kt * P:kt * P + P],
                       start=br == kt == 0, stop=False)
            r = slice(32 * (n % 4), 32 * (n % 4) + 32)
            ins = mm(o, c.vcb[r, g, :], c.pcT[r, n // 4, qt * P:qt * P + P], start=False, stop=True)
            if s == 1 and qt == NT - 1:
                ins.then_inc(c.attn_out, 1)
    for m in range(KT):
        gemm(("out", 1, m), a_hi, a_lo, needs=(lambda k: read(("o1", k))) if m == 0 else None)
    mlp(1)
    sum_squares(("ssq", "final"), ones, KT)

    k2 = {n: c.phase2[:, a:a + w] for n, (a, w) in PHASE2.items()}
    for l in range(LAYERS2):
        sum_squares(("ssq", 4 + l), ones, KT)
        for name, n in (("cq", 2), ("ckv", 2), ("kpe", 1), ("uf", 4)):
            for i in range(n):
                gemm((name, l, i), h_hi, h_lo, needs=parted("h", 4 + l) if name == "cq" and i == 0 else None)
        for which in range(2):
            sum_squares(("lat", l, which), ones, 2)
        cn_hi, cn_lo = tiles(c.cn_hi, 4), tiles(c.cn_lo, 4)
        for h in range(MLA_H):
            gemm(("uq", l, h), cn_hi[0:2], cn_lo[0:2], tile0=2 * (h % 4), needs=parted("cn", l) if h == 0 else None)
        for i in range(4):
            gemm(("kn", l, i), cn_hi[2:4], cn_lo[2:4], tile0=2 * i, needs=parted("cn", l, first=2) if i == 0 else None)
        token_major([("v2", l, tt) for tt in range(NT)], c.cn_hi[:, 2:4, :], c.cn_lo[:, 2:4, :], 2)

        if l == 0:
            pe.wait_ge(c.phase2_loaded, 16)
        for which in range(2):
            for h in range(MLA_H):
                i = MLA_H * which + h
                sum_squares(("hs2", l, which, h), ones[0:MLA_QK, 0:MLA_QK], rows=MLA_QK)
                out = claim(("rot2", l, which, h))
                n = (l * 2 + which) * MLA_H + h
                pe.wait_ge(c.head_t_ready, n + 1)
                mm(out[0:MLA_QK, :], k2["rot"][0:MLA_QK, 0:MLA_QK], c.head_t[0:MLA_QK, n % 2, :], start=True, stop=True)\
                    .then_inc(fill(("rot2", l, which, h)), 1)
                if i % 2:
                    gemm((("za", "zf")[i // 2 // 4], l, i // 2 % 4), h_hi, h_lo)
        pe.wait_ge(c.head_ready, (l + 1) * 2 * MLA_H)
        for tt in range(NT):
            read(("v2", l, tt))
        items = [(j, s, qt) for j in range(4) for s in range(2) for qt in range(NT)]
        base = l * len(items)
        for i in range(len(items) + 2):
            if i < len(items):
                j, s, qt = items[i]
                key, h = ("s2", l, j, s, qt), 2 * j + s
                out = claim(key)
                mm(out[:, :], c.q2[0:MLA_QK, h, qt * P:qt * P + P], c.k2[0:MLA_QK, h, :], start=True, stop=True)\
                    .then_inc(fill(key), 1)
            if 1 <= i <= len(items):
                j, s, qt = items[i - 1]
                key, key_s, n = ("t2", l, j, s, qt), ("s2", l, j, s, qt), i - 1
                out = claim(key)
                read(key_s)
                pe.wait_ge(c.diag2_ready, base + n + 1)
                for kt in range(NT):
                    ins = mm(out[:, kt * P:kt * P + P], c.prob2[:, n % 2, kt * P:kt * P + P], c.diag2[:, n % 2, :],
                             start=True, stop=True)
                ins.then_inc(fill(key), 1)
            if i >= 2:
                j, s, qt = items[i - 2]
                n, h = i - 2, 2 * j + s
                if s == qt == 0:
                    out_o = claim(("o2", l, j))
                o = out_o[64 * s:64 * s + 64, qt * P:qt * P + P]
                read(("t2", l, j, s, qt))
                for kt in range(NT):
                    ins = mm(o, c.v2[:, kt, h * 64:h * 64 + 64], c.probT2[:, n % 2, kt * P:kt * P + P],
                             start=kt == 0, stop=kt == NT - 1)
                if s == 1 and qt == NT - 1:
                    ins.then_inc(c.attn_out, 1)

        for g in range(FG):
            read(("uf", l, g))
        for g in range(FG):
            for tt in range(NT):
                key = ("dd", l, g, tt)
                out = claim(key)
                mm(out[:, 0:2 * P], c.u_f[:, g, tt * P:tt * P + P], k2["dft_d"], start=True, stop=True).then_inc(fill(key), 1)
        outs = [claim(("f", l, g)) for g in range(FG)]
        first = block[("f", l, 0)][0]
        for g in range(FG):
            for tt in range(NT):
                read(("dd", l, g, tt))
        for tt in range(NT):
            pe.wait_ge(c.w_lo_ready, first + tt + 1)
            for part in range(2):
                w, d = slice(part * T, part * T + T), slice(part * P, part * P + P)
                for g in range(FG):
                    slot = (first + tt) % RING
                    ins = three(outs[g][:, :], c.d_hi[:, tt, g, d], c.d_lo[:, tt, g, d], c.w_hi[:, slot, w], c.w_lo[:, slot, w],
                                tt == part == 0, tt == NT - 1 and part == 1)
            ins.then_inc(c.block_used, 1)
        for m in range(KT):
            gemm(("ga", l, m, 0), h_hi, h_lo)
            gemm(("gf", l, m, 0), h_hi, h_lo)
            gemm(("ya2", l, m), a_hi[0:4], a_lo[0:4], needs=parted("oa", l) if m == 0 else None)
            gemm(("yf2", l, m), a_hi[4:8], a_lo[4:8], tile0=4, needs=parted("of", l) if m == 0 else None)
        m_hi, m_lo = tiles(c.m_hi), tiles(c.m_lo)
        for m in range(KT):
            gemm(("out2", l, m), m_hi, m_lo, needs=parted("m", l) if m == 0 else None)


def x_final(eng, c, bank, n, k):
    if n == 0:
        eng.wait_ge(c.x_loaded, 16)
        return
    if n == 4:
        eng.wait_ge(c.final_ready, k + 1)
        return
    key = {1: ("out", 0, k), 2: ("down", 0, FF_PARTS - 1, k), 3: ("out", 1, k), "final": ("down", 1, FF_PARTS - 1, k),
           5: ("out2", 0, k)}[n]
    b, use, _ = bank[key]
    eng.wait_ge(c.bank_read[b], use + 1)


def source_numbers(split):
    return {key: n for n, key in enumerate(k for k in split if k[0] in ("h", "ya", "a", "cn", "m"))}


def program_scalar(act, nc, c, block, bank, split, n_blocks):
    f = nc.scalar.activation
    source = source_numbers(split)
    pa = {n: c.params[:, a:a + w] for n, (a, w) in PARAMS.items()}
    eps = pa["eps"]
    count = {"w": 0, "sq": 0, "used": 0, "rstd": 0, "step": 0}

    def weights(upto):
        while count["w"] <= min(upto, n_blocks - 1):
            b = count["w"]
            act.wait_ge(c.raw_loaded[b % RING], 16 * (b // RING + 1))
            if b >= RING:
                act.wait_ge(c.block_used, b - RING + 1)
            f(c.w_hi[:, b % RING, :], c.raw[:, b % RING, :], ACT.Copy).then_inc(c.w_hi_ready, 1)
            count["w"] += 1

    def product(key):
        weights(block[key][1] + 2)
        act.wait_ge(c.block_used, block[key][1] + 1)
        return c.psum[bank[key][0]]

    def filled(key):
        b, _, n = bank[key]
        act.wait_ge(c.bank_filled[b], n + 1)
        return c.psum[b]

    def read(key):
        b, n, _ = bank[key]
        act.wait_ge(c.bank_read[b], n + 1)

    def release(key):
        return c.bank_read[bank[key][0]]

    def step(ins):
        ins.then_inc(c.scalar_step, 1)
        count["step"] += 1
        act.wait_ge(c.scalar_step, count["step"])

    def square(src, rows=P):
        i = count["sq"]
        if i >= 2:
            act.wait_ge(c.sq_used, i - 1)
        f(c.sq[0:rows, i % 2, :], src, ACT.Square).then_inc(c.sq_ready, 1)
        count["sq"] += 1

    def rstd(key, width, n=1, rows=P):
        count["used"] += n
        act.wait_ge(c.sq_used, count["used"])
        out = c.rstd[0:rows, count["rstd"] % 2, :]
        f(out, c.psum[bank[key][0]][0:rows, :], ACT.Ln, bias=eps[0:rows, :], scale=1.0 / width).then_inc(release(key), 1)
        read(key)
        f(out, out, ACT.Exp, scale=-0.5).then_inc(c.rstd_ready, 1)
        count["rstd"] += 1

    def hi(key, dst, after=None):
        if after:
            read(after)
        else:
            act.wait_ge(c.split_src, source[key] + 1)
        f(dst, c.stage[:, split[key] % 3, :], ACT.Copy).then_inc(c.split_hi, 1)

    def norm(n):
        for k in range(KT):
            x_final(act, c, bank, n, k)
            square(c.x[:, k, :])
        rstd(("ssq", n), D, KT)
        if n != "final":
            for k in range(KT):
                hi(("h", n, k), c.h_hi[:, k, :])

    def passed(*key):
        weights(block[key][1] + 2)

    def mlp(layer):
        norm(2 * layer + 1)
        for q in range(FF_PARTS):
            for m in range(KT):
                key, i = ("up", layer, q, m), (layer * FF_PARTS + q) * KT + m
                out = product(key)
                f(c.relu[:, i % 2, :], out[:, :], ACT.Relu).then_inc(release(key), 1)
                if m:
                    hi(("a", layer, q, m - 1), c.a_hi[:, m - 1, :])
            hi(("a", layer, q, KT - 1), c.a_hi[:, KT - 1, :])
            for m in range(KT):
                passed("down", layer, q, m)

    act.dma_start(c.common[:, :], c.in_common).then_inc(c.common_loaded, 16)
    act.dma_start(c.params[:, :], c.in_params).then_inc(c.params_loaded, 16)
    act.dma_start(c.phase0[:, :], c.in_phase0).then_inc(c.phase0_loaded, 16)
    weights(1)
    act.wait_ge(c.params_loaded, 16)
    norm(0)
    key = ("ab",)
    out = product(key)
    act.wait_ge(c.g_x_ready, 1)
    f(c.beta_row[0:8, :], out[32:40, :], ACT.Sigmoid).then_inc(release(key), 1)
    for i in range(12):
        product(("qkv", i))
        read(("qkv", i))
        f(c.qkv[:, i, :], c.qkv[:, i, :], ACT.Silu).then_inc(c.silu_done, 1)
    for i in range(4):
        out = product(("z", i))
        f(c.z[:, i, :], out[:, :], ACT.Silu).then_inc(release(("z", i)), 1)
    for i in range(4):
        passed("bg", i)
        if i:
            hi(("yb", i - 1), c.a_hi[:, 3 + i, :], after=("bg", i - 1))
    hi(("yb", 3), c.a_hi[:, 7, :], after=("bg", 3))
    act.wait_ge(c.silu_done, 8)
    for i in range(9):
        if i < 8:
            square(c.qkv[:, i, :])
        if i:
            if i >= 3:
                act.wait_ge(c.l2_ready, i - 2)
            rstd(("l2", i - 1), 1.0)
    act.wait_ge(c.g_e_ready, 1)
    step(f(c.e_row[0:8, :], c.e_row[0:8, :], ACT.Exp, scale=-1.0))
    f(c.e_row[0:8, :], c.e_row[0:8, :], ACT.Ln, bias=c.common[0:8, P:P + 1]).then_inc(c.g_ln_ready, 1)
    f(c.tiny[0:8, 0:1], pa["a_log"][0:8, :], ACT.Exp).then_inc(c.a_exp_ready, 1)
    act.wait_ge(c.ekd_in, 1)
    f(c.tok[:, 3, :], c.tok[:, 7, :], ACT.Exp).then_inc(c.ekd_ready, 1)
    f(c.tok[:, 4, :], c.tok[:, 2, :], ACT.Exp).then_inc(c.egt_ready, 1)
    for p in range(4):
        for s in range(2):
            h = 2 * p + s
            out = filled(("gcb", h))
            for ch in range(NT):
                t = slice(ch * P, ch * P + P)
                ins = f(c.ML[:, s, t], out[:, t], ACT.Exp, bias=c.tok[:, 6, 8 * ch + h:8 * ch + h + 1])
            ins.then_inc(release(("gcb", h)), 1)
        for level in range(7):
            if level:
                for s in range(2):
                    key = ("y", 2 * p + s, level)
                    f(c.Y[:, s, :], filled(key)[:, :], ACT.Copy).then_inc(release(key), 1)
            if level < 6:
                for s in range(2):
                    key = ("xt", 2 * p + s, level)
                    f(c.X[:, s, :], filled(key)[:, :], ACT.Copy).then_inc(release(key), 1)
        for s in range(2):
            key, r = ("w", 2 * p + s), slice(64 * s, 64 * s + 64)
            f(c.wT[r, p, :], filled(key)[r, :], ACT.Copy).then_inc(release(key), 1)
    for p in range(4):
        f(c.egc[:, p, :], filled(("eg", p))[:, :], ACT.Exp).then_inc(release(("eg", p)), 1)
    read(("o", NT - 1))
    first = source[("ya", 0)]
    for p in range(5):
        if p < 4:
            square(c.gdn_o[:, p, :])
        if p:
            if p >= 3:
                act.wait_ge(c.split_src, first + p - 2)
            rstd(("on", p - 1), GDN_D)
    for p in range(4):
        hi(("ya", p), c.a_hi[:, p, :])
    for m in range(KT):
        passed("out", 0, m)
    act.dma_start(c.phase1[:, :], c.in_phase1).then_inc(c.phase1_loaded, 16)
    mlp(0)

    norm(2)
    key = ("gl_gates",)
    f(c.gate_row[0:48, :], product(key)[0:48, :], ACT.Sigmoid).then_inc(release(key), 1)
    act.wait_ge(c.kc_pad, 2)
    for kv in range(2):
        f(c.kc_hi[:, kv, 4, 0:16], pa["cmp_pos"], ACT.Copy).then_inc(c.kc_hi_ready, 1)
        for i in range(2):
            out = product((("kc", "vc")[kv], i))
            for g in range(2):
                for s in range(2):
                    f(c.kc_hi[64 * s:64 * s + 64, kv, 2 * i + g, 0:T // 2], out[64 * g:64 * g + 64, s:T:2], ACT.Copy)\
                        .then_inc(c.kc_hi_ready, 1)
    passed("q", 7)
    passed("kw", 1)
    for tt in range(NT):
        key = ("v", tt)
        f(c.v[:, tt, :], product(key)[:, :], ACT.Copy).then_inc(release(key), 1)
    for kv in range(2):
        for m in range(2):
            key, i = ("cmp1", kv, m), 2 * kv + m
            out = product(key)
            act.wait_ge(c.hid_bias, i + 1)
            dst, src = c.hid_k[:, m, :], out[:, 0:P]
            if kv:
                dst = c.hid_v[:, m, :].rearrange("p (g n c) -> p g n c", g=4, n=4)
                src = src.rearrange("p (g c) -> p g c", g=4).unsqueeze(2).to_broadcast([P, 4, 4, N_CMP])
            f(dst, src, ACT.Silu, bias=c.tiny[:, 8 + i:9 + i]).then_inc(release(key), 1)
    f(c.kcb[:, :], filled(("kcb",))[:, 0:P], ACT.Copy).then_inc(release(("kcb",)), 1)
    f(c.vcb[:, :, :].rearrange("p g d -> p (g d)"), filled(("vcb",))[:, 0:4 * NSA_D], ACT.Copy).then_inc(release(("vcb",)), 1)
    for qt in range(NT + 1):
        if qt < NT:
            act.wait_ge(c.cmp_shift, qt + 1)
            f(c.cmp_e[:, qt % 2, :], c.cmp_s[:, qt % 2, :], ACT.Exp).then_inc(c.cmp_exp, 1)
        if qt:
            key = ("pcT", qt - 1)
            f(c.pcT[:, :, (qt - 1) * P:qt * P], filled(key)[:, :].rearrange("p (i q) -> p i q", i=4), ACT.Copy)\
                .then_inc(release(key), 1)
    items = [(j, s, qt) for j in range(8) for s in range(2) for qt in range(NT)]
    for i in range(len(items) + 2):
        if i < len(items):
            j, s, qt = items[i]
            for br in range(2):
                n, key, end = 2 * i + br, ("s1", j, s, qt, br), (qt + 1) * P
                act.wait_ge(c.nb_ready, n + 1)
                f(c.prob[:, n % 4, 0:end], c.psum[bank[key][0]][:, 0:end], ACT.Exp, bias=c.nb[:, n % 4, 0:1],
                  accum_out=c.nb[:, n % 4, 1:2]).then_inc(release(key), 1)
        if 1 <= i <= len(items):
            j, s, qt = items[i - 1]
            for br in range(2):
                n, key, end = 2 * (i - 1) + br, ("t1", j, s, qt, br), (qt + 1) * P
                f(c.probT[:, n % 4, 0:end], filled(key)[:, 0:end], ACT.Copy).then_inc(release(key), 1)
        if i >= 2 and items[i - 2][1:] == (1, NT - 1):
            j = items[i - 2][0]
            act.wait_ge(c.attn_out, j + 1)
            f(c.a_hi[:, j, :], c.psum[bank[("o1", j)][0]][:, :], ACT.Copy).then_inc(c.attn_hi, 1)
    for m in range(KT):
        passed("out", 1, m)
    act.wait_ge(c.rope_ready, 12)
    act.dma_start(c.phase2[:, :], c.in_phase2).then_inc(c.phase2_loaded, 16)
    mlp(1)
    norm("final")

    for l in range(LAYERS2):
        norm(4 + l)
        for i in range(2):
            passed("ckv", l, i)
        passed("kpe", l, 0)
        for g in range(FG):
            key = ("uf", l, g)
            f(c.u_f[:, g, :], product(key)[:, :], ACT.Copy).then_inc(release(key), 1)
        for which, name in enumerate(("cq", "ckv")):
            for i in range(2):
                read((name, l, i))
                square(c.c[:, 2 * which + i, :])
            rstd(("lat", l, which), 2 * P, 2)
        for i in range(4):
            hi(("cn", l, i), c.cn_hi[:, i, :])
        for h in range(MLA_H):
            key = ("uq", l, h)
            f(c.q2[0:MLA_QK, h, :], product(key)[0:MLA_QK, :], ACT.Copy).then_inc(release(key), 1)
        passed("kn", l, 3)
        for tt in range(NT):
            key = ("v2", l, tt)
            f(c.v2[:, tt, :], product(key)[:, :], ACT.Copy).then_inc(release(key), 1)
        heads = [(which, h) for which in range(2) for h in range(MLA_H)]
        done = l * len(heads)
        for i in range(len(heads) + 1):
            if i < len(heads):
                which, h = heads[i]
                if which:
                    read(("kn", l, h // 2))
                    act.wait_ge(c.kpe_ready, l + 1)
                else:
                    read(("uq", l, h))
                square((c.k2 if which else c.q2)[0:MLA_QK, h, :], MLA_QK)
            if i:
                which, h = heads[i - 1]
                if i >= 3:
                    act.wait_ge(c.head_ready, done + i - 2)
                rstd(("hs2", l, which, h), MLA_QK, rows=MLA_QK)
                if i % 2 == 0:
                    z = i // 2 - 1
                    key, dst = ((("za", "zf")[z // 4]), l, z % 4), (c.z_a, c.z_f)[z // 4]
                    f(dst[:, z % 4, :], product(key)[:, :], ACT.Copy).then_inc(release(key), 1)
        read(("zf", l, 3))
        f(c.z_a[:, :, :], c.z_a[:, :, :], ACT.Silu).then_inc(c.z_ready, 1)
        f(c.z_f[:, :, :], c.z_f[:, :, :], ACT.Silu).then_inc(c.z_ready, 1)
        items = [(j, s, qt) for j in range(4) for s in range(2) for qt in range(NT)]
        base = l * len(items)
        for i in range(len(items) + 3):
            if i < len(items):
                key = ("s2", l, *items[i])
                act.wait_ge(c.nb2_ready, base + i + 1)
                f(c.prob2[:, i % 2, :], c.psum[bank[key][0]][:, :], ACT.Exp, bias=c.nb2[:, i % 2, 0:1],
                  accum_out=c.nb2[:, i % 2, 1:2]).then_inc(release(key), 1)
            if 1 <= i <= len(items):
                key = ("t2", l, *items[i - 1])
                f(c.probT2[:, (i - 1) % 2, :], filled(key)[:, :], ACT.Copy).then_inc(release(key), 1)
            if i >= 3 and items[i - 3][1:] == (1, NT - 1):
                j = items[i - 3][0]
                hi(("oa", l, j), c.a_hi[:, j, :], after=("o2", l, j))
        for g in range(FG):
            for tt in range(NT):
                f(c.d_hi[:, tt, g, :], filled(("dd", l, g, tt))[:, 0:2 * P], ACT.Copy).then_inc(c.d_hi_ready, 1)
        for g in range(FG):
            product(("f", l, g))
            hi(("of", l, g), c.a_hi[:, 4 + g, :], after=("f", l, g))
        for m in range(KT):
            for branch, name in enumerate(("ga", "gf")):
                key, at = (name, l, m, 0), (l * 2 + branch) * KT + m
                f(c.sig[:, 2 * (m % 2) + branch, :], product(key)[:, :], ACT.Sigmoid, bias=pa["merge"][:, at:at + 1])\
                    .then_inc(release(key), 1)
            passed("yf2", l, m)
            if m:
                hi(("m", l, m - 1), c.m_hi[:, m - 1, :])
        hi(("m", l, KT - 1), c.m_hi[:, KT - 1, :])
        for m in range(KT):
            passed("out2", l, m)


def program_vector(dve, nc, c, block, bank, split):
    v = nc.vector
    tt_op, stt = v.tensor_tensor, v.scalar_tensor_tensor
    source = source_numbers(split)
    pa = {n: c.params[:, a:a + w] for n, (a, w) in PARAMS.items()}
    ident = c.common[:, 0:P]
    count = {"step": 0, "rstd": 0}

    def product(key):
        dve.wait_ge(c.block_used, block[key][1] + 1)
        return c.psum[bank[key][0]]

    def filled(key):
        b, _, n = bank[key]
        dve.wait_ge(c.bank_filled[b], n + 1)
        return c.psum[b]

    def read(key):
        b, n, _ = bank[key]
        dve.wait_ge(c.bank_read[b], n + 1)

    def release(key):
        return c.bank_read[bank[key][0]]

    def step(ins):
        ins.then_inc(c.vector_step, 1)
        count["step"] += 1
        dve.wait_ge(c.vector_step, count["step"])

    def rstd(rows=P):
        dve.wait_ge(c.rstd_ready, count["rstd"] + 1)
        count["rstd"] += 1
        return c.rstd[0:rows, (count["rstd"] - 1) % 2, :]

    def stage(key, writes=True):
        if writes and split[key] >= 3:
            dve.wait_ge(c.split_lo, split[key] - 2)
        return c.stage[:, split[key] % 3, :]

    def lo(key, hi, dst):
        dve.wait_ge(c.split_hi, split[key] + 1)
        tt_op(dst, stage(key, False), hi.bitcast(F32), ALU.subtract).then_inc(c.split_lo, 1)

    def norm(n, gain, g0):
        r = rstd()
        for k in range(KT + 1):
            if k < KT:
                x_final(dve, c, bank, n, k)
                w = pa[gain][:, g0 + k:g0 + k + 1]
                if n == "final":
                    stt(c.x[:, k, :], c.x[:, k, :], w, r, ALU.mult, ALU.mult).then_inc(c.final_ready, 1)
                else:
                    stt(stage(("h", n, k)), c.x[:, k, :], w, r, ALU.mult, ALU.mult).then_inc(c.split_src, 1)
            if k and n != "final":
                lo(("h", n, k - 1), c.h_hi[:, k - 1, :], c.h_lo[:, k - 1, :])

    def add_to_x(key, m):
        out = product(key)
        tt_op(c.x[:, m, :], c.x[:, m, :], out[:, :], ALU.add).then_inc(release(key), 1)

    def mlp(layer):
        norm(2 * layer + 1, "mlp_norm", layer * KT)
        for q in range(FF_PARTS):
            for m in range(KT + 1):
                if m < KT:
                    i = (layer * FF_PARTS + q) * KT + m
                    read(("up", layer, q, m))
                    r = c.relu[:, i % 2, :]
                    tt_op(stage(("a", layer, q, m)), r, r, ALU.mult).then_inc(c.split_src, 1)
                if m:
                    lo(("a", layer, q, m - 1), c.a_hi[:, m - 1, :], c.a_lo[:, m - 1, :])
            for m in range(KT):
                add_to_x(("down", layer, q, m), m)

    dve.wait_ge(c.params_loaded, 16)
    norm(0, "mix_norm", 0)
    x_row, e_row = c.g_row[0:8, :], c.e_row[0:8, :]
    out = product(("ab",))
    v.tensor_scalar(x_row, out[0:8, :], pa["dt_bias"][0:8, :], None, ALU.add).then_inc(c.g_x_ready, 1)
    dve.wait_ge(c.g_x_ready, 1)
    stt(e_row, x_row, -1.0, x_row, ALU.mult, ALU.max).then_inc(c.g_e_ready, 1)
    for i in range(12):
        out, y = product(("qkv", i)), c.qkv[:, i, :]
        tap = [pa["conv"][:, 4 * i + n:4 * i + n + 1] for n in range(4)]
        step(v.tensor_scalar(y, out[:, :], tap[3], None, ALU.mult))
        step(stt(y[:, 1:T], out[:, 0:T - 1], tap[2], y[:, 1:T], ALU.mult, ALU.add))
        step(stt(y[:, 2:T], out[:, 0:T - 2], tap[1], y[:, 2:T], ALU.mult, ALU.add))
        stt(y[:, 3:T], out[:, 0:T - 3], tap[0], y[:, 3:T], ALU.mult, ALU.add).then_inc(release(("qkv", i)), 1)
    for i in range(4):
        gated, y = c.sc[:, 1, :], c.sc[:, 2, :]
        tap = [pa["sc_conv"][:, 3 * i + n:3 * i + n + 1] for n in range(3)]
        v.tensor_copy(c.sc[:, 0, :], product(("cg", i))[:, :]).then_inc(release(("cg", i)), 1)
        out = product(("hs", i))
        read(("cg", i))
        tt_op(gated, out[:, :], c.sc[:, 0, :], ALU.mult).then_inc(release(("hs", i)), 1)
        read(("hs", i))
        step(v.tensor_scalar(y, gated, tap[2], None, ALU.mult))
        step(stt(y[:, 1:T], gated[:, 0:T - 1], tap[1], y[:, 1:T], ALU.mult, ALU.add))
        step(stt(y[:, 2:T], gated[:, 0:T - 2], tap[0], y[:, 2:T], ALU.mult, ALU.add))
        out = product(("bg", i))
        tt_op(stage(("yb", i)), out[:, :], y, ALU.mult).then_inc(release(("bg", i)), 1)
        lo(("yb", i), c.a_hi[:, 4 + i, :], c.a_lo[:, 4 + i, :])

    for i in range(8):
        r, y = rstd(), c.qkv[:, i, :]
        if i < 4:
            stt(y, y, GDN_D ** -0.5, r, ALU.mult, ALU.mult).then_inc(c.l2_ready, 1)
        else:
            tt_op(y, y, r, ALU.mult).then_inc(c.l2_ready, 1)
    dve.wait_ge(c.g_ln_ready, 1)
    step(stt(x_row, x_row, 0.0, e_row, ALU.max, ALU.add))
    dve.wait_ge(c.a_exp_ready, 1)
    v.tensor_scalar(x_row, x_row, c.tiny[0:8, 0:1], -1.0, ALU.mult, ALU.mult).then_inc(c.g_ready, 1)
    v.tensor_copy(c.tok[:, 0:2, :].rearrange("p a b -> p (a b)"), filled(("gT",))[:, 0:64]).then_inc(release(("gT",)), 1)
    v.tensor_copy(c.tok[:, 2, :], filled(("gc",))[:, 0:32]).then_inc(release(("gc",)), 1)
    read(("gc",))
    v.tensor_scalar(c.tok[:, 6, :], c.tok[:, 2, :], -1.0, None, ALU.mult)
    out = filled(("gl",))
    tt_op(c.tok[:, 7, :], out[:, 0:32], c.tok[:, 2, :], ALU.subtract).then_inc(release(("gl",)), 1)
    read(("gl",))
    v.tensor_copy(c.tiny[:, 1:2], c.tok[:, 7, 0:1]).then_inc(c.ekd_in, 1)
    v.tensor_copy(c.gc_row[0:8, :], filled(("gcr",))[0:8, :]).then_inc(release(("gcr",)), 1)
    for p in range(4):
        out = filled(("bb", p))
        tt_op(c.kb[:, p, :], out[:, :], c.qkv[:, 4 + p, :], ALU.mult).then_inc(release(("bb", p)), 1)
    dve.wait_ge(c.egt_ready, 1)
    step(tt_op(c.tok[:, 5, :], c.tok[:, 4, :], c.tok[:, 1, :], ALU.mult))

    def by_head(a):
        return a.rearrange("p (h d) -> p h d", h=GDN_H)

    for ch in range(NT):
        def per_token(n):
            return c.tok[:, n, 8 * ch:8 * ch + 8].unsqueeze(2).to_broadcast([P, GDN_H, GDN_D])
        key = ("kt", ch)
        out = by_head(filled(key)[:, :])
        tt_op(by_head(c.kd[:, ch, :]), out, per_token(3), ALU.mult)
        tt_op(by_head(c.kbe[:, ch, :]), out, per_token(5), ALU.mult).then_inc(release(key), 1)
        key = ("vt", ch)
        tt_op(by_head(c.vb[:, ch, :]), by_head(filled(key)[:, :]), per_token(1), ALU.mult).then_inc(release(key), 1)

    def by_chunk(a):
        return a.rearrange("p (n i) -> p n i", n=NT)

    def level_mask(level):
        a = PHASE0["levels"][0] + level * P
        return c.phase0[:, a:a + P].unsqueeze(1).to_broadcast([P, NT, P])

    eye = ident.unsqueeze(1).to_broadcast([P, NT, P])
    for p in range(4):
        for s in range(2):
            h = 2 * p + s
            read(("gcb", h))
            tt_op(c.MT[:, s, :], filled(("kk", h))[:, :], c.ML[:, s, :], ALU.mult).then_inc(release(("kk", h)), 1)
        for s in range(2):
            h = 2 * p + s
            tt_op((c.AT0, c.AT1)[h // 4][:, h % 4, :], filled(("qk", h))[:, :], c.ML[:, s, :], ALU.mult).then_inc(release(("qk", h)), 1)
        for s in range(2):
            read(("kk", 2 * p + s))
            read(("qk", 2 * p + s))
            step(tt_op(by_chunk(c.ML[:, s, :]), by_chunk(c.MT[:, s, :]), level_mask(0), ALU.mult))
            tt_op(by_chunk(c.XT[:, s, :]), eye, by_chunk(c.ML[:, s, :]), ALU.subtract).then_inc(c.xt_ready, 1)
        for level in range(1, 7):
            for s in range(2):
                if level == 1:
                    dve.wait_ge(c.xt_ready, 2 * p + s + 1)
                tt_op(by_chunk(c.ML[:, s, :]), by_chunk(c.MT[:, s, :]), level_mask(level), ALU.mult).then_inc(c.ml_ready, 1)
            for s in range(2):
                key = ("yx", 2 * p + s, level)
                tt_op(c.XT[:, s, :], c.XT[:, s, :], filled(key)[:, :], ALU.subtract).then_inc(release(key), 1)
        for s in range(2):
            key, h = ("u", 2 * p + s), 2 * p + s
            v.tensor_copy(c.u[:, :, h * 64:h * 64 + 64], filled(key)[:, 0:256].rearrange("p (n d) -> p n d", n=NT))\
                .then_inc(release(key), 1)
    for p in range(4):
        read(("eg", p))
        tt_op(c.qkv[:, p, :], c.qkv[:, p, :], c.egc[:, p, :], ALU.mult).then_inc(c.qe_ready, 1)
    for ch in range(NT):
        if ch:
            for s in range(2):
                key = ("ws", ch, s)
                half = [a.rearrange("p (a s d) -> p s a d", s=2, d=GDN_D)[:, s] for a in (c.vnew[:, :], c.u[:, ch, :])]
                out = filled(key)[:, 0:256].rearrange("p (a d) -> p a d", a=4)
                tt_op(half[0], half[1], out, ALU.subtract).then_inc(release(key), 1)
        else:
            read(("u", GDN_H - 1))
            v.tensor_copy(c.vnew[:, :], c.u[:, 0, :]).then_inc(c.vnew_ready, 1)
        t = slice(ch * P, ch * P + P)
        key = ("o", ch)
        v.tensor_copy(c.gdn_o[:, :, t], filled(key)[:, :].rearrange("p (a i) -> p a i", a=4)).then_inc(release(key), 1)
        key = ("ds", ch)
        out = filled(key)[:, 0:256].rearrange("p (a d) -> p a d", a=4)
        if ch:
            read(("ds", ch - 1))
            step(tt_op(c.S[:, :, :], c.S[:, :, :], c.egc[:, :, ch * P + P - 1:ch * P + P].to_broadcast([P, 4, GDN_D]), ALU.mult))
            tt_op(c.S[:, :, :], c.S[:, :, :], out, ALU.add).then_inc(release(key), 1)
        else:
            v.tensor_copy(c.S[:, :, :], out).then_inc(release(key), 1)
    for p in range(5):
        if p < 4:
            r, y = rstd(), c.gdn_o[:, p, :]
            read(("o", NT - 1))
            step(stt(y, y, pa["o_norm"], r, ALU.mult, ALU.mult))
            read(("z", p))
            tt_op(stage(("ya", p)), y, c.z[:, p, :], ALU.mult).then_inc(c.split_src, 1)
        if p:
            lo(("ya", p - 1), c.a_hi[:, p - 1, :], c.a_lo[:, p - 1, :])
    for m in range(KT):
        add_to_x(("out", 0, m), m)
    mlp(0)

    v.memset(c.kc_hi[:, :, :, :].bitcast(F32), 0.0).then_inc(c.kc_pad, 1)
    v.memset(c.kc_lo[:, :, :, :].bitcast(F32), 0.0).then_inc(c.kc_pad, 1)
    norm(2, "mix_norm", KT)
    dve.wait_ge(c.kc_pad, 2)
    n = 0
    for kv in range(2):
        n += 1
        dve.wait_ge(c.kc_hi_ready, n)
        tt_op(c.kc_lo[:, kv, 4, 0:16], pa["cmp_pos"], c.kc_hi[:, kv, 4, 0:16].bitcast(F32), ALU.subtract)
        for i in range(2):
            key = (("kc", "vc")[kv], i)
            out = product(key)
            n += 4
            dve.wait_ge(c.kc_hi_ready, n)
            for g in range(2):
                for s in range(2):
                    r = slice(64 * s, 64 * s + 64)
                    ins = tt_op(c.kc_lo[r, kv, 2 * i + g, 0:T // 2], out[64 * g:64 * g + 64, s:T:2],
                                c.kc_hi[r, kv, 2 * i + g, 0:T // 2].bitcast(F32), ALU.subtract)
            ins.then_inc(release(key), 1)
    for i in range(8):
        v.tensor_scalar(c.q[:, i, :], product(("q", i))[:, :], NSA_D ** -0.5, None, ALU.mult).then_inc(release(("q", i)), 1)
    for name, dst in (("ks", c.ks), ("kw", c.kw)):
        for i in range(2):
            v.tensor_copy(dst[:, i, :], product((name, i))[:, :]).then_inc(release((name, i)), 1)
    for kv in range(2):
        for m in range(2):
            i = 8 + 2 * kv + m
            v.tensor_copy(c.tiny[:, i:i + 1], product(("cmp1", kv, m))[:, P:P + 1]).then_inc(c.hid_bias, 1)
    v.tensor_copy(c.gate[:, :, :].rearrange("p a b -> p (a b)"), filled(("gateT",))[:, 0:NT * 48]).then_inc(release(("gateT",)), 1)
    read(("gateT",))
    a = PHASE1["cmp_mask"][0]
    dve.wait_ge(c.phase1_loaded, 16)
    for qt in range(NT + 1):
        if qt < NT:
            b = 4 * (qt % 2)
            sc = c.cmp_s[:, qt % 2, :].rearrange("p (h c) -> p h c", h=NSA_H)
            mask = c.phase1[:, a + qt * N_CMP:a + (qt + 1) * N_CMP].unsqueeze(1).to_broadcast([P, 8, N_CMP])
            for s in range(2):
                key = ("sc", qt, s)
                half = c.cmp_s[:, qt % 2, :].rearrange("p (j s c) -> p s j c", s=2, c=N_CMP)[:, s]
                tt_op(half, filled(key)[:, 0:256].rearrange("p (j c) -> p j c", j=8), mask, ALU.add).then_inc(release(key), 1)
            read(("sc", qt, 0))
            read(("sc", qt, 1))
            step(v.reduce_max(c.stat[:, b, :], sc, axis=AX))
            step(v.tensor_scalar(c.stat[:, b, :], c.stat[:, b, :], -1e20, None, ALU.max))
            tt_op(sc, sc, c.stat[:, b, :].unsqueeze(2).to_broadcast([P, NSA_H, N_CMP]), ALU.subtract).then_inc(c.cmp_shift, 1)
        if qt:
            q, b = qt - 1, 4 * ((qt - 1) % 2)
            e = c.cmp_e[:, q % 2, :].rearrange("p (h c) -> p h c", h=NSA_H)
            dve.wait_ge(c.cmp_exp, q + 1)
            step(v.reduce_sum(c.stat[:, b + 1, :], e, axis=AX))
            step(v.tensor_scalar(c.stat[:, b + 1, :], c.stat[:, b + 1, :], 1e-30, None, ALU.max))
            step(v.reciprocal(c.stat[:, b + 2, :], c.stat[:, b + 1, :]))
            step(tt_op(c.stat[:, b + 3, :], c.stat[:, b + 2, :], c.gate[:, q, 0:NSA_H], ALU.mult))
            tt_op(e, e, c.stat[:, b + 3, :].unsqueeze(2).to_broadcast([P, NSA_H, N_CMP]), ALU.mult).then_inc(c.cmp_p, 1)
    k1 = {n: c.phase1[:, a:a + w] for n, (a, w) in PHASE1.items()}
    read(("kw", 1))
    for i in range(12):
        key, b = ("rope", i), 2 * (i % 2)
        y = c.q[:, i, :] if i < 8 else (c.ks, c.kw)[(i - 8) // 2][:, i % 2, :]
        tt_op(c.rope_t[:, b, :], y, k1["cos"], ALU.mult)
        tt_op(c.rope_t[:, b + 1, :], filled(key)[:, :], k1["sin"], ALU.mult).then_inc(release(key), 1)
        read(key)
        tt_op(y, c.rope_t[:, b, :], c.rope_t[:, b + 1, :], ALU.add).then_inc(c.rope_ready, 1)
    items = [(j, s, qt) for j in range(8) for s in range(2) for qt in range(NT)]
    for i in range(len(items) + 3):
        if 1 <= i <= len(items):
            j, s, qt = items[i - 1]
            for br in range(2):
                n, g = 2 * (i - 1) + br, NSA_H * (1 + br) + 2 * j + s
                read(("s1", j, s, qt, br))
                step(v.reciprocal(c.nb[:, n % 4, 2:3], c.nb[:, n % 4, 1:2]))
                v.tensor_scalar(c.diag[:, n % 4, :], ident, c.nb[:, n % 4, 2:3], c.gate[:, qt, g:g + 1], ALU.mult, ALU.mult)\
                    .then_inc(c.diag_ready, 1)
        if i < len(items):
            j, s, qt = items[i]
            for br in range(2):
                n, key, end = 2 * i + br, ("s1", j, s, qt, br), (qt + 1) * P
                v.reduce_max(c.nb[:, n % 4, 0:1], filled(key)[:, 0:end], axis=AX, negate=True).then_inc(c.nb_ready, 1)
        if i >= 3 and items[i - 3][1:] == (1, NT - 1):
            j = items[i - 3][0]
            dve.wait_ge(c.attn_hi, j + 1)
            tt_op(c.a_lo[:, j, :], c.psum[bank[("o1", j)][0]][:, :], c.a_hi[:, j, :].bitcast(F32), ALU.subtract)\
                .then_inc(release(("o1", j)), 1)
    for m in range(KT):
        add_to_x(("out", 1, m), m)
    mlp(1)
    norm("final", "final_norm", 0)

    k2 = {n: c.phase2[:, a:a + w] for n, (a, w) in PHASE2.items()}
    for l in range(LAYERS2):
        norm(4 + l, "norm2", l * KT)
        for which, name in enumerate(("cq", "ckv")):
            for i in range(2):
                v.tensor_copy(c.c[:, 2 * which + i, :], product((name, l, i))[:, :]).then_inc(release((name, l, i)), 1)
        r32 = slice(MLA_NOPE, MLA_QK)
        v.tensor_copy(c.kpe[r32, :], product(("kpe", l, 0))[0:MLA_ROPE, :]).then_inc(release(("kpe", l, 0)), 1)
        read(("kpe", l, 0))
        v.tensor_copy(c.k2[r32, :, :], c.kpe[r32, :].unsqueeze(1).to_broadcast([MLA_ROPE, MLA_H, T])).then_inc(c.kpe_ready, 1)
        for i in range(5):
            if i < 4:
                if i % 2 == 0:
                    r = rstd()
                w = pa[("q_latent", "kv_latent")[i // 2]][:, 2 * l + i % 2:2 * l + i % 2 + 1]
                stt(stage(("cn", l, i)), c.c[:, i, :], w, r, ALU.mult, ALU.mult).then_inc(c.split_src, 1)
            if i:
                lo(("cn", l, i - 1), c.cn_hi[:, i - 1, :], c.cn_lo[:, i - 1, :])
        for i in range(4):
            key = ("kn", l, i)
            out = product(key)
            v.tensor_copy(c.k2[0:64, 2 * i, :], out[0:64, :])
            v.tensor_copy(c.k2[0:64, 2 * i + 1, :], out[64:P, :]).then_inc(release(key), 1)
        if l == 0:
            dve.wait_ge(c.phase2_loaded, 16)
        heads = [(which, h) for which in range(2) for h in range(MLA_H)]
        done, sq0 = l * len(heads), count_squares(l)
        for i in range(len(heads) + 1):
            if i < len(heads):
                which, h = heads[i]
                if which:
                    read(("kn", l, h // 2))
                    dve.wait_ge(c.kpe_ready, l + 1)
                else:
                    read(("uq", l, h))
                src = (c.k2 if which else c.q2)[0:MLA_QK, h, :]
                gain = pa[("q_head", "k_head")[which]][0:MLA_QK, l:l + 1]
                v.tensor_scalar(c.head_t[0:MLA_QK, i % 2, :], src, gain, None, ALU.mult).then_inc(c.head_t_ready, 1)
            if i:
                which, h = heads[i - 1]
                y, t = (c.k2 if which else c.q2)[0:MLA_QK, h, :], c.head_t[0:MLA_QK, (i - 1) % 2, :]
                dve.wait_ge(c.sq_ready, sq0 + i)
                dve.wait_ge(c.head_t_ready, done + i)
                step(tt_op(y, t, k2["cos"][0:MLA_QK, :], ALU.mult))
                key = ("rot2", l, which, h)
                tt_op(t, filled(key)[0:MLA_QK, :], k2["sin"][0:MLA_QK, :], ALU.mult).then_inc(release(key), 1)
                read(key)
                step(tt_op(y, y, t, ALU.add))
                stt(y, y, 1.0 if which else MLA_QK ** -0.5, rstd(MLA_QK), ALU.mult, ALU.mult).then_inc(c.head_ready, 1)
        items = [(j, s, qt) for j in range(4) for s in range(2) for qt in range(NT)]
        base = l * len(items)
        dve.wait_ge(c.z_ready, 2 * l + 2)
        for i in range(len(items) + 4):
            if 1 <= i <= len(items):
                n = i - 1
                read(("s2", l, *items[n]))
                step(v.reciprocal(c.nb2[:, n % 2, 2:3], c.nb2[:, n % 2, 1:2]))
                v.tensor_scalar(c.diag2[:, n % 2, :], ident, c.nb2[:, n % 2, 2:3], None, ALU.mult).then_inc(c.diag2_ready, 1)
            if i < len(items):
                v.reduce_max(c.nb2[:, i % 2, 0:1], filled(("s2", l, *items[i]))[:, :], axis=AX, negate=True)\
                    .then_inc(c.nb2_ready, 1)
            if i >= 2 and i - 2 < len(items) and items[i - 2][1:] == (1, NT - 1):
                j = items[i - 2][0]
                dve.wait_ge(c.attn_out, 8 + 4 * l + j + 1)
                tt_op(stage(("oa", l, j)), c.psum[bank[("o2", l, j)][0]][:, :], c.z_a[:, j, :], ALU.mult)\
                    .then_inc(release(("o2", l, j)), 1)
            if i >= 4 and items[i - 4][1:] == (1, NT - 1):
                j = items[i - 4][0]
                lo(("oa", l, j), c.a_hi[:, j, :], c.a_lo[:, j, :])
        n = l * FG * NT
        for g in range(FG):
            for tt in range(NT):
                n += 1
                key = ("dd", l, g, tt)
                dve.wait_ge(c.d_hi_ready, n)
                tt_op(c.d_lo[:, tt, g, :], c.psum[bank[key][0]][:, 0:2 * P], c.d_hi[:, tt, g, :].bitcast(F32), ALU.subtract)\
                    .then_inc(release(key), 1)
        for g in range(FG + 1):
            if g < FG:
                key = ("f", l, g)
                tt_op(stage(("of", l, g)), product(key)[:, :], c.z_f[:, g, :], ALU.mult).then_inc(release(key), 1)
            if g:
                lo(("of", l, g - 1), c.a_hi[:, 3 + g, :], c.a_lo[:, 3 + g, :])
        for m in range(KT + 1):
            if m < KT:
                g = [c.sig[:, 2 * (m % 2) + branch, :] for branch in range(2)]
                for branch, (gate, key) in enumerate(((("ga", l, m, 0), ("ya2", l, m)), (("gf", l, m, 0), ("yf2", l, m)))):
                    out = product(key)
                    read(gate)
                    tt_op(g[branch], out[:, :], g[branch], ALU.mult).then_inc(release(key), 1)
                read(("ya2", l, m))
                read(("yf2", l, m))
                tt_op(stage(("m", l, m)), g[0], g[1], ALU.add).then_inc(c.split_src, 1)
            if m:
                lo(("m", l, m - 1), c.m_hi[:, m - 1, :], c.m_lo[:, m - 1, :])
        for m in range(KT):
            add_to_x(("out2", l, m), m)


def count_squares(l):
    before = 5 * KT + 8 + 4
    return before + (l + 1) * (KT + 4) + l * 2 * MLA_H


def build(nc, in_x, in_weights, in_common, in_phase0, in_phase1, in_phase2, in_params, out):
    from contextlib import ExitStack

    block, bank, split, n_blocks = plan_core()
    assert in_weights.shape[0] == n_blocks, (in_weights.shape, n_blocks)
    ctx = ExitStack()
    with ctx:
        c = Core()
        c.in_common, c.in_phase0, c.in_phase1, c.in_phase2, c.in_params = in_common, in_phase0, in_phase1, in_phase2, in_params
        place(nc, c)
        c.psum = [ctx.enter_context(nc.psum_tensor(f"bank{i}", [P, T], F32)) for i in range(8)]
        add_semaphores(nc, ctx, c)
        blocks = ctx.enter_context(nc.Block())

        @blocks.sync
        def _(sp):
            sp.dma_start(c.x[:, :, :], in_x.rearrange("(k p) t -> p k t", p=P)).then_inc(c.x_loaded, 16)
            for b in range(RING):
                sp.dma_start(c.raw[:, b, :], in_weights[b]).then_inc(c.raw_loaded[b], 16)
            with sp.Fori(1, n_blocks // RING) as turn:
                for slot in range(RING):
                    sp.wait_ge(c.w_lo_ready, (turn - 1) * RING + slot + 1)
                    sp.dma_start(c.raw[:, slot, :], in_weights[turn * RING + slot]).then_inc(c.raw_loaded[slot], 16)
            for b in range(n_blocks // RING * RING, n_blocks):
                sp.wait_ge(c.w_lo_ready, b - RING + 1)
                sp.dma_start(c.raw[:, b % RING, :], in_weights[b]).then_inc(c.raw_loaded[b % RING], 16)
            for m in range(KT):
                bnk, use, _ = bank[("out2", LAYERS2 - 1, m)]
                sp.wait_ge(c.bank_read[bnk], use + 1)
                sp.dma_start(out[m * P:m * P + P, :], c.x[:, m, :]).then_inc(c.out_written, 16)
            sp.wait_ge(c.out_written, 16 * KT)

        @blocks.gpsimd
        def _(pool):
            def low_part(slot):
                return nc.gpsimd.tensor_tensor(c.w_lo[:, slot, :], c.raw[:, slot, :], c.w_hi[:, slot, :].bitcast(F32),
                                               ALU.subtract)

            with pool.Fori(0, n_blocks // RING) as turn:
                for slot in range(RING):
                    pool.wait_ge(c.w_hi_ready, turn * RING + slot + 1)
                    low_part(slot).then_inc(c.w_lo_ready, 1)
            for b in range(n_blocks // RING * RING, n_blocks):
                pool.wait_ge(c.w_hi_ready, b + 1)
                low_part(b % RING).then_inc(c.w_lo_ready, 1)

        @blocks.scalar
        def _(act):
            program_scalar(act, nc, c, block, bank, split, n_blocks)

        @blocks.vector
        def _(dve):
            program_vector(dve, nc, c, block, bank, split)

        @blocks.tensor
        def _(pe):
            program_tensor(pe, nc, c, block, bank, split)


def kernel(**inputs):
    import concourse.bacc as bacc
    from concourse.bass_utils import run_bass_kernel_spmd

    inp = {k: np.asarray(a) for k, a in inputs.items()}
    common, phase0, phase1, phase2 = constant_arrays()
    arrays = {
        "in_x": np.ascontiguousarray(inp["x"][0].T), "in_weights": stream_of(inp), "in_common": common, "in_phase0": phase0,
        "in_phase1": phase1, "in_phase2": phase2, "in_params": parameter_array(inp),
    }
    nc = bacc.Bacc("TRN2", target_bir_lowering=False, num_devices=1)
    args = [nc.dram_tensor(name, a.shape, F32, kind="ExternalInput").ap() for name, a in arrays.items()]
    out = nc.dram_tensor("out", (D, T), F32, kind="ExternalOutput").ap()
    build(nc, *args, out)
    r = run_bass_kernel_spmd(nc, [arrays], core_ids=[0])
    return np.ascontiguousarray(r.results[0]["out"].T)[None]
```

```python
import numpy as np
from concourse import mybir

F32 = mybir.dt.float32
F32R = mybir.dt.float32r
BF16 = mybir.dt.bfloat16
ACT = mybir.ActivationFunctionType
ALU = mybir.AluOpType
AX = mybir.AxisListType.X

P = 128
T = 512
D = 1024
KT = D // P
NT = T // P
FF_PARTS = 4
RING = 3
TILES = 8
GEMM_BANKS = 4
EPS = 1e-6

GDN_H, GDN_D = 8, 64
NSA_H, NSA_D, NSA_G = 16, 64, 4
N_CMP = T // 16
KC_ROW = (T + 16) // 2
MLA_H, MLA_QK, MLA_NOPE, MLA_ROPE = 8, 96, 64, 32
FG = 4
ROPE_SWAP = np.roll(np.arange(MLA_ROPE), MLA_ROPE // 2)
LAYERS2 = 2
NEG = -1e30
NSA_HEADS = [4 * (2 * (j // 4) + s) + j % 4 for j in range(8) for s in range(2)]


def columns(widths):
    at, out = 0, {}
    for name, width in widths:
        out[name] = (at, width)
        at += width
    return out, at


COMMON, COMMON_N = columns([("ident", P), ("ones", P)])
PHASE0, PHASE0_N = columns([("blk64", P), ("triu", P), ("notyet", P), ("levels", 6 * P), ("pair_row", 4 * P)])
PHASE1, PHASE1_N = columns([("causal", P), ("cmp_mask", NT * N_CMP), ("rot", P), ("cos", T), ("sin", T)])
PHASE2, PHASE2_N = columns([("dft_d", 2 * P), ("cos_sin", T)])
PHASE_N = max(PHASE0_N, PHASE1_N, PHASE2_N)
PARAMS, PARAMS_N = columns([
    ("eps", 1), ("mix_norm", 2 * KT), ("mlp_norm", 2 * KT), ("final_norm", KT), ("conv", 12 * 4), ("sc_conv", 4 * 3),
    ("o_norm", 1), ("a_log", 1), ("dt_bias", 1), ("cmp_pos", 16), ("cmp_k_w2", 2 * P), ("cmp_v_w2", 2 * NSA_D),
    ("norm2", LAYERS2 * KT), ("q_latent", LAYERS2 * 2), ("kv_latent", LAYERS2 * 2),
    ("q_head", LAYERS2), ("k_head", LAYERS2), ("merge", LAYERS2 * 2 * KT)])


def rope_rows(theta, rot, base, width):
    f4 = np.float32
    half = rot // 2
    inv = (f4(theta) ** (-np.arange(half, dtype=f4) / f4(half))).astype(f4)
    ang = np.arange(T, dtype=f4)[None, :] * inv[:, None]
    cos, sin, part = np.ones((P, T), f4), np.zeros((P, T), f4), np.zeros((P, P), f4)
    for r0 in range(base, P, width):
        for i in range(half):
            a, b = r0 + i, r0 + half + i
            if b >= P:
                continue
            cos[a] = cos[b] = np.cos(ang[i])
            sin[a] = sin[b] = np.sin(ang[i])
            part[b, a], part[a, b] = -1.0, 1.0
    return cos, sin, part


def constant_arrays():
    f4 = np.float32
    eye, i, j = np.eye(P, dtype=f4), np.arange(P)[None, :], np.arange(P)[:, None]
    common = np.concatenate([eye, np.ones((P, P), f4)], 1)

    levels = []
    for size in (1, 2, 4, 8, 16, 32):
        levels.append((i // (2 * size) == j // (2 * size)) & (i // size % 2 == 1) & (j // size % 2 == 0))
    pair_row = np.zeros((P, 4, P), f4)
    for h in range(GDN_H):
        pair_row[h, h // 2, 64 * (h % 2):64 * (h % 2) + 64] = 1.0
    phase0 = np.concatenate([
        (i // 64 == j // 64).astype(f4), (j <= i).astype(f4), np.where(i >= j, f4(0), f4(NEG)),
        *[m.astype(f4) for m in levels], pair_row.reshape(P, -1)], 1)

    cos, sin, rot = rope_rows(500000.0, NSA_D // 4, 0, NSA_D)
    t = np.arange(T).reshape(NT, P).T[:, :, None]
    c = np.arange(N_CMP)[None, None, :]
    cmp_mask = np.where((c * 16 + 31 <= t) & (c < N_CMP - 1), f4(0), f4(NEG)).reshape(P, -1)
    phase1 = np.concatenate([np.where(i <= j, f4(0), f4(NEG)), cmp_mask, rot, cos, sin], 1)

    cos, sin, _ = rope_rows(10000.0, MLA_ROPE, MLA_NOPE, P)
    half = MLA_ROPE // 2
    cos[MLA_QK:MLA_QK + half], cos[MLA_QK + half:] = -sin[MLA_NOPE:MLA_NOPE + half], sin[MLA_NOPE + half:MLA_QK]
    ang = 2 * np.pi * (np.arange(P)[:, None] * np.arange(P)[None, :] % P) / P
    norm = 1.0 / np.sqrt(T * P)
    phase2 = np.concatenate([np.cos(ang) * norm, -np.sin(ang) * norm, cos], 1)

    out = [common, phase0, phase1, phase2]
    return [np.ascontiguousarray(a.astype(f4)) for a in out]


def stream_of(inp):
    blocks = []

    def pad(w, cols):
        return np.pad(w, ((0, 0), (0, cols - w.shape[1])))

    def add(tiles):
        tiles = list(tiles)
        assert len(tiles) % TILES == 0
        for n in range(0, len(tiles), TILES):
            blocks.append(np.concatenate(tiles[n:n + TILES], 1))

    def out_major(w):
        return [w[k:k + P, m:m + P] for m in range(0, w.shape[1], P) for k in range(0, w.shape[0], P)]

    def in_major(w):
        return [w[k:k + P, m:m + P] for k in range(0, w.shape[0], P) for m in range(0, w.shape[1], P)]

    def mlp(layer):
        up, down = inp["w_up"][layer], inp["w_down"][layer]
        for q in range(FF_PARTS):
            add(out_major(up[:, q * D:(q + 1) * D]))
            add(out_major(down[q * D:(q + 1) * D]))

    w = inp["ev_w_in"][0]
    ab = np.zeros((D, P), w.dtype)
    ab[:, 0:GDN_H], ab[:, 32:32 + GDN_H] = w[:, 2048:2056], w[:, 2056:2064]
    add(out_major(ab))
    add(out_major(w[:, 0:2048]))
    for m in range(4):
        for first in (2064 + 512, 2064 + 1024, 2064):
            add(out_major(w[:, first + m * P:first + (m + 1) * P]))
    w = inp["ev_w_out"][0]
    add(out_major(w[512:]))
    add(out_major(w[:512]))
    mlp(0)

    w = inp["od_w_in"][0]
    order = [d for h in NSA_HEADS for d in range(h * NSA_D, (h + 1) * NSA_D)]
    gate = [3 * h + branch for branch in range(3) for h in NSA_HEADS]
    kc, vc, ks, vs, kw, vw = [w[:, 1024 + 256 * n:1280 + 256 * n] for n in range(6)]
    add(out_major(pad(w[:, 2560:2608][:, gate], P)))
    for part in (kc, vc, w[:, order], inp["od_cmp_k_w1"][0], inp["od_cmp_v_w1"][0], ks, kw):
        add(out_major(part))
    add(in_major(np.concatenate([vs, vw], 1)))
    add(out_major(inp["od_w_out"][0][order]))
    mlp(1)

    ang = 2 * np.pi * (np.arange(T)[:, None] * np.arange(T)[None, :] % T) / T
    dft_t = [np.cos(ang).astype(np.float32), np.sin(ang).astype(np.float32)]
    for l in range(LAYERS2):
        w = inp["w_in_2"][l]
        cq, ckv, kpe, za, uf, zf, ga, gf = np.split(w, np.cumsum([256, 256, 32, 512, 512, 512, 1024]), axis=1)
        kpe = np.concatenate([np.zeros((D, MLA_NOPE), w.dtype), kpe, kpe[:, ROPE_SWAP]], 1)
        for part in (cq, ckv, kpe, uf):
            add(out_major(part))
        uq = inp["w_uq_2"][l].reshape(256, MLA_H, MLA_QK)
        add(out_major(np.concatenate([uq, uq[:, :, MLA_NOPE + ROPE_SWAP]], 2).reshape(256, MLA_H * P)))
        ukv = inp["w_ukv_2"][l].reshape(256, MLA_H, 2, 64)
        add(out_major(ukv[:, :, 0].reshape(256, 512)))
        add(in_major(ukv[:, :, 1].reshape(256, 512)))
        add(out_major(za))
        add(out_major(zf))
        add(b for k in range(NT) for part in dft_t for b in in_major(part[k * P:(k + 1) * P]))
        pa, pf = out_major(inp["w_attn_proj_2"][l]), out_major(inp["w_fourier_proj_2"][l])
        for m in range(KT):
            add(out_major(ga[:, m * P:(m + 1) * P]))
            add(out_major(gf[:, m * P:(m + 1) * P]))
            add(pa[4 * m:4 * m + 4] + pf[4 * m:4 * m + 4])
        add(out_major(inp["w_out_2"][l]))
    return np.ascontiguousarray(np.stack(blocks))


def parameter_array(inp):
    out = np.zeros((P, PARAMS_N), np.float32)

    def put(name, a, n=0):
        at = PARAMS[name][0] + n
        out[:a.shape[0], at:at + a.shape[1]] = a

    def tiles(v):
        return v.reshape(-1, P).T

    out[:, PARAMS["eps"][0]] = EPS
    for l in range(2):
        put("mix_norm", tiles(inp["mix_norm"][l]), l * KT)
        put("mlp_norm", tiles(inp["mlp_norm"][l]), l * KT)
    put("final_norm", tiles(inp["final_norm"]))
    put("conv", inp["ev_qkv_conv"][0].reshape(4, 12, P).transpose(2, 1, 0).reshape(P, 48))
    put("sc_conv", inp["ev_sc_conv"][0].reshape(3, 4, P).transpose(2, 1, 0).reshape(P, 12))
    put("o_norm", np.tile(inp["ev_o_norm"][0], 2)[:, None])
    put("a_log", inp["ev_a_log"][0][:, None])
    put("dt_bias", inp["ev_dt_bias"][0][:, None])
    put("cmp_pos", inp["od_cmp_pos"][0].reshape(16, P).T)
    for k in range(2):
        put("cmp_k_w2", np.tile(inp["od_cmp_k_w2"][0][k * P:(k + 1) * P], (1, 2)), k * P)
        put("cmp_v_w2", inp["od_cmp_v_w2"][0][k * P:(k + 1) * P], k * NSA_D)
    for l in range(LAYERS2):
        put("norm2", tiles(inp["norm_g_2"][l]), l * KT)
        put("q_latent", tiles(inp["q_latent_g_2"][l]), l * 2)
        put("kv_latent", tiles(inp["kv_latent_g_2"][l]), l * 2)
        for name in ("q_head", "k_head"):
            gain = inp[name + "_g_2"][l]
            put(name, np.concatenate([gain, gain[MLA_NOPE + ROPE_SWAP]])[:, None], l)
        for branch in range(2):
            put("merge", tiles(inp["b_merge_2"][l, branch]), (l * 2 + branch) * KT)
    return out


L2_ORDER = [4, 5, 6, 7, 0, 1, 2, 3]
BESIDE = {2: [("gT",)], 3: [("gc",)], 4: [("gl",)], 5: [("gcr",)], **{6 + p: [("bb", p)] for p in range(4)}, 10: []}
for n, i in enumerate(L2_ORDER):
    BESIDE[3 + n] = BESIDE[3 + n] + [("l2", i)]
BESIDE_V = [[("pcT", n) for n in range(NT) if k == (0, 1, 3, 5)[n]] + [("rope", k)] for k in range(KT)]
ROPE_KEYS = {0: (8, 9), 2: (10, 11)}
SCAN_OUT = [(0,), (1,), (2, 3), (), (4, 5), (6, 7)]
DECAYED = ("gcb", "qk", "kk")
NORMS = [0, 1, 2, 3, "final", 4, 5]


def plan_core():
    block, bank, split = {}, {}, {}
    uses, fills, turn, at = [0] * 8, [0] * 8, [0, 0], 0

    def use(key, pool):
        b = pool * GEMM_BANKS + turn[pool] % 4
        turn[pool] += 1
        take(key, b, key[0] in DECAYED + ("kt", "vt") or pool == 1 and key[0] not in ("l2", "on", "lat", "hs2"))

    def take(key, b, announced=True):
        bank[key] = (b, uses[b], fills[b])
        uses[b] += 1
        fills[b] += announced

    def gemm(keys, blocks):
        nonlocal at
        for key in keys:
            block[key] = (at, at + blocks - 1)
            use(key, 0)
        at += blocks

    def scratch(*key):
        use(key, 1)

    def splits(*keys):
        for key in keys:
            split[key] = len(split)

    def norm(n):
        scratch("ssq", n)
        if n != "final":
            splits(*[("h", n, k) for k in range(KT)])

    def each(name, *rest, n):
        for m in range(n):
            gemm([(name, *rest, m)], 1)

    def mlp(layer):
        norm(2 * layer + 1)
        for q in range(FF_PARTS):
            each("up", layer, q, n=KT)
            splits(*[("a", layer, q, m) for m in range(KT)])
            each("down", layer, q, n=KT)

    norm(0)
    gemm([("ab",)], 1)
    each("qkv", n=12)
    each("z", n=4)
    for i in range(4):
        for name in ("cg", "hs", "bg"):
            gemm([(name, i)], 1)
        splits(("yb", i))
    for t in range(12):
        for key in BESIDE.get(t, ()):
            scratch(*key)
    for name in DECAYED:
        for s in range(2):
            use((name, s), 0)
    for p in range(4):
        for level in range(7):
            for name in (("y", "dx") if level else ("xt",)):
                for s in range(2):
                    scratch(name, 2 * p + s, level)
            if p == 0 and 1 <= level <= NT:
                use(("kt", level - 1), 0)
                use(("vt", level - 1), 0)
            if p < 3 and 1 <= level <= 2:
                use(("gcb", 2 * p + 2 + level - 1), 0)
            if p < 3 and 3 <= level <= 4:
                for s in range(2):
                    use((DECAYED[level - 2], 2 * p + 2 + s), 0)
        for s in range(2):
            scratch("u", 2 * p + s)
            scratch("w", 2 * p + s)
    for p in range(4):
        scratch("eg", p)
    for c in range(NT):
        if c:
            scratch("ws", c, 0)
            scratch("ws", c, 1)
        scratch("o", c)
        scratch("ds", c)
    for m in range(0, KT, 2):
        gemm([("outb", m), ("outb", m + 1)], 1)
    for p in range(4):
        scratch("on", p)
    splits(*[("ya", p) for p in range(4)])
    for m in range(0, KT, 2):
        gemm([("out", 0, m), ("out", 0, m + 1)], 1)
    mlp(0)

    norm(2)
    gemm([("gl_gates",)], 1)
    each("kc", n=2)
    each("vc", n=2)
    splits(*[("kc", kv, i) for kv in range(2) for i in range(2)])
    each("q", n=8)
    for kv in range(2):
        for m in range(2):
            gemm([("cmp1", kv, m)], 2)
    scratch("rcol")
    scratch("gateT")
    each("ks", n=2)
    scratch("kcb")
    scratch("vcb")
    each("kw", n=2)
    gemm([("v", tt) for tt in range(NT)], 4)
    for qt in range(NT):
        scratch("sc", qt)
        for i in ROPE_KEYS.get(qt, ()):
            scratch("rope", i)
    for keys in BESIDE_V:
        for key in keys:
            scratch(*key)
    for j in range(8):
        use(("o1", j), 0)
        for s in range(2):
            for qt in range(NT):
                for br in range(2):
                    take(("s1", j, s, qt, br), 4 + br)
                    take(("t1", j, s, qt, br), 6 + br)
    each("out", 1, n=KT)
    mlp(1)
    norm("final")

    for l in range(LAYERS2):
        norm(4 + l)
        each("cq", l, n=2)
        each("ckv", l, n=2)
        each("kpe", l, n=1)
        each("uf", l, n=4)
        for which in range(2):
            scratch("lat", l, which)
        splits(*[("cn", l, i) for i in range(4)])
        for i in range(2):
            gemm([("uq", l, 4 * i + n) for n in range(4)], 1)
        gemm([("kn", l, i) for i in range(4)], 1)
        gemm([("v2", l, tt) for tt in range(NT)], 1)
        for which in range(2):
            for h in range(MLA_H):
                scratch("hs2", l, which, h)
        each("za", l, n=4)
        each("zf", l, n=4)
        for j in range(4):
            use(("o2", l, j), 0)
            for s in range(2):
                for qt in range(NT):
                    i = (2 * j + s) * NT + qt
                    take(("s2", l, j, s, qt), 4 + i % 2)
                    take(("t2", l, j, s, qt), 6 + i % 2)
            splits(("oa", l, j))
        for g in range(FG):
            for tt in range(NT):
                scratch("dd", l, g, tt)
        gemm([("f", l, g) for g in range(FG)], 4)
        splits(*[("of", l, g) for g in range(FG)])
        for m in range(KT):
            each("ga", l, m, n=1)
            each("gf", l, m, n=1)
            gemm([("ya2", l, m), ("yf2", l, m)], 1)
            splits(("m", l, m))
        each("out2", l, n=KT)
    return block, bank, split, at


def halves(a, level, odd):
    return a.rearrange("p (g two e) -> p two g e", two=2, e=2 ** level)[:, odd]


def grouped(a, level):
    return a.rearrange("p (g e) -> p g e", e=2 ** level)


class Core:
    pass


def place(nc, c):
    at = (nc.sbuf_base + 63) // 64 * 64
    top = nc.sbuf_usable_end

    def put(name, shape, offset, dtype=F32):
        size = (4 * int(np.prod(shape[1:])) + 31) // 32 * 32
        assert offset + size <= top, (name, offset + size - top)
        return nc.alloc_sbuf_tensor_at(name, shape, dtype, offset=offset), offset + size

    c.x, at = put("x", [P, KT, T], at)
    c.raw, at = put("raw", [P, RING, TILES * P], at)
    c.w_hi, at = put("w_hi", [P, RING, TILES * P], at, F32R)
    c.w_lo, at = put("w_lo", [P, RING, TILES * P], at, F32R)
    c.Y, _ = put("Y", [P, 2, T], at)
    c.stage, at = put("stage", [P, 3, T], at)
    c.common, at = put("common", [P, COMMON_N], at)
    c.params, at = put("params", [P, PARAMS_N], at)
    c.tiny, at = put("tiny", [P, 64], at)
    c.norm, at = put("norm", [P, 2, T], at)
    c.rstd, at = put("rstd", [P, 2, T], at)
    c.XT, _ = put("XT", [P, 2, T], at)
    c.sq, at = put("sq", [P, 2, T], at)
    at = (at + 63) // 64 * 64
    phase = at
    at += 4 * PHASE_N
    at = (at + 63) // 64 * 64
    c.phase0, _ = put("phase0", [P, PHASE0_N], phase)
    c.phase1, _ = put("phase1", [P, PHASE1_N], phase)
    c.phase2, _ = put("phase2", [P, PHASE2_N], phase)
    tail = (top - 2 * 32768) // 64 * 64
    h, a, local = tail, tail + 32768, at
    c.h_hi, _ = put("h_hi", [P, KT, T], h, F32R)
    c.h_lo, _ = put("h_lo", [P, KT, T], h + 16384, F32R)
    c.a_hi, _ = put("a_hi", [P, KT, T], a, F32R)
    c.a_lo, _ = put("a_lo", [P, KT, T], a + 16384, F32R)
    room = tail - local
    assert room > 0

    c.relu, _ = put("relu", [P, 2, T], local)

    c.qkv, o = put("qkv", [P, 12, T], local)
    c.u, _ = put("u", [P, NT, T], local + 8 * 2048)
    c.z, o = put("z", [P, 4, T], o)
    c.egc, _ = put("egc", [P, 4, T], o)
    c.kb, o = put("kb", [P, 4, T], o)
    c.sc, _ = put("sc", [P, 3, T], o)
    c.wT, o = put("wT", [P, 4, T], o)
    c.X, _ = put("X", [P, 2, T], o)
    c.g_row, o = put("g_row", [P, T], o)
    c.e_row, o = put("e_row", [P, T], o)
    c.beta_row, o = put("beta_row", [P, T], o)
    c.gc_row, o = put("gc_row", [P, T], o)
    c.tok, o = put("tok", [P, 8, 32], o)
    c.S, o = put("S", [P, 4, GDN_D], o)
    MT_0, o = put("MT_0", [P, 2, T], o)
    c.notyet16, o = put("notyet16", [P, P], o, BF16)
    c.eye16, o = put("eye16", [P, P], o, BF16)
    assert o <= tail, o - tail
    c.kd, o = put("kd", [P, NT, T], h)
    c.gdn_o, _ = put("gdn_o", [P, 4, T], o)
    c.kbe, o = put("kbe", [P, NT, T], o)
    c.vb, o = put("vb", [P, NT, T], o)
    c.vnew, _ = put("vnew", [P, T], o)
    MT_1, o = put("MT_1", [P, 2, T], o)
    c.MT = [MT_0, MT_1]
    c.ML, o = put("ML", [P, 2, T], o)
    assert o == a
    c.AT0, _ = put("AT0", [P, 4, T], a)
    c.AT1, _ = put("AT1", [P, 4, T], a + 16384)

    c.q, o = put("q", [P, 8, T], local)
    c.ks, o = put("ks", [P, 2, T], o)
    c.kw, o = put("kw", [P, 2, T], o)
    c.v, o = put("v", [P, NT, T], o)
    c.gate_row, o = put("gate_row", [P, T], o)
    c.gate, o = put("gate", [P, NT, 48], o)
    c.kcb, o = put("kcb", [P, 2, 2, N_CMP], o)
    c.vcb, o = put("vcb", [P, 4, NSA_D], o)
    c.stat, o = put("stat", [P, 16, 16], o)
    o1 = o
    c.kc_hi, o = put("kc_hi", [P, 2, 5, KC_ROW], o1, F32R)
    c.kc_lo, o = put("kc_lo", [P, 2, 5, KC_ROW], o, F32R)
    assert o <= tail, o - tail
    c.pcT, o = put("pcT", [P, 4, T], o1)
    c.nb, o = put("nb", [P, 4, 4], o)
    c.ident16, o = put("ident16", [P, P], o, BF16)
    c.causal16, o = put("causal16", [P, P], o, BF16)
    assert o <= tail
    c.hid_k, o = put("hid_k", [P, 2, P], a)
    c.hid_v, o = put("hid_v", [P, 2, 4 * P], o)
    c.cmp_s, o = put("cmp_s", [P, NT, T], o)
    c.cmp_e, o = put("cmp_e", [P, NT, T], o)
    c.rope_t, o = put("rope_t", [P, 4, T], o)
    c.prob, o = put("prob", [P, 4, T], h)
    c.probT, o = put("probT", [P, 4, T], o)

    c.c, o = put("c", [P, 4, T], local)
    c.v2, _ = put("v2", [P, NT, T], local)
    c.z_a, _ = put("z_a", [P, 4, T], o)
    c.z_f, _ = put("z_f", [P, 4, T], o + 8192)
    c.cn_hi, o = put("cn_hi", [P, 4, T], o, F32R)
    c.cn_lo, o = put("cn_lo", [P, 4, T], o, F32R)
    c.d_hi, _ = put("d_hi", [P, NT, FG, 2 * P], o, F32R)
    c.d_lo, _ = put("d_lo", [P, NT, FG, 2 * P], o + 16384, F32R)
    c.m_hi, _ = put("m_hi", [P, KT, T], o, F32R)
    c.m_lo, _ = put("m_lo", [P, KT, T], o + 16384, F32R)
    c.q2, o = put("q2", [P, MLA_H, T], o)
    c.k2, o = put("k2", [P, MLA_H, T], o)
    c.head_t, _ = put("head_t", [P, 2, T], o)
    c.prob2, o = put("prob2", [P, 3, T], o)
    c.nb2, o = put("nb2", [P, 2, 4], o)
    c.sig, _ = put("sig", [P, 4, T], local)
    c.probT2, _ = put("probT2", [P, 2, T], a + 8192)
    c.kpe, _ = put("kpe", [P, T], a + 8192 + 4096)
    c.head_r = [put(f"head_r{i}", [P, 4, T], a + 16384 * i)[0] for i in range(2)]
    assert o <= tail, o - tail
    c.u_f, _ = put("u_f", [P, 4, T], a + 16384 + 8192)


def add_semaphores(nc, ctx, c):
    def sem(name):
        return ctx.enter_context(nc.semaphore(name))

    c.raw_loaded = [sem(f"raw_loaded_{i}") for i in range(RING)]
    c.bank_filled = [sem(f"bank_filled_{i}") for i in range(8)]
    c.bank_read = [sem(f"bank_read_{i}") for i in range(8)]
    c.x_loaded = [sem(f"x_loaded_{i}") for i in range(4)]
    c.common_loaded = sem("common_loaded")
    c.params_loaded = sem("params_loaded")
    c.phase0_loaded = sem("phase0_loaded")
    c.phase1_loaded = sem("phase1_loaded")
    c.phase2_loaded = sem("phase2_loaded")
    c.out_written = sem("out_written")
    c.w_hi_ready = sem("w_hi_ready")
    c.w_lo_ready = sem("w_lo_ready")
    c.block_used = sem("block_used")
    c.split_src = sem("split_src")
    c.split_hi = sem("split_hi")
    c.split_lo = sem("split_lo")
    c.vector_step = sem("vector_step")
    c.scalar_step = sem("scalar_step")
    c.sq_ready = sem("sq_ready")
    c.sq_used = sem("sq_used")
    c.norm_sq = sem("norm_sq")
    c.norm_sum = sem("norm_sum")
    c.norm_ready = sem("norm_ready")
    c.rstd_ready = sem("rstd_ready")
    c.final_ready = sem("final_ready")
    c.conv_ready = sem("conv_ready")
    c.silu_done = sem("silu_done")
    c.gate_ready = sem("gate_ready")
    c.sig_ready = sem("sig_ready")
    c.g_x_ready = sem("g_x_ready")
    c.g_e_ready = sem("g_e_ready")
    c.g_ln_ready = sem("g_ln_ready")
    c.a_exp_ready = sem("a_exp_ready")
    c.g_ready = sem("g_ready")
    c.ekd_in = sem("ekd_in")
    c.egt_ready = sem("egt_ready")
    c.l2_ready = sem("l2_ready")
    c.qe_ready = sem("qe_ready")
    c.vnew_ready = sem("vnew_ready")
    c.ml_ready = sem("ml_ready")
    c.xt_ready = sem("xt_ready")
    c.kc_pad = sem("kc_pad")
    c.kc_hi_ready = sem("kc_hi_ready")
    c.hid_bias = sem("hid_bias")
    c.kcb_clear = sem("kcb_clear")
    c.cmp_shift = sem("cmp_shift")
    c.cmp_exp = sem("cmp_exp")
    c.cmp_p = sem("cmp_p")
    c.rope_ready = sem("rope_ready")
    c.nb_ready = sem("nb_ready")
    c.prob_ready = sem("prob_ready")
    c.attn_out = sem("attn_out")
    c.attn_hi = sem("attn_hi")
    c.kpe_ready = sem("kpe_ready")
    c.head_r_ready = sem("head_r_ready")
    c.head_ready = sem("head_ready")
    c.z_ready = sem("z_ready")
    c.nb2_ready = sem("nb2_ready")
    c.prob2_ready = sem("prob2_ready")
    c.notyet16_ready = sem("notyet16_ready")
    c.masks16_ready = sem("masks16_ready")
    c.d_hi_ready = sem("d_hi_ready")


def program_tensor(pe, nc, c, block, bank, split):
    mm = nc.tensor.matmul
    ident, ones = c.common[:, 0:P], c.common[:, P:2 * P]
    sums = [0]

    def claim(key):
        b, n, _ = bank[key]
        if n:
            pe.wait_ge(c.bank_read[b], n)
        return c.psum[b]

    def fill(key):
        return c.bank_filled[bank[key][0]]

    def read(key):
        b, n, _ = bank[key]
        pe.wait_ge(c.bank_read[b], n + 1)

    def three(out, w_hi, w_lo, x_hi, x_lo, first, last):
        mm(out, w_hi, x_lo, start=first, stop=False)
        mm(out, w_lo, x_hi, start=False, stop=False)
        return mm(out, w_hi, x_hi, start=False, stop=last)

    def gemm(key, x_hi, x_lo, tile0=0, needs=None, cols=T, view=None):
        out = claim(key)[:, 0:cols]
        if view:
            out = view(out)
        for k in range(len(x_hi)):
            b, t = block[key][0] + (tile0 + k) // TILES, (tile0 + k) % TILES
            if k == 0 or t == 0:
                pe.wait_ge(c.w_lo_ready, b + 1)
            if needs:
                needs(k)
            w = slice(t * P, t * P + P)
            ins = three(out, c.w_hi[:, b % RING, w], c.w_lo[:, b % RING, w], x_hi[k], x_lo[k],
                        k == 0, k == len(x_hi) - 1)
            if t == TILES - 1:
                ins.then_inc(c.block_used, 1)

    def token_major(keys, x_hi, x_lo, n_in, needs=None, beside=None):
        outs = [claim(key) for key in keys]
        first, last = block[keys[0]]
        for k in range(n_in):
            b, half = first + k // 2, k % 2
            if half == 0:
                pe.wait_ge(c.w_lo_ready, b + 1)
            if needs:
                needs(k)
            w = slice(half * T, half * T + T)
            for tt in range(NT):
                t = slice(tt * P, tt * P + P)
                ins = three(outs[tt][:, :], x_hi[:, k, t], x_lo[:, k, t], c.w_hi[:, b % RING, w], c.w_lo[:, b % RING, w],
                            k == 0, k == n_in - 1)
            if half:
                ins.then_inc(c.block_used, 1)
            if beside:
                beside(k)

    def sum_squares(key, over, n=1, rows=P):
        out = claim(key)
        for k in range(n):
            i = sums[0]
            pe.wait_ge(c.sq_ready, i + 1)
            mm(out[0:rows, :], over, c.sq[0:rows, i % 2, :], start=k == 0, stop=k == n - 1).then_inc(c.sq_used, 1)
            sums[0] += 1

    def norm_sum(n):
        i = NORMS.index(n)
        out = claim(("ssq", n))
        pe.wait_ge(c.norm_sum, (i + 1) * (KT - 1))
        mm(out[:, :], ones, c.norm[:, i % 2, :], start=True, stop=True).then_inc(fill(("ssq", n)), 1)

    def tiles(t, n=KT, first=0):
        return [t[:, first + k, :] for k in range(n)]

    def parted(*key, first=0):
        return lambda k: pe.wait_ge(c.split_lo, split[(*key, first + k)] + 1)

    h_hi, h_lo = tiles(c.h_hi), tiles(c.h_lo)
    a_hi, a_lo = tiles(c.a_hi), tiles(c.a_lo)

    def mlp(layer):
        n = 2 * layer + 1
        for q in range(FF_PARTS):
            for m in range(KT):
                gemm(("up", layer, q, m), h_hi, h_lo, needs=parted("h", n) if q == m == 0 else None)
                if q == m == 0:
                    norm_sum(n)
            for m in range(KT):
                gemm(("down", layer, q, m), a_hi, a_lo, needs=parted("a", layer, q) if m == 0 else None)

    gemm(("ab",), h_hi, h_lo, needs=parted("h", 0))
    pe.wait_ge(c.common_loaded, 16)
    norm_sum(0)
    for i in range(12):
        gemm(("qkv", i), h_hi, h_lo)
    for i in range(4):
        gemm(("z", i), h_hi, h_lo)
    k0 = {n: c.phase0[:, a:a + w] for n, (a, w) in PHASE0.items()}
    pe.wait_ge(c.phase0_loaded, 16)
    for t in range(12):
        gemm((("cg", "hs", "bg")[t % 3], t // 3), h_hi, h_lo)
        for key in BESIDE.get(t, ()):
            if key[0] == "l2":
                sum_squares(key, k0["blk64"])
                continue
            out = claim(key)
            if key[0] == "gT":
                pe.wait_ge(c.g_ready, 1)
                for n, row in enumerate((c.g_row, c.beta_row)):
                    for ch in range(NT):
                        ins = nc.tensor.transpose(out[:, 32 * n + 8 * ch:32 * n + 8 * ch + 8], row[0:8, ch * P:ch * P + P],
                                                  ident[0:8, 0:8])
            elif key[0] == "gc":
                read(("gT",))
                ins = mm(out[:, 0:32], k0["triu"], c.tok[:, 0, :], start=True, stop=True)
            elif key[0] == "gl":
                read(("gc",))
                ins = mm(out[:, 0:32], ident[:, P - 1:P].to_broadcast([P, P]), c.tok[:, 2, :], start=True, stop=True)
            elif key[0] == "gcr":
                for ch in range(NT):
                    ins = nc.tensor.transpose(out[0:8, ch * P:ch * P + P], c.tok[:, 2, 8 * ch:8 * ch + 8], ident)
            else:
                p = key[1]
                ins = mm(out[:, :], k0["pair_row"][0:8, p * P:p * P + P], c.beta_row[0:8, :], start=True, stop=True)
            ins.then_inc(fill(key), 1)
    pe.wait_ge(c.l2_ready, 8)
    pe.wait_ge(c.silu_done, 12)
    read(("gcr",))
    for p in range(4):
        read(("bb", p))
    pe.wait_ge(c.notyet16_ready, 1)
    chunks = [slice(ch * P, ch * P + P) for ch in range(NT)]

    def decayed(p, name, heads=(0, 1)):
        for s in heads:
            h, r = 2 * p + s, slice(64 * s, 64 * s + 64)
            out = claim((name, h))
            if name == "gcb":
                mm(out[:, :], ident[0:8, h:h + 1].to_broadcast([8, P]), c.gc_row[0:8, :], start=True, stop=False)
                ins = mm(out[:, :].rearrange("p (n i) -> p n i", n=NT), c.eye16[:, :],
                         c.notyet16[:, :].unsqueeze(1).to_broadcast([P, NT, P]), start=False, stop=True)
            else:
                for t in chunks:
                    right = c.kb[r, p, t] if name == "kk" else c.qkv[r, p, t]
                    ins = mm(out[:, t], c.qkv[r, 4 + p, t], right, start=True, stop=True)
            ins.then_inc(fill((name, h)), 1)

    for name in DECAYED:
        decayed(0, name)
    for p in range(4):
        for s in range(2):
            h = 2 * p + s
            out = claim(("xt", h, 0))
            pe.wait_ge(c.xt_ready, h + 1)
            for t in chunks:
                ins = nc.tensor.transpose(out[:, t], c.XT[:, s, t], ident)
            ins.then_inc(fill(("xt", h, 0)), 1)
        for level in range(1, 6):
            for s in range(2):
                h, n = 2 * p + s, (5 * p + level - 1) * 2 + s
                out = claim(("y", h, level))
                pe.wait_ge(c.ml_ready, n + 1)
                read(("dx", h, level - 1) if level > 1 else ("xt", h, 0))
                for t in chunks:
                    ins = mm(out[:, t], c.ML[:, s, t], c.X[:, s, t], start=True, stop=True)
                ins.then_inc(fill(("y", h, level)), 1)
            if p == 0 and level <= NT:
                ch = level - 1
                for name, first in (("kt", 4), ("vt", 8)):
                    out = claim((name, ch))
                    for n in range(4):
                        ins = nc.tensor.transpose(out[:, n * P:n * P + P], c.qkv[:, first + n, ch * P:ch * P + P], ident)
                    ins.then_inc(fill((name, ch)), 1)
            if p < 3:
                if level <= 2:
                    decayed(p + 1, "gcb", (level - 1,))
                elif level <= 4:
                    decayed(p + 1, DECAYED[level - 2])
            for s in range(2):
                h = 2 * p + s
                out = claim(("dx", h, level))
                read(("y", h, level))
                for ch, t in enumerate(chunks):
                    u = slice(ch * 64, ch * 64 + 64)
                    mm(grouped(out[:, u], level), c.XT[:, s, t], halves(c.Y[:, s, t], level, 0), start=True, stop=True)
                    v = slice(256 + ch * 64, 256 + ch * 64 + 64)
                    ins = mm(grouped(out[:, v], level), c.Y[:, s, t], halves(c.XT[:, s, t], level, 1), start=True, stop=True)
                ins.then_inc(fill(("dx", h, level)), 1)
        low, high = slice(0, 64), slice(64, P)
        for s in range(2):
            out = claim(("y", 2 * p + s, 6))
            read(("dx", 2 * p + s, 5))
            for ch in range(NT):
                ins = mm(out[high, ch * 64:ch * 64 + 64], c.MT[p % 2][low, s, ch * P + 64:ch * P + P], c.X[low, s, ch * P:ch * P + 64],
                         start=True, stop=True)
            ins.then_inc(fill(("y", 2 * p + s, 6)), 1)
        for s in range(2):
            out = claim(("dx", 2 * p + s, 6))
            read(("y", 2 * p + s, 6))
            for ch in range(NT):
                ins = mm(out[low, ch * 64:ch * 64 + 64], c.Y[high, s, ch * 64:ch * 64 + 64], c.XT[high, s, ch * P + 64:ch * P + P],
                         start=True, stop=True)
            ins.then_inc(fill(("dx", 2 * p + s, 6)), 1)
        for s in range(2):
            h = 2 * p + s
            out = claim(("u", h))
            read(("dx", h, 6))
            if p == s == 0:
                read(("kt", NT - 1))
                read(("vt", NT - 1))
            for ch, t in enumerate(chunks):
                ins = mm(out[:, ch * 64:ch * 64 + 64], c.XT[:, s, t], c.vb[:, ch, h * 64:h * 64 + 64], start=True, stop=True)
            ins.then_inc(fill(("u", h)), 1)
            out = claim(("w", h))
            for ch, t in enumerate(chunks):
                ins = mm(out[64 * s:64 * s + 64, t], c.kbe[:, ch, h * 64:h * 64 + 64], c.XT[:, s, t], start=True, stop=True)
            ins.then_inc(fill(("w", h)), 1)
    for p in range(4):
        out = claim(("eg", p))
        mm(out[:, :], k0["pair_row"][0:8, p * P:p * P + P], c.gc_row[0:8, :], start=True, stop=True)\
            .then_inc(fill(("eg", p)), 1)

    def short_half(tiles_out):
        for m in tiles_out:
            gemm(("outb", m), a_hi[4:8], a_lo[4:8], tile0=4 * (m % 2), needs=parted("yb") if m == 0 else None)

    for h in range(GDN_H):
        read(("w", h))
    pe.wait_ge(c.qe_ready, 4)
    for ch, t in enumerate(chunks):
        if ch:
            read(("ds", ch - 1))
            for s in range(2):
                out, r = claim(("ws", ch, s)), slice(64 * s, 64 * s + 64)
                for p in range(4):
                    ins = mm(out[:, p * 64:p * 64 + 64], c.wT[r, p, t], c.S[r, p, :], start=True, stop=True)
                ins.then_inc(fill(("ws", ch, s)), 1)
        out = claim(("o", ch))
        if ch:
            read(("ws", ch, 1))
        else:
            pe.wait_ge(c.vnew_ready, 1)
        for h in range(GDN_H):
            r, p = slice(64 * (h % 2), 64 * (h % 2) + 64), h // 2
            o = out[r, p * P:p * P + P]
            if ch:
                mm(o, c.S[r, p, :], c.qkv[r, p, t], start=True, stop=False)
            ins = mm(o, c.vnew[:, h * 64:h * 64 + 64], (c.AT0, c.AT1)[h // 4][:, h % 4, t], start=ch == 0, stop=True)
        ins.then_inc(fill(("o", ch)), 1)
        out = claim(("ds", ch))
        for h in range(GDN_H):
            r, p = slice(64 * (h % 2), 64 * (h % 2) + 64), h // 2
            ins = mm(out[r, p * 64:p * 64 + 64], c.kd[:, ch, h * 64:h * 64 + 64], c.vnew[:, h * 64:h * 64 + 64],
                     start=True, stop=True)
        ins.then_inc(fill(("ds", ch)), 1)
        short_half(SCAN_OUT[ch])
    for p in range(4):
        sum_squares(("on", p), k0["blk64"])
        if p % 2:
            short_half(SCAN_OUT[NT + p // 2])
    for m in range(KT):
        gemm(("out", 0, m), a_hi[0:4], a_lo[0:4], tile0=4 * (m % 2), needs=parted("ya") if m == 0 else None)
    mlp(0)

    gemm(("gl_gates",), h_hi, h_lo, needs=parted("h", 2))
    norm_sum(2)
    for name, n in (("kc", 2), ("vc", 2), ("q", 8)):
        for i in range(n):
            gemm((name, i), h_hi, h_lo)
    for kv in range(2):
        parted("kc", kv)(1)
        for m in range(2):
            rows = [[t[:, kv, :, pp:pp + 8 * (N_CMP - 1) + 1:8] for pp in range(16)] for t in (c.kc_hi, c.kc_lo)]
            gemm(("cmp1", kv, m), rows[0], rows[1], cols=5 * N_CMP,
                 view=lambda o: o.rearrange("p (g c) -> p g c", g=5))
    out = claim(("rcol",))
    pe.wait_ge(c.norm_ready, NORMS.index(2) + 1)
    for tt in range(NT):
        ins = mm(out[:, tt:tt + 1], c.norm[0:1, NORMS.index(2) % 2, tt * P:tt * P + P], ones[0:1, 0:1], start=True, stop=True)
    ins.then_inc(fill(("rcol",)), 1)
    out = claim(("gateT",))
    pe.wait_ge(c.gate_ready, 1)
    for tt in range(NT):
        ins = nc.tensor.transpose(out[:, 48 * tt:48 * tt + 48], c.gate_row[0:48, tt * P:tt * P + P], ident[0:48, 0:48])
    ins.then_inc(fill(("gateT",)), 1)
    gemm(("ks", 0), h_hi, h_lo)
    pa = {n: c.params[:, a:a + w] for n, (a, w) in PARAMS.items()}
    out = claim(("kcb",))
    read(("cmp1", 0, 0))
    read(("cmp1", 0, 1))
    for k in range(2):
        ins = mm(out[:, 0:P], pa["cmp_k_w2"][:, k * P:k * P + P], c.hid_k[:, k, :], start=k == 0, stop=k == 1)
    ins.then_inc(fill(("kcb",)), 1)
    gemm(("ks", 1), h_hi, h_lo)
    out = claim(("vcb",))
    read(("cmp1", 1, 0))
    read(("cmp1", 1, 1))
    for g in range(NSA_G):
        for k in range(2):
            ins = mm(out[:, g * 64:g * 64 + 64], c.hid_v[:, k, g * P:g * P + P], pa["cmp_v_w2"][:, k * 64:k * 64 + 64],
                     start=k == 0, stop=k == 1)
    ins.then_inc(fill(("vcb",)), 1)

    def block_scores(qt):
        out = claim(("sc", qt))
        for j in range(8):
            ins = mm(out[:, j * 64:j * 64 + 64], c.q[:, j, qt * P:qt * P + P], c.kcb[:, j // 4, :, :].rearrange("p s c -> p (s c)"),
                     start=True, stop=True)
        ins.then_inc(fill(("sc", qt)), 1)

    k1 = {n: c.phase1[:, a:a + w] for n, (a, w) in PHASE1.items()}
    pe.wait_ge(c.phase1_loaded, 16)

    def partners(i):
        out, src = claim(("rope", i)), c.q[:, i, :] if i < 8 else (c.ks, c.kw)[(i - 8) // 2][:, i % 2, :]
        if i >= 8:
            read((("ks", "kw")[(i - 8) // 2], i % 2))
        mm(out[:, :], k1["rot"], src, start=True, stop=True).then_inc(fill(("rope", i)), 1)

    read(("kcb",))
    read(("q", 7))
    for qt in range(NT):
        block_scores(qt)
        for i in ROPE_KEYS.get(qt, ()):
            partners(i)
        if qt < 2:
            gemm(("kw", qt), h_hi, h_lo)

    def beside_values(k):
        for name, i in BESIDE_V[k]:
            if name == "rope":
                partners(i)
                continue
            out = claim(("pcT", i))
            pe.wait_ge(c.cmp_p, i + 1)
            for n in range(4):
                ins = nc.tensor.transpose(out[:, n * P:n * P + P], c.cmp_e[:, i, n * P:n * P + P], ident)
            ins.then_inc(fill(("pcT", i)), 1)

    token_major([("v", tt) for tt in range(NT)], c.h_hi, c.h_lo, KT, beside=beside_values)
    pe.wait_ge(c.rope_ready, 12)
    pe.wait_ge(c.masks16_ready, 1)
    read(("vcb",))
    for qt in range(NT):
        read(("v", qt))
        read(("pcT", qt))
    items = [(j, s, qt) for j in range(8) for s in range(2) for qt in range(NT)]
    for i in range(len(items) + 2):
        if i < len(items):
            j, s, qt = items[i]
            r, end = slice(64 * s, 64 * s + 64), (qt + 1) * P
            for br, keys in enumerate((c.ks, c.kw)):
                key = ("s1", j, s, qt, br)
                out = claim(key)
                mm(out[:, 0:end], c.q[r, j, qt * P:end], keys[r, j // 4, 0:end], start=True, stop=False)
                mm(out[:, qt * P:end], c.ident16[:, :], c.causal16[:, :], start=False, stop=True).then_inc(fill(key), 1)
        if 1 <= i <= len(items):
            j, s, qt = items[i - 1]
            for br in range(2):
                key, n = ("t1", j, s, qt, br), 2 * (i - 1) + br
                out = claim(key)
                pe.wait_ge(c.prob_ready, n + 1)
                for kt in range(qt + 1):
                    ins = nc.tensor.transpose(out[:, kt * P:kt * P + P], c.prob[:, n % 4, kt * P:kt * P + P], ident)
                ins.then_inc(fill(key), 1)
        if i >= 2:
            j, s, qt = items[i - 2]
            n, g = 2 * j + s, 2 * (j // 4) + s
            if s == qt == 0:
                out_o = claim(("o1", j))
            o = out_o[64 * s:64 * s + 64, qt * P:qt * P + P]
            for br in range(2):
                m = 2 * (i - 2) + br
                read(("t1", j, s, qt, br))
                for kt in range(qt + 1):
                    mm(o, c.v[:, kt, br * 256 + g * 64:br * 256 + g * 64 + 64], c.probT[:, m % 4, kt * P:kt * P + P],
                       start=br == kt == 0, stop=False)
            r = slice(32 * (n % 4), 32 * (n % 4) + 32)
            ins = mm(o, c.vcb[r, g, :], c.pcT[r, n // 4, qt * P:qt * P + P], start=False, stop=True)
            if s == 1 and qt == NT - 1:
                ins.then_inc(c.attn_out, 1)
    for m in range(KT):
        gemm(("out", 1, m), a_hi, a_lo, needs=(lambda k: read(("o1", k))) if m == 0 else None)
    mlp(1)

    k2 = {n: c.phase2[:, a:a + w] for n, (a, w) in PHASE2.items()}
    for l in range(LAYERS2):
        for name, n in (("cq", 2), ("ckv", 2), ("kpe", 1), ("uf", 4)):
            for i in range(n):
                gemm((name, l, i), h_hi, h_lo, needs=parted("h", 4 + l) if name == "cq" and i == 0 else None)
                if name == "cq" and i == 0:
                    norm_sum(5 if l else "final")
                if l == 0 and name == "ckv" and i == 1:
                    norm_sum(4)
                if name == "uf" and i == 1:
                    for which in range(2):
                        sum_squares(("lat", l, which), ones, 2)
        cn_hi, cn_lo = tiles(c.cn_hi, 4), tiles(c.cn_lo, 4)
        for h in range(MLA_H):
            gemm(("uq", l, h), cn_hi[0:2], cn_lo[0:2], tile0=2 * (h % 4), needs=parted("cn", l) if h == 0 else None)
        for i in range(4):
            gemm(("kn", l, i), cn_hi[2:4], cn_lo[2:4], tile0=2 * i, needs=parted("cn", l, first=2) if i == 0 else None)
        for batch in range(4):
            for h in range(4):
                sum_squares(("hs2", l, batch // 2, 4 * (batch % 2) + h), ones[0:MLA_QK, 0:MLA_QK], rows=MLA_QK)
            if batch == 0:
                token_major([("v2", l, tt) for tt in range(NT)], c.cn_hi[:, 2:4, :], c.cn_lo[:, 2:4, :], 2)
            for z in (2 * batch, 2 * batch + 1):
                gemm((("za", "zf")[z // 4], l, z % 4), h_hi, h_lo)
        for tt in range(NT):
            read(("v2", l, tt))
        items = [(j, s, qt) for j in range(4) for s in range(2) for qt in range(NT)]
        base = l * len(items)
        for i in range(len(items) + 3):
            if i < len(items):
                j, s, qt = items[i]
                key, h = ("s2", l, j, s, qt), 2 * j + s
                out = claim(key)
                if qt == 0:
                    pe.wait_ge(c.head_ready, (l * 2 + 1) * MLA_H + h + 1)
                mm(out[:, :], c.q2[0:MLA_QK, h, qt * P:qt * P + P], c.k2[0:MLA_QK, h, :], start=True, stop=True)\
                    .then_inc(fill(key), 1)
            if 2 <= i < len(items) + 2:
                j, s, qt = items[i - 2]
                key, n = ("t2", l, j, s, qt), i - 2
                out = claim(key)
                pe.wait_ge(c.prob2_ready, base + n + 1)
                for kt in range(NT):
                    ins = nc.tensor.transpose(out[:, kt * P:kt * P + P], c.prob2[:, n % 3, kt * P:kt * P + P], ident)
                ins.then_inc(fill(key), 1)
            if i >= 3:
                j, s, qt = items[i - 3]
                n, h = i - 3, 2 * j + s
                if s == qt == 0:
                    out_o = claim(("o2", l, j))
                o = out_o[64 * s:64 * s + 64, qt * P:qt * P + P]
                read(("t2", l, j, s, qt))
                for kt in range(NT):
                    ins = mm(o, c.v2[:, kt, h * 64:h * 64 + 64], c.probT2[:, n % 2, kt * P:kt * P + P],
                             start=kt == 0, stop=kt == NT - 1)
                if s == 1 and qt == NT - 1:
                    ins.then_inc(c.attn_out, 1)

        if l == 0:
            pe.wait_ge(c.phase2_loaded, 16)
        for g in range(FG):
            read(("uf", l, g))
        for g in range(FG):
            for tt in range(NT):
                key = ("dd", l, g, tt)
                out = claim(key)
                mm(out[:, 0:2 * P], c.u_f[:, g, tt * P:tt * P + P], k2["dft_d"], start=True, stop=True).then_inc(fill(key), 1)
        outs = [claim(("f", l, g)) for g in range(FG)]
        first = block[("f", l, 0)][0]
        for g in range(FG):
            for tt in range(NT):
                read(("dd", l, g, tt))
        for tt in range(NT):
            pe.wait_ge(c.w_lo_ready, first + tt + 1)
            for part in range(2):
                w, d = slice(part * T, part * T + T), slice(part * P, part * P + P)
                for g in range(FG):
                    slot = (first + tt) % RING
                    ins = three(outs[g][:, :], c.d_hi[:, tt, g, d], c.d_lo[:, tt, g, d], c.w_hi[:, slot, w], c.w_lo[:, slot, w],
                                tt == part == 0, tt == NT - 1 and part == 1)
            ins.then_inc(c.block_used, 1)
        for m in range(KT):
            gemm(("ga", l, m, 0), h_hi, h_lo)
            gemm(("gf", l, m, 0), h_hi, h_lo)
            gemm(("ya2", l, m), a_hi[0:4], a_lo[0:4], needs=parted("oa", l) if m == 0 else None)
            gemm(("yf2", l, m), a_hi[4:8], a_lo[4:8], tile0=4, needs=parted("of", l) if m == 0 else None)
        m_hi, m_lo = tiles(c.m_hi), tiles(c.m_lo)
        for m in range(KT):
            gemm(("out2", l, m), m_hi, m_lo, needs=parted("m", l) if m == 0 else None)


def x_final(eng, c, bank, n, k):
    if n == 0:
        eng.wait_ge(c.x_loaded[k // 2], 16)
        return
    if n == 4:
        eng.wait_ge(c.final_ready, k + 1)
        return
    key = {1: ("out", 0, k), 2: ("down", 0, FF_PARTS - 1, k), 3: ("out", 1, k), "final": ("down", 1, FF_PARTS - 1, k),
           5: ("out2", 0, k)}[n]
    b, use, _ = bank[key]
    eng.wait_ge(c.bank_read[b], use + 1)


def source_numbers(split):
    return {key: n for n, key in enumerate(k for k in split if k[0] in ("h", "ya", "cn", "m"))}


def program_scalar(act, nc, c, block, bank, split, n_blocks):
    f = nc.scalar.activation
    source = source_numbers(split)
    pa = {n: c.params[:, a:a + w] for n, (a, w) in PARAMS.items()}
    eps = pa["eps"]
    count = {"w": 0, "sq": 0, "used": 0, "rstd": 0, "step": 0, "norm_sq": 0}
    reader = [None, None]

    def weights(upto):
        while count["w"] <= min(upto, n_blocks - 1):
            b = count["w"]
            act.wait_ge(c.raw_loaded[b % RING], 16 * (b // RING + 1))
            if b >= RING:
                act.wait_ge(c.block_used, b - RING + 1)
            f(c.w_hi[:, b % RING, :], c.raw[:, b % RING, :], ACT.Copy).then_inc(c.w_hi_ready, 1)
            count["w"] += 1

    def product(key):
        weights(block[key][1] + 2)
        act.wait_ge(c.block_used, block[key][1] + 1)
        return c.psum[bank[key][0]]

    def filled(key):
        b, _, n = bank[key]
        act.wait_ge(c.bank_filled[b], n + 1)
        return c.psum[b]

    def read(key):
        b, n, _ = bank[key]
        act.wait_ge(c.bank_read[b], n + 1)

    def release(key):
        return c.bank_read[bank[key][0]]

    def step(ins):
        ins.then_inc(c.scalar_step, 1)
        count["step"] += 1
        act.wait_ge(c.scalar_step, count["step"])

    def square_buffer(i, sem, value):
        if reader[i % 2]:
            act.wait_ge(*reader[i % 2])
        reader[i % 2] = (sem, value)
        return c.sq[:, i % 2, :]

    def square(src, rows=P):
        i = count["sq"]
        f(square_buffer(i, c.sq_used, i + 1)[0:rows, :], src, ACT.Square).then_inc(c.sq_ready, 1)
        count["sq"] += 1

    def log_mean(dst, key, width, n=1, rows=P):
        count["used"] += n
        act.wait_ge(c.sq_used, count["used"])
        f(dst, c.psum[bank[key][0]][0:rows, :], ACT.Ln, bias=eps[0:rows, :], scale=1.0 / width).then_inc(release(key), 1)

    def rstds(keys, width, n=1):
        outs = [c.rstd[:, (count["rstd"] + i) % 2, :] for i in range(len(keys))]
        for key, out in zip(keys, outs):
            log_mean(out, key, width, n)
        for key, out in zip(keys, outs):
            read(key)
            f(out, out, ACT.Exp, scale=-0.5).then_inc(c.rstd_ready, 1)
        count["rstd"] += len(keys)

    def hi(key, dst, after=None):
        if after:
            read(after)
        elif key in source:
            act.wait_ge(c.split_src, source[key] + 1)
        f(dst, c.stage[:, split[key] % 3, :], ACT.Copy).then_inc(c.split_hi, 1)

    def norm_tile(n, k, split_too=True):
        slot = NORMS.index(n) % 2
        x_final(act, c, bank, n, k)
        if k == 0:
            dst = c.norm[:, slot, :]
        else:
            i = count["norm_sq"]
            dst = square_buffer(i, c.norm_sum, i + 1)
            count["norm_sq"] += 1
        f(dst, c.x[:, k, :], ACT.Square).then_inc(c.norm_sq, 1)
        if split_too:
            h = 4 if n == "final" else n
            hi(("h", h, k), c.h_hi[:, k, :])

    def norm_root(n):
        out = c.norm[:, NORMS.index(n) % 2, :]
        f(out, filled(("ssq", n))[:, :], ACT.Ln, bias=eps, scale=1.0 / D).then_inc(release(("ssq", n)), 1)
        read(("ssq", n))
        f(out, out, ACT.Exp, scale=-0.5).then_inc(c.norm_ready, 1)

    def products_before_norm(n, *key):
        for m in range(KT):
            passed(*key, m)
            if m:
                norm_tile(n, m - 1)
        norm_tile(n, KT - 1)

    def passed(*key):
        weights(block[key][1] + 2)

    def mlp(layer):
        weights(block[("up", layer, 0, 0)][1] + 2)
        norm_root(2 * layer + 1)
        for q in range(FF_PARTS):
            for m in range(KT):
                up, key, i = ("up", layer, q, m), ("a", layer, q, m), (layer * FF_PARTS + q) * KT + m
                passed(*up)
                read(up)
                act.wait_ge(c.split_lo, split[key] - 2)
                step(f(c.stage[:, split[key] % 3, :], c.relu[:, i % 2, :], ACT.Square))
                hi(key, c.a_hi[:, m, :])
            if q < FF_PARTS - 1:
                for m in range(KT):
                    passed("down", layer, q, m)
            else:
                products_before_norm((2, "final")[layer], "down", layer, q)

    act.dma_start(c.params[:, :], c.in_params).then_inc(c.params_loaded, 16)
    act.dma_start(c.common[:, :], c.in_common).then_inc(c.common_loaded, 16)
    act.dma_start(c.phase0[:, :], c.in_phase0).then_inc(c.phase0_loaded, 16)
    act.wait_ge(c.params_loaded, 16)
    for k in range(KT):
        norm_tile(0, k)
        if k == 0:
            weights(0)
    weights(block[("ab",)][1] + 2)
    norm_root(0)
    for i in range(12):
        passed("qkv", i)
        act.wait_ge(c.conv_ready, i + 1)
        f(c.qkv[:, i, :], c.qkv[:, i, :], ACT.Silu).then_inc(c.silu_done, 1)
    for i in range(4):
        passed("z", i)
        read(("z", i))
        f(c.z[:, i, :], c.z[:, i, :], ACT.Silu).then_inc(c.silu_done, 1)
    act.wait_ge(c.g_e_ready, 1)
    f(c.beta_row[0:8, :], c.beta_row[0:8, :], ACT.Sigmoid)
    step(f(c.e_row[0:8, :], c.e_row[0:8, :], ACT.Exp, scale=-1.0))
    f(c.tiny[0:8, 0:1], pa["a_log"][0:8, :], ACT.Exp).then_inc(c.a_exp_ready, 1)
    f(c.e_row[0:8, :], c.e_row[0:8, :], ACT.Ln, bias=c.common[0:8, P:P + 1]).then_inc(c.g_ln_ready, 1)
    for t in range(12):
        passed(("cg", "hs", "bg")[t % 3], t // 3)
        if t and t % 3 == 0:
            hi(("yb", t // 3 - 1), c.a_hi[:, 3 + t // 3, :], after=("bg", t // 3 - 1))
        n = t - 3
        if 0 <= n + 1 < 8:
            square(c.qkv[:, L2_ORDER[n + 1], :])
        if 0 <= n < 8:
            if n >= 2:
                act.wait_ge(c.l2_ready, n - 1)
            rstds([("l2", L2_ORDER[n])], 1.0)
    hi(("yb", 3), c.a_hi[:, 7, :], after=("bg", 3))
    act.wait_ge(c.ekd_in, 1)
    f(c.tok[:, 3, :], c.tok[:, 7, :], ACT.Exp)
    f(c.tok[:, 4, :], c.tok[:, 2, :], ACT.Exp).then_inc(c.egt_ready, 1)

    def decays(p, s):
        h = 2 * p + s
        out = filled(("gcb", h))
        for ch in range(NT):
            t = slice(ch * P, ch * P + P)
            ins = f(c.MT[p % 2][:, s, t], out[:, t], ACT.Exp, bias=c.tok[:, 6, 8 * ch + h:8 * ch + h + 1])
        ins.then_inc(release(("gcb", h)), 1)

    decays(0, 0)
    decays(0, 1)
    for p in range(4):
        for level in range(7):
            for s in range(2):
                key, dst = (("y", 2 * p + s, level), c.Y) if level else (("xt", 2 * p + s, 0), c.X)
                part = (slice(64, P), slice(0, NT * 64)) if level == 6 else (slice(0, P), slice(0, T))
                f(dst[:, s, :][part], filled(key)[part], ACT.Copy).then_inc(release(key), 1)
            if p < 3 and 1 <= level <= 2:
                decays(p + 1, level - 1)
        for s in range(2):
            key, r = ("w", 2 * p + s), slice(64 * s, 64 * s + 64)
            f(c.wT[r, p, :], filled(key)[r, :], ACT.Copy).then_inc(release(key), 1)
    for p in range(4):
        f(c.egc[:, p, :], filled(("eg", p))[:, :], ACT.Exp).then_inc(release(("eg", p)), 1)
    for m in range(KT - 2):
        passed("outb", m)
    read(("o", NT - 1))
    square(c.gdn_o[:, 0, :])
    square(c.gdn_o[:, 1, :])
    rstds([("on", 0), ("on", 1)], GDN_D)
    square(c.gdn_o[:, 2, :])
    square(c.gdn_o[:, 3, :])
    for p in range(4):
        if p == 2:
            passed("outb", KT - 1)
            rstds([("on", 2), ("on", 3)], GDN_D)
        hi(("ya", p), c.a_hi[:, p, :])
    act.dma_start(c.phase1[:, :], c.in_phase1).then_inc(c.phase1_loaded, 16)
    products_before_norm(1, "out", 0)
    mlp(0)

    weights(block[("gl_gates",)][1] + 2)
    norm_root(2)
    read(("gl_gates",))
    f(c.gate_row[0:48, :], c.gate_row[0:48, :], ACT.Sigmoid).then_inc(c.gate_ready, 1)
    act.wait_ge(c.kc_pad, 2)
    for kv in range(2):
        f(c.kc_hi[:, kv, 4, 0:16], pa["cmp_pos"], ACT.Copy).then_inc(c.kc_hi_ready, 1)
        for i in range(2):
            key, bank_key = ("kc", kv, i), (("kc", "vc")[kv], i)
            passed(*bank_key)
            read(bank_key)
            tile = c.stage[:, split[key] % 3, :]
            for g in range(2):
                for s in range(2):
                    ins = f(c.kc_hi[64 * s:64 * s + 64, kv, 2 * i + g, 0:T // 2], tile[64 * g:64 * g + 64, s:T:2], ACT.Copy)
            ins.then_inc(c.split_hi, 1)
    passed("q", 7)
    for kv in range(2):
        for m in range(2):
            key, i = ("cmp1", kv, m), 2 * kv + m
            out = product(key)
            act.wait_ge(c.hid_bias, i + 1)
            dst, src = c.hid_k[:, m, :], out[:, 0:P]
            if kv:
                dst = c.hid_v[:, m, :].rearrange("p (g n c) -> p g n c", g=4, n=4)
                src = src.rearrange("p (g c) -> p g c", g=4).unsqueeze(2).to_broadcast([P, 4, 4, N_CMP])
            f(dst, src, ACT.Silu, bias=c.tiny[:, 8 + i:9 + i]).then_inc(release(key), 1)
    passed("ks", 0)
    key = ("kcb",)
    act.wait_ge(c.kcb_clear, 1)
    for s in range(2):
        rows = slice(64 * s, 64 * s + 64)
        src = filled(key)[rows, 0:P].rearrange("p (n s c) -> p n s c", s=2, c=N_CMP)[:, :, s]
        ins = f(c.kcb[rows, :, s, :], src, ACT.Copy)
    ins.then_inc(release(key), 1)
    passed("ks", 1)
    f(c.vcb[:, :, :].rearrange("p g d -> p (g d)"), filled(("vcb",))[:, 0:4 * NSA_D], ACT.Copy).then_inc(release(("vcb",)), 1)

    def block_exp(qt):
        act.wait_ge(c.cmp_shift, qt + 1)
        f(c.cmp_e[:, qt, :], c.cmp_s[:, qt, :], ACT.Exp).then_inc(c.cmp_exp, 1)

    def turned(qt):
        key = ("pcT", qt)
        f(c.pcT[:, :, qt * P:(qt + 1) * P], filled(key)[:, :].rearrange("p (i q) -> p i q", i=4), ACT.Copy)\
            .then_inc(release(key), 1)

    first = block[("v", 0)][0]
    passed("kw", 0)
    block_exp(0)
    passed("kw", 1)
    block_exp(1)
    weights(first + 2)
    block_exp(2)
    block_exp(3)
    turned(0)
    turned(1)
    weights(first + 3)
    turned(2)
    turned(3)
    passed("v", 0)
    items = [(j, s, qt) for j in range(8) for s in range(2) for qt in range(NT)]
    for i in range(len(items) + 2):
        if i < len(items):
            j, s, qt = items[i]
            for br in range(2):
                n, key, end = 2 * i + br, ("s1", j, s, qt, br), (qt + 1) * P
                act.wait_ge(c.nb_ready, n + 1)
                f(c.prob[:, n % 4, 0:end], c.psum[bank[key][0]][:, 0:end], ACT.Exp, bias=c.nb[:, n % 4, 0:1],
                  accum_out=c.nb[:, n % 4, 1:2]).then_inc(release(key), 1)
        if 1 <= i <= len(items):
            j, s, qt = items[i - 1]
            for br in range(2):
                n, key, end = 2 * (i - 1) + br, ("t1", j, s, qt, br), (qt + 1) * P
                f(c.probT[:, n % 4, 0:end], filled(key)[:, 0:end], ACT.Copy).then_inc(release(key), 1)
        if i >= 2 and items[i - 2][1:] == (1, NT - 1):
            j = items[i - 2][0]
            act.wait_ge(c.attn_out, j + 1)
            f(c.a_hi[:, j, :], c.psum[bank[("o1", j)][0]][:, :], ACT.Copy).then_inc(c.attn_hi, 1)
    act.dma_start(c.phase2[:, :], c.in_phase2).then_inc(c.phase2_loaded, 16)
    products_before_norm(3, "out", 1)
    mlp(1)

    for l in range(LAYERS2):
        first = block[("cq", l, 0)][1]
        weights(first + 2)
        if l == 0:
            norm_root("final")
            weights(first + 3)
            for k in range(KT):
                norm_tile(4, k, split_too=False)
            weights(first + 4)
        norm_root(4 + l)
        for i in range(2):
            passed("ckv", l, i)
        passed("kpe", l, 0)
        passed("uf", l, 1)
        for which, name in enumerate(("cq", "ckv")):
            for i in range(2):
                read((name, l, i))
                square(c.c[:, 2 * which + i, :])
        passed("uf", l, 2)
        rstds([("lat", l, 0), ("lat", l, 1)], 2 * P, 2)
        passed("uf", l, 3)
        for i in range(4):
            hi(("cn", l, i), c.cn_hi[:, i, :])
        for h in range(MLA_H):
            key = ("uq", l, h)
            f(c.q2[:, h, :], product(key)[:, :], ACT.Copy).then_inc(release(key), 1)
        passed("kn", l, 3)

        def square_head(batch, i):
            h = 4 * (batch % 2) + i
            if batch < 2:
                read(("uq", l, h))
            else:
                read(("kn", l, h // 2))
                act.wait_ge(c.kpe_ready, l + 1)
            square((c.q2, c.k2)[batch // 2][0:MLA_QK, h, :], MLA_QK)

        for i in range(4):
            square_head(0, i)
        for tt in range(NT):
            key = ("v2", l, tt)
            f(c.v2[:, tt, :], product(key)[:, :], ACT.Copy).then_inc(release(key), 1)
        for batch in range(4):
            keys = [("hs2", l, batch // 2, 4 * (batch % 2) + i) for i in range(4)]
            roots = [c.head_r[batch % 2][0:MLA_QK, i, :] for i in range(4)]
            if batch < 3:
                square_head(batch + 1, 0)
                square_head(batch + 1, 1)
            if batch == 3:
                read(("za", l, 3))
                f(c.z_a[:, :, :], c.z_a[:, :, :], ACT.Silu).then_inc(c.z_ready, 1)
            if batch >= 2:
                act.wait_ge(c.head_ready, l * 2 * MLA_H + 4 * (batch - 1))
            for key, out in zip(keys, roots):
                log_mean(out, key, MLA_QK, rows=MLA_QK)
            for key, out in zip(keys, roots):
                read(key)
                f(out, out, ACT.Exp, scale=-0.5).then_inc(c.head_r_ready, 1)
            for z in (2 * batch, 2 * batch + 1):
                passed(("za", "zf")[z // 4], l, z % 4)
            if batch < 3:
                square_head(batch + 1, 2)
                square_head(batch + 1, 3)
        items = [(j, s, qt) for j in range(4) for s in range(2) for qt in range(NT)]
        base = l * len(items)
        for i in range(len(items) + 6):
            if i < len(items):
                key = ("s2", l, *items[i])
                act.wait_ge(c.nb2_ready, base + i + 1)
                f(c.prob2[:, i % 3, :], c.psum[bank[key][0]][:, :], ACT.Exp, bias=c.nb2[:, i % 2, 0:1],
                  accum_out=c.nb2[:, i % 2, 1:2]).then_inc(release(key), 1)
            if 2 <= i < len(items) + 2:
                key = ("t2", l, *items[i - 2])
                f(c.probT2[:, i % 2, :], filled(key)[:, :], ACT.Copy).then_inc(release(key), 1)
            if i >= 5 and i - 5 < len(items) and items[i - 5][1:] == (1, NT - 1):
                j = items[i - 5][0]
                hi(("oa", l, j), c.a_hi[:, j, :], after=("o2", l, j))
        for g in range(FG):
            for tt in range(NT):
                f(c.d_hi[:, tt, g, :], filled(("dd", l, g, tt))[:, 0:2 * P], ACT.Copy).then_inc(c.d_hi_ready, 1)
        read(("zf", l, 3))
        f(c.z_f[:, :, :], c.z_f[:, :, :], ACT.Silu).then_inc(c.z_ready, 1)
        for g in range(FG):
            product(("f", l, g))
            hi(("of", l, g), c.a_hi[:, 4 + g, :], after=("f", l, g))
        for m in range(KT):
            for branch, name in enumerate(("ga", "gf")):
                key, at, gate = (name, l, m, 0), (l * 2 + branch) * KT + m, c.sig[:, 2 * (m % 2) + branch, :]
                passed(*key)
                read(key)
                f(gate, gate, ACT.Sigmoid, bias=pa["merge"][:, at:at + 1]).then_inc(c.sig_ready, 1)
            passed("yf2", l, m)
            if m:
                hi(("m", l, m - 1), c.m_hi[:, m - 1, :])
        hi(("m", l, KT - 1), c.m_hi[:, KT - 1, :])
        if l < LAYERS2 - 1:
            products_before_norm(5 + l, "out2", l)
        else:
            for m in range(KT):
                passed("out2", l, m)


def program_vector(dve, nc, c, block, bank, split):
    v = nc.vector
    tt_op, stt = v.tensor_tensor, v.scalar_tensor_tensor
    source = source_numbers(split)
    pa = {n: c.params[:, a:a + w] for n, (a, w) in PARAMS.items()}
    ident = c.common[:, 0:P]
    count = {"step": 0, "rstd": 0, "norm_sq": 0, "norm_sum": 0}

    def product(key):
        dve.wait_ge(c.block_used, block[key][1] + 1)
        return c.psum[bank[key][0]]

    def filled(key):
        b, _, n = bank[key]
        dve.wait_ge(c.bank_filled[b], n + 1)
        return c.psum[b]

    def read(key):
        b, n, _ = bank[key]
        dve.wait_ge(c.bank_read[b], n + 1)

    def release(key):
        return c.bank_read[bank[key][0]]

    def step(ins):
        ins.then_inc(c.vector_step, 1)
        count["step"] += 1
        dve.wait_ge(c.vector_step, count["step"])

    def rstd(rows=P):
        dve.wait_ge(c.rstd_ready, count["rstd"] + 1)
        count["rstd"] += 1
        return c.rstd[0:rows, (count["rstd"] - 1) % 2, :]

    def stage(key, writes=True):
        if writes and split[key] >= 3:
            dve.wait_ge(c.split_lo, split[key] - 2)
        return c.stage[:, split[key] % 3, :]

    def lo(key, hi, dst):
        dve.wait_ge(c.split_hi, split[key] + 1)
        tt_op(dst, stage(key, False), hi.bitcast(F32), ALU.subtract).then_inc(c.split_lo, 1)

    def norm_tile(n, k, gain=None):
        h, slot = 4 if n == "final" else n, NORMS.index(n) % 2
        if k < KT:
            x_final(dve, c, bank, n, k)
            if gain:
                v.tensor_scalar(stage(("h", h, k)), c.x[:, k, :], gain(k), None, ALU.mult).then_inc(c.split_src, 1)
        if k:
            count["norm_sq"] += 1
            if k > 1:
                add_square(slot)
            if gain:
                lo(("h", h, k - 1), c.h_hi[:, k - 1, :], c.h_lo[:, k - 1, :])

    def add_square(slot):
        i = count["norm_sum"]
        dve.wait_ge(c.norm_sq, count["norm_sq"])
        if i % (KT - 1):
            dve.wait_ge(c.norm_sum, i)
        tt_op(c.norm[:, slot, :], c.norm[:, slot, :], c.sq[:, i % 2, :], ALU.add).then_inc(c.norm_sum, 1)
        count["norm_sum"] += 1

    def gains(name, first):
        return lambda k: pa[name][:, first + k:first + k + 1]

    def root(n):
        i = NORMS.index(n)
        dve.wait_ge(c.norm_ready, i + 1)
        return c.norm[:, i % 2, :]

    def sums_before_norm(n, gain, *key):
        for m in range(KT):
            add_to_x((*key, m), m)
            norm_tile(n, m, gain)
        norm_tile(n, KT, gain)

    def add_to_x(key, m):
        out = product(key)
        tt_op(c.x[:, m, :], c.x[:, m, :], out[:, :], ALU.add).then_inc(release(key), 1)

    def mlp(layer, next_norm, gain):
        r = root(2 * layer + 1)
        for q in range(FF_PARTS):
            for m in range(KT + 1):
                if m < KT:
                    i, key = (layer * FF_PARTS + q) * KT + m, ("up", layer, q, m)
                    stt(c.relu[:, i % 2, :], product(key)[:, :], 0.0, r, ALU.max, ALU.mult).then_inc(release(key), 1)
                if m:
                    lo(("a", layer, q, m - 1), c.a_hi[:, m - 1, :], c.a_lo[:, m - 1, :])
            if q < FF_PARTS - 1:
                for m in range(KT):
                    add_to_x(("down", layer, q, m), m)
            else:
                sums_before_norm(next_norm, gain, "down", layer, q)

    dve.wait_ge(c.params_loaded, 16)
    gain = gains("mix_norm", 0)
    for k in range(KT + 1):
        norm_tile(0, k, gain)
    r = root(0)
    x_row, e_row = c.g_row[0:8, :], c.e_row[0:8, :]
    out = product(("ab",))
    step(tt_op(x_row, out[0:8, :], r[0:8, :], ALU.mult))
    tt_op(c.beta_row[0:8, :], out[32:40, :], r[32:40, :], ALU.mult).then_inc(release(("ab",)), 1)
    v.tensor_scalar(x_row, x_row, pa["dt_bias"][0:8, :], None, ALU.add).then_inc(c.g_x_ready, 1)
    dve.wait_ge(c.g_x_ready, 1)
    stt(e_row, x_row, -1.0, x_row, ALU.mult, ALU.max).then_inc(c.g_e_ready, 1)
    for i in range(12):
        key, u, y = ("qkv", i), c.sc[:, i % 2, :], c.qkv[:, i, :]
        tap = [pa["conv"][:, 4 * i + n:4 * i + n + 1] for n in range(4)]
        tt_op(u, product(key)[:, :], r, ALU.mult).then_inc(release(key), 1)
        read(key)
        step(v.tensor_scalar(y, u, tap[3], None, ALU.mult))
        step(stt(y[:, 1:T], u[:, 0:T - 1], tap[2], y[:, 1:T], ALU.mult, ALU.add))
        step(stt(y[:, 2:T], u[:, 0:T - 2], tap[1], y[:, 2:T], ALU.mult, ALU.add))
        stt(y[:, 3:T], u[:, 0:T - 3], tap[0], y[:, 3:T], ALU.mult, ALU.add).then_inc(c.conv_ready, 1)
    for i in range(4):
        key = ("z", i)
        tt_op(c.z[:, i, :], product(key)[:, :], r, ALU.mult).then_inc(release(key), 1)
    dve.wait_ge(c.phase0_loaded, 16)
    a = PHASE0["notyet"][0]
    v.tensor_copy(c.eye16[:, :], ident)
    v.tensor_copy(c.notyet16[:, :], c.phase0[:, a:a + P]).then_inc(c.notyet16_ready, 1)
    dve.wait_ge(c.conv_ready, 12)
    for t in range(13):
        for key in BESIDE.get(t - 1, ()):
            if key[0] == "l2":
                y = c.qkv[:, key[1], :]
                if key[1] < 4:
                    stt(y, y, GDN_D ** -0.5, rstd(), ALU.mult, ALU.mult).then_inc(c.l2_ready, 1)
                else:
                    tt_op(y, y, rstd(), ALU.mult).then_inc(c.l2_ready, 1)
                continue
            out, done = filled(key), release(key)
            if key[0] == "gT":
                v.tensor_copy(c.tok[:, 0:2, :].rearrange("p a b -> p (a b)"), out[:, 0:64]).then_inc(done, 1)
            elif key[0] == "gc":
                v.tensor_copy(c.tok[:, 2, :], out[:, 0:32]).then_inc(done, 1)
                read(key)
                v.tensor_scalar(c.tok[:, 6, :], c.tok[:, 2, :], -1.0, None, ALU.mult)
            elif key[0] == "gl":
                tt_op(c.tok[:, 7, :], out[:, 0:32], c.tok[:, 2, :], ALU.subtract).then_inc(done, 1)
                read(key)
                v.tensor_copy(c.tiny[:, 1:2], c.tok[:, 7, 0:1]).then_inc(c.ekd_in, 1)
            elif key[0] == "gcr":
                v.tensor_copy(c.gc_row[0:8, :], out[0:8, :]).then_inc(done, 1)
            else:
                p = key[1]
                dve.wait_ge(c.l2_ready, p + 1)
                tt_op(c.kb[:, p, :], out[:, :], c.qkv[:, 4 + p, :], ALU.mult).then_inc(done, 1)
        i, raw, gated, y = t // 3, c.sc[:, 0, :], c.sc[:, 1, :], c.sc[:, 2, :]
        if t < 12:
            key = (("cg", "hs", "bg")[t % 3], i)
            out = product(key)
            if t % 3 == 0:
                tt_op(raw, out[:, :], r, ALU.mult).then_inc(release(key), 1)
            elif t % 3 == 1:
                read(("cg", i))
                tt_op(gated, out[:, :], raw, ALU.mult).then_inc(release(key), 1)
                read(key)
                step(tt_op(gated, gated, r, ALU.mult))
                tap = [pa["sc_conv"][:, 3 * i + n:3 * i + n + 1] for n in range(3)]
                step(v.tensor_scalar(y, gated, tap[2], None, ALU.mult))
                step(stt(y[:, 1:T], gated[:, 0:T - 1], tap[1], y[:, 1:T], ALU.mult, ALU.add))
                step(stt(y[:, 2:T], gated[:, 0:T - 2], tap[0], y[:, 2:T], ALU.mult, ALU.add))
                step(tt_op(y, y, r, ALU.mult))
            else:
                tt_op(stage(("yb", i)), out[:, :], y, ALU.mult).then_inc(release(key), 1)
        if t and t % 3 == 0:
            lo(("yb", i - 1), c.a_hi[:, 3 + i, :], c.a_lo[:, 3 + i, :])
        if t == 1:
            dve.wait_ge(c.g_ln_ready, 1)
            step(stt(x_row, x_row, 0.0, e_row, ALU.max, ALU.add))
            dve.wait_ge(c.a_exp_ready, 1)
            v.tensor_scalar(x_row, x_row, c.tiny[0:8, 0:1], -1.0, ALU.mult, ALU.mult).then_inc(c.g_ready, 1)
    dve.wait_ge(c.egt_ready, 1)
    step(tt_op(c.tok[:, 5, :], c.tok[:, 4, :], c.tok[:, 1, :], ALU.mult))

    def by_head(a):
        return a.rearrange("p (h d) -> p h d", h=GDN_H)

    def token_major(ch):
        def per_token(n):
            return c.tok[:, n, 8 * ch:8 * ch + 8].unsqueeze(2).to_broadcast([P, GDN_H, GDN_D])
        key = ("kt", ch)
        out = by_head(filled(key)[:, :])
        tt_op(by_head(c.kd[:, ch, :]), out, per_token(3), ALU.mult)
        tt_op(by_head(c.kbe[:, ch, :]), out, per_token(5), ALU.mult).then_inc(release(key), 1)
        key = ("vt", ch)
        tt_op(by_head(c.vb[:, ch, :]), by_head(filled(key)[:, :]), per_token(1), ALU.mult).then_inc(release(key), 1)

    def by_chunk(a):
        return a.rearrange("p (n i) -> p n i", n=NT)

    def level_mask(level):
        a = PHASE0["levels"][0] + level * P
        return c.phase0[:, a:a + P].unsqueeze(1).to_broadcast([P, NT, P])

    eye = ident.unsqueeze(1).to_broadcast([P, NT, P])

    def decay(p, name):
        for s in range(2):
            h, key = 2 * p + s, (name, 2 * p + s)
            decays = c.MT[p % 2][:, s, :]
            read(("gcb", h) if name == "qk" else ("qk", h))
            dst = decays if name == "kk" else (c.AT0, c.AT1)[h // 4][:, h % 4, :]
            tt_op(dst, filled(key)[:, :], decays, ALU.mult).then_inc(release(key), 1)

    decay(0, "qk")
    decay(0, "kk")
    for p in range(4):
        for s in range(2):
            if p:
                filled(("w", 2 * p - 2 + s))
            read(("kk", 2 * p + s))
            step(tt_op(by_chunk(c.ML[:, s, :]), by_chunk(c.MT[p % 2][:, s, :]), level_mask(0), ALU.mult))
            tt_op(by_chunk(c.XT[:, s, :]), eye, by_chunk(c.ML[:, s, :]), ALU.subtract).then_inc(c.xt_ready, 1)
        for level in range(7):
            for s in range(2):
                if level < 5:
                    if level:
                        filled(("y", 2 * p + s, level))
                    else:
                        dve.wait_ge(c.xt_ready, 2 * p + s + 1)
                    tt_op(by_chunk(c.ML[:, s, :]), by_chunk(c.MT[p % 2][:, s, :]), level_mask(level + 1), ALU.mult).then_inc(c.ml_ready, 1)
            for s in range(2) if level else ():
                key = ("dx", 2 * p + s, level)
                out, x, xt = filled(key), halves(c.X[:, s, :], level, 0), halves(c.XT[:, s, :], level, 1)
                if level < 6:
                    tt_op(x, x, grouped(out[:, 0:256], level), ALU.subtract)
                    tt_op(xt, xt, grouped(out[:, 256:T], level), ALU.subtract).then_inc(release(key), 1)
                else:
                    tt_op(xt[0:64], xt[0:64], grouped(out[0:64, 0:256], level), ALU.subtract).then_inc(release(key), 1)
            if p == 0 and 1 <= level <= NT:
                token_major(level - 1)
            if p < 3 and 3 <= level <= 4:
                decay(p + 1, DECAYED[level - 2])
        for s in range(2):
            key, h = ("u", 2 * p + s), 2 * p + s
            v.tensor_copy(c.u[:, :, h * 64:h * 64 + 64], filled(key)[:, 0:256].rearrange("p (n d) -> p n d", n=NT))\
                .then_inc(release(key), 1)
    for p in range(4):
        read(("eg", p))
        tt_op(c.qkv[:, p, :], c.qkv[:, p, :], c.egc[:, p, :], ALU.mult).then_inc(c.qe_ready, 1)
    for ch in range(NT):
        if ch:
            for s in range(2):
                key = ("ws", ch, s)
                half = [a.rearrange("p (a s d) -> p s a d", s=2, d=GDN_D)[:, s] for a in (c.vnew[:, :], c.u[:, ch, :])]
                out = filled(key)[:, 0:256].rearrange("p (a d) -> p a d", a=4)
                tt_op(half[0], half[1], out, ALU.subtract).then_inc(release(key), 1)
        else:
            read(("u", GDN_H - 1))
            v.tensor_copy(c.vnew[:, :], c.u[:, 0, :]).then_inc(c.vnew_ready, 1)
        t = slice(ch * P, ch * P + P)
        key = ("ds", ch)
        out = filled(key)[:, 0:256].rearrange("p (a d) -> p a d", a=4)
        if ch:
            read(("ds", ch - 1))
            step(tt_op(c.S[:, :, :], c.S[:, :, :], c.egc[:, :, ch * P + P - 1:ch * P + P].to_broadcast([P, 4, GDN_D]), ALU.mult))
            tt_op(c.S[:, :, :], c.S[:, :, :], out, ALU.add).then_inc(release(key), 1)
        else:
            v.tensor_copy(c.S[:, :, :], out).then_inc(release(key), 1)
        key = ("o", ch)
        v.tensor_copy(c.gdn_o[:, :, t], filled(key)[:, :].rearrange("p (a i) -> p a i", a=4)).then_inc(release(key), 1)
        for m in SCAN_OUT[ch - 1] if ch else ():
            add_to_x(("outb", m), m)
    for p in range(5):
        if p == 2:
            for m in SCAN_OUT[NT - 1] + SCAN_OUT[NT]:
                add_to_x(("outb", m), m)
        if p < 4:
            r, y = rstd(), c.gdn_o[:, p, :]
            read(("o", NT - 1))
            step(stt(y, y, pa["o_norm"], r, ALU.mult, ALU.mult))
            dve.wait_ge(c.silu_done, 12 + p + 1)
            tt_op(stage(("ya", p)), y, c.z[:, p, :], ALU.mult).then_inc(c.split_src, 1)
        if p:
            lo(("ya", p - 1), c.a_hi[:, p - 1, :], c.a_lo[:, p - 1, :])
    for m in SCAN_OUT[NT + 1]:
        add_to_x(("outb", m), m)
    sums_before_norm(1, gains("mlp_norm", 0), "out", 0)
    mlp(0, 2, gains("mix_norm", KT))

    v.memset(c.kc_hi[:, :, :, :].bitcast(F32), 0.0).then_inc(c.kc_pad, 1)
    v.memset(c.kc_lo[:, :, :, :].bitcast(F32), 0.0).then_inc(c.kc_pad, 1)
    v.memset(c.kcb[:, :, :, :], 0.0).then_inc(c.kcb_clear, 1)
    r = root(2)
    key = ("gl_gates",)
    tt_op(c.gate_row[0:48, :], product(key)[0:48, :], r[0:48, :], ALU.mult).then_inc(release(key), 1)
    dve.wait_ge(c.kc_pad, 2)
    for n in range(5):
        if n < 4:
            kv, i = n // 2, n % 2
            bank_key = (("kc", "vc")[kv], i)
            tt_op(stage(("kc", kv, i)), product(bank_key)[:, :], r, ALU.mult).then_inc(release(bank_key), 1)
        if n:
            kv, i = (n - 1) // 2, (n - 1) % 2
            key = ("kc", kv, i)
            if i == 0:
                dve.wait_ge(c.kc_hi_ready, kv + 1)
                tt_op(c.kc_lo[:, kv, 4, 0:16], pa["cmp_pos"], c.kc_hi[:, kv, 4, 0:16].bitcast(F32), ALU.subtract)
            dve.wait_ge(c.split_hi, split[key] + 1)
            for g in range(2):
                for s in range(2):
                    rows = slice(64 * s, 64 * s + 64)
                    ins = tt_op(c.kc_lo[rows, kv, 2 * i + g, 0:T // 2], stage(key, False)[64 * g:64 * g + 64, s:T:2],
                                c.kc_hi[rows, kv, 2 * i + g, 0:T // 2].bitcast(F32), ALU.subtract)
            ins.then_inc(c.split_lo, 1)
    for i in range(8):
        stt(c.q[:, i, :], product(("q", i))[:, :], NSA_D ** -0.5, r, ALU.mult, ALU.mult).then_inc(release(("q", i)), 1)
    for kv in range(2):
        for m in range(2):
            i = 8 + 2 * kv + m
            v.tensor_copy(c.tiny[:, i:i + 1], product(("cmp1", kv, m))[:, P:P + 1]).then_inc(c.hid_bias, 1)
    v.tensor_copy(c.tiny[:, 20:24], filled(("rcol",))[:, 0:NT]).then_inc(release(("rcol",)), 1)
    v.tensor_copy(c.gate[:, :, :].rearrange("p a b -> p (a b)"), filled(("gateT",))[:, 0:NT * 48]).then_inc(release(("gateT",)), 1)
    read(("gateT",))

    def key_tile(name, i):
        dst = {"ks": c.ks, "kw": c.kw}[name]
        tt_op(dst[:, i, :], product((name, i))[:, :], r, ALU.mult).then_inc(release((name, i)), 1)

    def by_block(a):
        return a.rearrange("p (h c) -> p h c", h=NSA_H)

    def block_shift(qt):
        a = PHASE1["cmp_mask"][0] + qt * N_CMP
        top, scores = c.stat[:, 4 * qt, :], by_block(c.cmp_s[:, qt, :])
        mask = c.phase1[:, a:a + N_CMP].unsqueeze(1).to_broadcast([P, NSA_H, N_CMP])
        tt_op(scores, by_block(filled(("sc", qt))[:, :]), mask, ALU.add).then_inc(release(("sc", qt)), 1)
        read(("sc", qt))
        step(v.reduce_max(top, scores, axis=AX))
        step(v.tensor_scalar(top, top, -1e20, None, ALU.max))
        tt_op(scores, scores, top.unsqueeze(2).to_broadcast([P, NSA_H, N_CMP]), ALU.subtract).then_inc(c.cmp_shift, 1)

    def block_probs(qt):
        total, inverse, scale = [c.stat[:, 4 * qt + n, :] for n in (1, 2, 3)]
        e = by_block(c.cmp_e[:, qt, :])
        dve.wait_ge(c.cmp_exp, qt + 1)
        step(v.reduce_sum(total, e, axis=AX))
        step(v.tensor_scalar(total, total, 1e-30, None, ALU.max))
        step(v.reciprocal(inverse, total))
        step(tt_op(scale, inverse, c.gate[:, qt, 0:NSA_H], ALU.mult))
        tt_op(e, e, scale.unsqueeze(2).to_broadcast([P, NSA_H, N_CMP]), ALU.mult).then_inc(c.cmp_p, 1)

    dve.wait_ge(c.phase1_loaded, 16)
    k1 = {n: c.phase1[:, a:a + w] for n, (a, w) in PHASE1.items()}
    v.tensor_copy(c.ident16[:, :], ident)
    v.tensor_copy(c.causal16[:, :], k1["causal"]).then_inc(c.masks16_ready, 1)

    def rotate(i):
        key, b = ("rope", i), 2 * (i % 2)
        y = c.q[:, i, :] if i < 8 else (c.ks, c.kw)[(i - 8) // 2][:, i % 2, :]
        out = filled(key)
        tt_op(c.rope_t[:, b, :], y, k1["cos"], ALU.mult)
        tt_op(c.rope_t[:, b + 1, :], out[:, :], k1["sin"], ALU.mult).then_inc(release(key), 1)
        read(key)
        tt_op(y, c.rope_t[:, b, :], c.rope_t[:, b + 1, :], ALU.add).then_inc(c.rope_ready, 1)

    key_tile("ks", 0)
    key_tile("ks", 1)
    block_shift(0)
    read(("ks", 1))
    rotate(8)
    rotate(9)
    key_tile("kw", 0)
    block_shift(1)
    block_probs(0)
    key_tile("kw", 1)
    block_shift(2)
    block_probs(1)
    read(("kw", 1))
    rotate(10)
    rotate(11)
    block_shift(3)
    block_probs(2)
    block_probs(3)
    for i in range(8):
        rotate(i)
    read(("rcol",))
    for tt in range(NT):
        v.tensor_scalar(c.v[:, tt, :], product(("v", tt))[:, :], c.tiny[:, 20 + tt:21 + tt], None, ALU.mult)\
            .then_inc(release(("v", tt)), 1)
    items = [(j, s, qt) for j in range(8) for s in range(2) for qt in range(NT)]
    for i in range(len(items) + 3):
        if 1 <= i <= len(items):
            j, s, qt = items[i - 1]
            for br in range(2):
                n, g = 2 * (i - 1) + br, NSA_H * (1 + br) + 2 * j + s
                read(("s1", j, s, qt, br))
                step(v.reciprocal(c.nb[:, n % 4, 2:3], c.nb[:, n % 4, 1:2]))
                e = c.prob[:, n % 4, 0:(qt + 1) * P]
                v.tensor_scalar(e, e, c.nb[:, n % 4, 2:3], c.gate[:, qt, g:g + 1], ALU.mult, ALU.mult).then_inc(c.prob_ready, 1)
        if i < len(items):
            j, s, qt = items[i]
            for br in range(2):
                n, key, end = 2 * i + br, ("s1", j, s, qt, br), (qt + 1) * P
                v.reduce_max(c.nb[:, n % 4, 0:1], filled(key)[:, 0:end], axis=AX, negate=True).then_inc(c.nb_ready, 1)
        if i >= 3 and items[i - 3][1:] == (1, NT - 1):
            j = items[i - 3][0]
            dve.wait_ge(c.attn_hi, j + 1)
            tt_op(c.a_lo[:, j, :], c.psum[bank[("o1", j)][0]][:, :], c.a_hi[:, j, :].bitcast(F32), ALU.subtract)\
                .then_inc(release(("o1", j)), 1)
    sums_before_norm(3, gains("mlp_norm", KT), "out", 1)
    step(tt_op(c.tiny[:, 24:24 + KT], pa["final_norm"], pa["norm2"][:, 0:KT], ALU.mult))
    mlp(1, "final", lambda k: c.tiny[:, 24 + k:25 + k])
    r = root("final")
    for k in range(KT):
        stt(c.x[:, k, :], c.x[:, k, :], pa["final_norm"][:, k:k + 1], r, ALU.mult, ALU.mult).then_inc(c.final_ready, 1)
    for k in range(KT + 1):
        norm_tile(4, k)

    k2 = {n: c.phase2[:, a:a + w] for n, (a, w) in PHASE2.items()}
    for l in range(LAYERS2):
        r = root(4 + l)
        if l == 0:
            step(tt_op(r, r, root("final"), ALU.mult))
        for which, name in enumerate(("cq", "ckv")):
            for i in range(2):
                tt_op(c.c[:, 2 * which + i, :], product((name, l, i))[:, :], r, ALU.mult).then_inc(release((name, l, i)), 1)
        if l == 0:
            dve.wait_ge(c.phase2_loaded, 16)
        pe_rows, swapped, key, k_gain = slice(MLA_NOPE, MLA_QK), slice(MLA_QK, P), ("kpe", l, 0), pa["k_head"][:, l:l + 1]
        tt_op(c.kpe[MLA_NOPE:P, :], product(key)[MLA_NOPE:P, :], r[MLA_NOPE:P, :], ALU.mult).then_inc(release(key), 1)
        read(key)
        v.tensor_copy(c.k2[pe_rows, :, :], c.kpe[pe_rows, :].unsqueeze(1).to_broadcast([MLA_ROPE, MLA_H, T])).then_inc(c.kpe_ready, 1)
        t0, t1 = c.head_t[pe_rows, 0, :], c.head_t[pe_rows, 1, :]
        stt(t0, c.kpe[pe_rows, :], k_gain[pe_rows, :], k2["cos_sin"][pe_rows, :], ALU.mult, ALU.mult)
        step(stt(t1, c.kpe[swapped, :], k_gain[swapped, :], k2["cos_sin"][swapped, :], ALU.mult, ALU.mult))
        step(tt_op(c.kpe[pe_rows, :], t0, t1, ALU.add))

        def group_out(g):
            key = ("uf", l, g)
            tt_op(c.u_f[:, g, :], product(key)[:, :], r, ALU.mult).then_inc(release(key), 1)

        group_out(0)
        group_out(1)
        for i in range(5):
            if i < 4:
                if i % 2 == 0:
                    root_c = rstd()
                w = pa[("q_latent", "kv_latent")[i // 2]][:, 2 * l + i % 2:2 * l + i % 2 + 1]
                stt(stage(("cn", l, i)), c.c[:, i, :], w, root_c, ALU.mult, ALU.mult).then_inc(c.split_src, 1)
            if i:
                lo(("cn", l, i - 1), c.cn_hi[:, i - 1, :], c.cn_lo[:, i - 1, :])
        group_out(2)
        group_out(3)
        for i in range(4):
            key = ("kn", l, i)
            out = product(key)
            v.tensor_copy(c.k2[0:64, 2 * i, :], out[0:64, :])
            v.tensor_copy(c.k2[0:64, 2 * i + 1, :], out[64:P, :]).then_inc(release(key), 1)
        q_gain, done, sq0 = pa["q_head"][:, l:l + 1], l * 2 * MLA_H, count_squares(l)
        for batch in range(5):
            for h in range(4 * batch, 4 * batch + 4) if batch < 2 else ():
                y, t = c.q2[:, h, :], c.head_t[pe_rows, h % 2, :]
                dve.wait_ge(c.sq_ready, sq0 + h + 1)
                step(stt(t, y[swapped, :], q_gain[swapped, :], k2["cos_sin"][swapped, :], ALU.mult, ALU.mult))
                step(stt(y[0:MLA_QK, :], y[0:MLA_QK, :], q_gain[0:MLA_QK, :], k2["cos_sin"][0:MLA_QK, :], ALU.mult, ALU.mult))
                step(tt_op(y[pe_rows, :], y[pe_rows, :], t, ALU.add))
            for i in range(4 * batch - 4, 4 * batch) if batch else ():
                h, root_h = i % MLA_H, c.head_r[(batch - 1) % 2][:, i % 4, :]
                dve.wait_ge(c.head_r_ready, done + i + 1)
                if i < MLA_H:
                    y = c.q2[0:MLA_QK, h, :]
                    stt(y, y, MLA_QK ** -0.5, root_h[0:MLA_QK, :], ALU.mult, ALU.mult).then_inc(c.head_ready, 1)
                else:
                    y = c.k2[0:MLA_NOPE, h, :]
                    dve.wait_ge(c.sq_ready, sq0 + i + 1)
                    stt(y, y, k_gain[0:MLA_NOPE, :], root_h[0:MLA_NOPE, :], ALU.mult, ALU.mult)
                    tt_op(c.k2[pe_rows, h, :], c.kpe[pe_rows, :], root_h[pe_rows, :], ALU.mult).then_inc(c.head_ready, 1)
            for z in (2 * batch - 2, 2 * batch - 1) if batch else ():
                key, dst = ((("za", "zf")[z // 4]), l, z % 4), (c.z_a, c.z_f)[z // 4]
                tt_op(dst[:, z % 4, :], product(key)[:, :], r, ALU.mult).then_inc(release(key), 1)
        items = [(j, s, qt) for j in range(4) for s in range(2) for qt in range(NT)]
        base = l * len(items)
        dve.wait_ge(c.z_ready, 2 * l + 1)
        for i in range(len(items) + 7):
            if i < len(items):
                v.reduce_max(c.nb2[:, i % 2, 0:1], filled(("s2", l, *items[i]))[:, :], axis=AX, negate=True)\
                    .then_inc(c.nb2_ready, 1)
            if 1 <= i <= len(items):
                n = i - 1
                read(("s2", l, *items[n]))
                step(v.reciprocal(c.nb2[:, n % 2, 2:3], c.nb2[:, n % 2, 1:2]))
                e = c.prob2[:, n % 3, :]
                v.tensor_scalar(e, e, c.nb2[:, n % 2, 2:3], None, ALU.mult).then_inc(c.prob2_ready, 1)
            if i >= 4 and i - 4 < len(items) and items[i - 4][1:] == (1, NT - 1):
                j = items[i - 4][0]
                dve.wait_ge(c.attn_out, 8 + 4 * l + j + 1)
                tt_op(stage(("oa", l, j)), c.psum[bank[("o2", l, j)][0]][:, :], c.z_a[:, j, :], ALU.mult)\
                    .then_inc(release(("o2", l, j)), 1)
            if i >= 6 and i - 6 < len(items) and items[i - 6][1:] == (1, NT - 1):
                j = items[i - 6][0]
                lo(("oa", l, j), c.a_hi[:, j, :], c.a_lo[:, j, :])
        n = l * FG * NT
        for g in range(FG):
            for tt in range(NT):
                n += 1
                key = ("dd", l, g, tt)
                dve.wait_ge(c.d_hi_ready, n)
                tt_op(c.d_lo[:, tt, g, :], c.psum[bank[key][0]][:, 0:2 * P], c.d_hi[:, tt, g, :].bitcast(F32), ALU.subtract)\
                    .then_inc(release(key), 1)
        dve.wait_ge(c.z_ready, 2 * l + 2)
        for g in range(FG + 1):
            if g < FG:
                key = ("f", l, g)
                tt_op(stage(("of", l, g)), product(key)[:, :], c.z_f[:, g, :], ALU.mult).then_inc(release(key), 1)
            if g:
                lo(("of", l, g - 1), c.a_hi[:, 3 + g, :], c.a_lo[:, 3 + g, :])
        for m in range(KT + 1):
            if m < KT:
                g = [c.sig[:, 2 * (m % 2) + branch, :] for branch in range(2)]
                for branch, name in enumerate(("ga", "gf")):
                    key = (name, l, m, 0)
                    tt_op(g[branch], product(key)[:, :], r, ALU.mult).then_inc(release(key), 1)
                for branch, key in enumerate((("ya2", l, m), ("yf2", l, m))):
                    out = product(key)
                    dve.wait_ge(c.sig_ready, (l * KT + m) * 2 + branch + 1)
                    tt_op(g[branch], out[:, :], g[branch], ALU.mult).then_inc(release(key), 1)
                read(("ya2", l, m))
                read(("yf2", l, m))
                tt_op(stage(("m", l, m)), g[0], g[1], ALU.add).then_inc(c.split_src, 1)
            if m:
                lo(("m", l, m - 1), c.m_hi[:, m - 1, :], c.m_lo[:, m - 1, :])
        if l < LAYERS2 - 1:
            sums_before_norm(5 + l, gains("norm2", (l + 1) * KT), "out2", l)
        else:
            for m in range(KT):
                add_to_x(("out2", l, m), m)


def count_squares(l):
    before = 8 + 4
    return before + (l + 1) * 4 + l * 2 * MLA_H


def build(nc, in_x, in_weights, in_common, in_phase0, in_phase1, in_phase2, in_params, out):
    from contextlib import ExitStack

    block, bank, split, n_blocks = plan_core()
    assert in_weights.shape[0] == n_blocks, (in_weights.shape, n_blocks)
    ctx = ExitStack()
    with ctx:
        c = Core()
        c.in_common, c.in_phase0, c.in_phase1, c.in_phase2, c.in_params = in_common, in_phase0, in_phase1, in_phase2, in_params
        place(nc, c)
        c.psum = [ctx.enter_context(nc.psum_tensor(f"bank{i}", [P, T], F32)) for i in range(8)]
        add_semaphores(nc, ctx, c)
        blocks = ctx.enter_context(nc.Block())

        @blocks.sync
        def _(sp):
            sp.dma_start(c.raw[:, 0, :], in_weights[0]).then_inc(c.raw_loaded[0], 16)
            for i in range(KT // 2):
                sp.dma_start(c.x[:, 2 * i:2 * i + 2, :], in_x[2 * i * P:2 * (i + 1) * P, :].rearrange("(k p) t -> p k t", p=P))\
                    .then_inc(c.x_loaded[i], 16)
            for b in range(1, RING):
                sp.dma_start(c.raw[:, b, :], in_weights[b]).then_inc(c.raw_loaded[b], 16)
            with sp.Fori(1, n_blocks // RING) as turn:
                for slot in range(RING):
                    sp.wait_ge(c.w_lo_ready, (turn - 1) * RING + slot + 1)
                    sp.dma_start(c.raw[:, slot, :], in_weights[turn * RING + slot]).then_inc(c.raw_loaded[slot], 16)
            for b in range(n_blocks // RING * RING, n_blocks):
                sp.wait_ge(c.w_lo_ready, b - RING + 1)
                sp.dma_start(c.raw[:, b % RING, :], in_weights[b]).then_inc(c.raw_loaded[b % RING], 16)
            for m in range(KT):
                bnk, use, _ = bank[("out2", LAYERS2 - 1, m)]
                sp.wait_ge(c.bank_read[bnk], use + 1)
                sp.dma_start(out[m * P:m * P + P, :], c.x[:, m, :]).then_inc(c.out_written, 16)
            sp.wait_ge(c.out_written, 16 * KT)

        @blocks.gpsimd
        def _(pool):
            def low_part(slot):
                return nc.gpsimd.tensor_tensor(c.w_lo[:, slot, :], c.raw[:, slot, :], c.w_hi[:, slot, :].bitcast(F32),
                                               ALU.subtract)

            with pool.Fori(0, n_blocks // RING) as turn:
                for slot in range(RING):
                    pool.wait_ge(c.w_hi_ready, turn * RING + slot + 1)
                    low_part(slot).then_inc(c.w_lo_ready, 1)
            for b in range(n_blocks // RING * RING, n_blocks):
                pool.wait_ge(c.w_hi_ready, b + 1)
                low_part(b % RING).then_inc(c.w_lo_ready, 1)

        @blocks.scalar
        def _(act):
            program_scalar(act, nc, c, block, bank, split, n_blocks)

        @blocks.vector
        def _(dve):
            program_vector(dve, nc, c, block, bank, split)

        @blocks.tensor
        def _(pe):
            program_tensor(pe, nc, c, block, bank, split)


def kernel(**inputs):
    import concourse.bacc as bacc
    from concourse.bass_utils import run_bass_kernel_spmd

    inp = {k: np.asarray(a) for k, a in inputs.items()}
    common, phase0, phase1, phase2 = constant_arrays()
    arrays = {
        "in_x": np.ascontiguousarray(inp["x"][0].T), "in_weights": stream_of(inp), "in_common": common, "in_phase0": phase0,
        "in_phase1": phase1, "in_phase2": phase2, "in_params": parameter_array(inp),
    }
    nc = bacc.Bacc("TRN2", target_bir_lowering=False, num_devices=1)
    args = [nc.dram_tensor(name, a.shape, F32, kind="ExternalInput").ap() for name, a in arrays.items()]
    out = nc.dram_tensor("out", (D, T), F32, kind="ExternalOutput").ap()
    build(nc, *args, out)
    r = run_bass_kernel_spmd(nc, [arrays], core_ids=[0])
    return np.ascontiguousarray(r.results[0]["out"].T)[None]
```
